# Optimizing a Trainium2 kernel written in Bass

```python
import math
import jax, jax.numpy as jnp
from jax import lax
import numpy as np

D_MODEL = 1024
BATCH = 1
SEQ = 256
DEPTH = 2
DEC_BATCH = 8
DEC_SEQ = 1
PAST_LEN = 2048
PAGE_SIZE = 128

N_RET_LAYERS = (DEPTH + 1) // 2
N_HG_LAYERS = DEPTH // 2
RET_HEADS = 4
RET_DK = D_MODEL // RET_HEADS
RET_DV = 2 * D_MODEL // RET_HEADS
RET_QK = RET_HEADS * RET_DK
RET_V = RET_HEADS * RET_DV
HG_EXPAND = 128
HG_HEADS = D_MODEL // HG_EXPAND
HG_DK = HG_EXPAND
HG_DV = D_MODEL // HG_HEADS
HG_W = HG_HEADS * HG_DK
D_FF = 2816
N_EXPERTS = 8
TOP_K = 2
D_FF_EXPERT = 3584
CHUNK = 64
ROPE_THETA = 10000.0
NORM_EPS = 1e-6
GN_EPS = 1e-5

kernel_name = "retnet_hgrn2_hybrid_moe_step"

F32 = jnp.float32

def rmsnorm(x, g, eps=NORM_EPS):
    xf = x.astype(F32)
    y = xf * lax.rsqrt(jnp.mean(xf * xf, axis=-1, keepdims=True) + eps)
    return (y * g.astype(F32)).astype(x.dtype)

def rotary(x, pos):
    half = x.shape[-1] // 2
    inv = jnp.power(ROPE_THETA, -jnp.arange(half, dtype=F32) / half)
    ang = pos[:, None] * inv[None, :]
    cos = jnp.cos(ang)[None, :, None, :]
    sin = jnp.sin(ang)[None, :, None, :]
    x1, x2 = x[..., :half], x[..., half:]
    return jnp.concatenate([x1 * cos - x2 * sin, x2 * cos + x1 * sin], axis=-1)

def to_chunks(a, c):
    b, l = a.shape[0], a.shape[1]
    return jnp.moveaxis(a.reshape(b, l // c, c, *a.shape[2:]), 1, 0)

def from_chunks(a):
    a = jnp.moveaxis(a, 0, 1)
    return a.reshape(a.shape[0], a.shape[1] * a.shape[2], *a.shape[3:])

def retention_scan(q, k, v, s0):
    l, h = q.shape[1], q.shape[2]
    c = math.gcd(l, CHUNK)
    log_gamma = jnp.log1p(-jnp.exp2(-5.0 - jnp.arange(h, dtype=F32)))
    t = jnp.arange(c, dtype=F32)
    rel = t[:, None] - t[None, :]
    causal = rel >= 0
    decay_mask = jnp.where(causal[None], jnp.exp(jnp.where(causal, rel, 0.0)[None] * log_gamma[:, None, None]), 0.0)
    decay_in = jnp.exp((t + 1.0)[:, None] * log_gamma[None, :])
    decay_out = jnp.exp((c - 1.0 - t)[:, None] * log_gamma[None, :])
    decay_chunk = jnp.exp(c * log_gamma)

    def step(s, xs):
        qc, kc, vc = xs
        scores = jnp.einsum('bthd,bshd->bhts', qc, kc) * decay_mask[None]
        o = jnp.einsum('bhts,bshe->bthe', scores, vc) + jnp.einsum('bthd,bhde->bthe', qc * decay_in[None, :, :, None], s)
        s_new = s * decay_chunk[None, :, None, None] + jnp.einsum('bshd,bshe->bhde', kc * decay_out[None, :, :, None], vc)
        return s_new, o

    s_fin, o = lax.scan(step, s0, (to_chunks(q, c), to_chunks(k, c), to_chunks(v, c)))
    return from_chunks(o), s_fin

def hgrn_scan(q, k, logf, i, s0):
    l = q.shape[1]
    c = math.gcd(l, CHUNK)
    tri = jnp.tril(jnp.ones((c, c), dtype=bool))

    def step(s, xs):
        qc, kc, gc, ic = xs
        b = jnp.cumsum(gc, axis=1)
        diff = b[:, :, None] - b[:, None, :]
        w = jnp.exp(jnp.where(tri[None, :, :, None, None], diff, -jnp.inf))
        a = jnp.einsum('bthd,btshd->bhts', qc, w * kc[:, None])
        o = jnp.einsum('bhts,bshe->bthe', a, ic) + jnp.einsum('bthd,bhde->bthe', qc * jnp.exp(b), s)
        b_last = b[:, -1]
        s_new = s * jnp.exp(b_last)[..., None] + jnp.einsum('bshd,bshe->bhde', kc * jnp.exp(b_last[:, None] - b), ic)
        return s_new, o

    xs = (to_chunks(q, c), to_chunks(k, c), to_chunks(logf, c), to_chunks(i, c))
    s_fin, o = lax.scan(step, s0, xs)
    return from_chunks(o), s_fin

def retention_mixer(h, w_in, gn_g, w_out, s0, pos):
    bsz, l, _ = h.shape
    proj = h @ w_in
    q, k, v, g = jnp.split(proj, [RET_QK, 2 * RET_QK, 2 * RET_QK + RET_V], axis=-1)
    q = rotary(q.reshape(bsz, l, RET_HEADS, RET_DK).astype(F32), pos)
    k = rotary(k.reshape(bsz, l, RET_HEADS, RET_DK).astype(F32), pos) * (RET_DK ** -0.5)
    v = v.reshape(bsz, l, RET_HEADS, RET_DV).astype(F32)
    o, s = retention_scan(q, k, v, s0.astype(F32))
    mu = jnp.mean(o, axis=-1, keepdims=True)
    var = jnp.mean(jnp.square(o - mu), axis=-1, keepdims=True)
    on = (o - mu) * lax.rsqrt(var + GN_EPS) * gn_g.astype(F32).reshape(RET_HEADS, RET_DV)
    o = (jax.nn.silu(g.astype(F32)) * on.reshape(bsz, l, RET_V)).astype(h.dtype)
    return o @ w_out, s

def hgrn_mixer(h, w_in, lb, norm_g, w_out, s0):
    bsz, l, _ = h.shape
    proj = h @ w_in
    q, f, i, g = jnp.split(proj, 4, axis=-1)
    q = jax.nn.silu(q.astype(F32)).reshape(bsz, l, HG_HEADS, HG_DK)
    forget = lb[None, None, :] + (1.0 - lb[None, None, :]) * jax.nn.sigmoid(f.astype(F32))
    k = (1.0 - forget).reshape(bsz, l, HG_HEADS, HG_DK)
    logf = jnp.log(forget).reshape(bsz, l, HG_HEADS, HG_DK)
    i = i.astype(F32).reshape(bsz, l, HG_HEADS, HG_DV)
    o, s = hgrn_scan(q, k, logf, i, s0.astype(F32))
    on = o * lax.rsqrt(jnp.mean(o * o, axis=-1, keepdims=True) + NORM_EPS) * norm_g.astype(F32).reshape(HG_HEADS, HG_DV)
    o = (jax.nn.silu(g.astype(F32)) * on.reshape(bsz, l, HG_HEADS * HG_DV)).astype(h.dtype)
    return o @ w_out, s

def swiglu(h, wg, wu, wd):
    return (jax.nn.silu(h @ wg) * (h @ wu)) @ wd

def moe_swiglu(h, router, wg, wu, wd):
    probs = jax.nn.softmax((h @ router).astype(F32), axis=-1)
    vals, idx = lax.top_k(probs, TOP_K)
    vals = vals / jnp.sum(vals, axis=-1, keepdims=True)
    combine = jnp.sum(jax.nn.one_hot(idx, N_EXPERTS, dtype=F32) * vals[..., None], axis=-2)
    out = jnp.zeros(h.shape, F32)
    for e in range(N_EXPERTS):
        out = out + combine[..., e:e + 1] * swiglu(h, wg[e], wu[e], wd[e]).astype(F32)
    return out.astype(h.dtype)

def trunk(x, ret_states, hg_states, pos, state_dtype,
          norm_mix_g, norm_ffn_g, final_norm_g, ret_w_in, ret_gn_g, ret_w_out,
          hg_w_in, hg_lb_param, hg_norm_g, hg_w_out, ffn_w_gate, ffn_w_up, ffn_w_down,
          moe_router, moe_w_gate, moe_w_up, moe_w_down):
    p = jax.nn.softmax(hg_lb_param.astype(F32), axis=0)
    lbs = jnp.cumsum(p, axis=0) - p[0:1]
    new_ret, new_hg = [], []
    for layer in range(DEPTH):
        j = layer // 2
        h = rmsnorm(x, norm_mix_g[layer])
        if layer % 2 == 0:
            out, s = retention_mixer(h, ret_w_in[j], ret_gn_g[j], ret_w_out[j], ret_states[j], pos)
            new_ret.append(s.astype(state_dtype))
        else:
            out, s = hgrn_mixer(h, hg_w_in[j], lbs[layer], hg_norm_g[j], hg_w_out[j], hg_states[j])
            new_hg.append(s.astype(state_dtype))
        x = x + out
        h = rmsnorm(x, norm_ffn_g[layer])
        if layer % 2 == 0:
            x = x + swiglu(h, ffn_w_gate[j], ffn_w_up[j], ffn_w_down[j])
        else:
            x = x + moe_swiglu(h, moe_router[j], moe_w_gate[j], moe_w_up[j], moe_w_down[j])
    return rmsnorm(x, final_norm_g), jnp.stack(new_ret), jnp.stack(new_hg)

def setup_inputs(seed: int = 0) -> dict:
    key = jax.random.key(seed)
    ks = jax.random.split(key, 24)
    nrm = lambda k, shape, s: jax.random.normal(k, shape, F32) * s
    d = D_MODEL
    return {
        "x_prompt": nrm(ks[0], (BATCH, SEQ, d), 1.0),
        "x_sample": nrm(ks[1], (DEC_BATCH, DEC_SEQ, d), 1.0),
        "state_retention": nrm(ks[2], (N_RET_LAYERS, DEC_BATCH, RET_HEADS, RET_DK, RET_DV), 0.1),
        "state_hgrn": nrm(ks[3], (N_HG_LAYERS, DEC_BATCH, HG_HEADS, HG_DK, HG_DV), 0.5),
        "norm_mix_g": 1.0 + nrm(ks[4], (DEPTH, d), 0.02),
        "norm_ffn_g": 1.0 + nrm(ks[5], (DEPTH, d), 0.02),
        "final_norm_g": 1.0 + nrm(ks[6], (d,), 0.02),
        "ret_w_in": nrm(ks[7], (N_RET_LAYERS, d, 2 * RET_QK + 2 * RET_V), d ** -0.5),
        "ret_gn_g": 1.0 + nrm(ks[8], (N_RET_LAYERS, RET_V), 0.02),
        "ret_w_out": nrm(ks[9], (N_RET_LAYERS, RET_V, d), RET_V ** -0.5),
        "hg_w_in": nrm(ks[10], (N_HG_LAYERS, d, 4 * HG_W), d ** -0.5),
        "hg_lb_param": 1.0 + nrm(ks[11], (DEPTH, HG_W), 0.1),
        "hg_norm_g": 1.0 + nrm(ks[12], (N_HG_LAYERS, HG_HEADS * HG_DV), 0.02),
        "hg_w_out": nrm(ks[13], (N_HG_LAYERS, HG_HEADS * HG_DV, d), (HG_HEADS * HG_DV) ** -0.5),
        "ffn_w_gate": nrm(ks[14], (N_RET_LAYERS, d, D_FF), d ** -0.5),
        "ffn_w_up": nrm(ks[15], (N_RET_LAYERS, d, D_FF), d ** -0.5),
        "ffn_w_down": nrm(ks[16], (N_RET_LAYERS, D_FF, d), D_FF ** -0.5),
        "moe_router": nrm(ks[17], (N_HG_LAYERS, d, N_EXPERTS), d ** -0.5),
        "moe_w_gate": nrm(ks[18], (N_HG_LAYERS, N_EXPERTS, d, D_FF_EXPERT), d ** -0.5),
        "moe_w_up": nrm(ks[19], (N_HG_LAYERS, N_EXPERTS, d, D_FF_EXPERT), d ** -0.5),
        "moe_w_down": nrm(ks[20], (N_HG_LAYERS, N_EXPERTS, D_FF_EXPERT, d), D_FF_EXPERT ** -0.5),
    }

def reference(x_prompt, x_sample, state_retention, state_hgrn, norm_mix_g, norm_ffn_g, final_norm_g,
              ret_w_in, ret_gn_g, ret_w_out, hg_w_in, hg_lb_param, hg_norm_g, hg_w_out,
              ffn_w_gate, ffn_w_up, ffn_w_down, moe_router, moe_w_gate, moe_w_up, moe_w_down):
    weights = (norm_mix_g, norm_ffn_g, final_norm_g, ret_w_in, ret_gn_g, ret_w_out,
               hg_w_in, hg_lb_param, hg_norm_g, hg_w_out, ffn_w_gate, ffn_w_up, ffn_w_down,
               moe_router, moe_w_gate, moe_w_up, moe_w_down)
    bp, lp = x_prompt.shape[0], x_prompt.shape[1]
    ls = x_sample.shape[1]
    ret0 = jnp.zeros((N_RET_LAYERS, bp, RET_HEADS, RET_DK, RET_DV), F32)
    hg0 = jnp.zeros((N_HG_LAYERS, bp, HG_HEADS, HG_DK, HG_DV), F32)
    pos_p = jnp.arange(lp, dtype=F32)
    y_prompt, ret_p, hg_p = trunk(x_prompt, ret0, hg0, pos_p, x_prompt.dtype, *weights)
    pos_s = PAST_LEN + jnp.arange(ls, dtype=F32)
    y_sample, ret_s, hg_s = trunk(x_sample, state_retention, state_hgrn, pos_s, state_retention.dtype, *weights)
    return (y_prompt, y_sample, ret_p, ret_s, hg_p, hg_s)


_drawn_inputs = setup_inputs


def setup_inputs(seed=0):
    import zlib

    import numpy as np

    out = dict(_drawn_inputs(seed))
    spreads = {}
    factors = {}
    for name, (base, spread) in spreads.items():
        noise = np.random.default_rng([zlib.crc32(name.encode()), seed]).standard_normal(out[name].shape)
        drawn = base * np.exp(spread * noise) if base else spread * noise
        out[name] = __import__('jax').numpy.asarray(drawn.astype(out[name].dtype))
    for name, factor in factors.items():
        out[name] = (out[name] * factor).astype(out[name].dtype)
    return out
```

```python
from contextlib import ExitStack

import numpy as np

import concourse.bass as bass
from concourse import mybir

ALU = mybir.AluOpType
ACT = mybir.ActivationFunctionType
F32 = mybir.dt.float32
I32 = mybir.dt.int32
U32 = mybir.dt.uint32
AX = mybir.AxisListType

P = 128
D = 1024
KD = D // P
NP_ = 256
NS = 8
NT = NP_ + NS
PAST = 2048
RH, RDK, RDV = 4, 256, 512
HH = 8
FF = 2816
FT = FF // P
NE, FE = 8, 3584
C = 96
ROUNDS = -(-NT // C)
CHUNK = 64
NEPS, GEPS = 1e-6, 1e-5

PIECE = 4096
RING = 7
DRING = 5
EP = 3 * (FE // 512)
UNITS = 4

CONST = {}
_at = 0
for _n, _w in (("cos", NT), ("sin", NT), ("dmask", RH * 256), ("dout", 2 * RH), ("ident", P), ("mean_d", P),
               ("mean_gn", P), ("ones", P), ("col_gn", 64), ("col_hg", 64), ("rowsel", 8 * P),
               ("ltri", P), ("slot", C), ("exp8", 8), ("valid", 3), ("reset", NP_), ("lvl", 7 * P), ("eps", 2)):
    CONST[_n] = (_at, _at + _w)
    _at += _w
NCONST = _at


def constants():
    c = np.zeros((P, NCONST), np.float32)

    def put(name, v):
        a, b = CONST[name]
        c[:v.shape[0], a:b] = v.reshape(v.shape[0], -1)

    f = np.float32
    half = RDK // 2
    inv = np.power(f(10000.0), -np.arange(half, dtype=f) / f(half)).astype(f)
    pos = np.concatenate([np.arange(NP_), PAST + np.zeros(NS)]).astype(f)
    ang = (pos[None, :] * inv[:, None]).astype(f)
    put("cos", np.cos(ang))
    put("sin", np.sin(ang))
    lg = np.log1p(-np.exp2(-5.0 - np.arange(RH)))
    s, t = np.arange(P)[:, None], np.arange(P)[None, :]
    scale = RDK ** -0.5
    dm = np.zeros((P, RH, 2, P))
    for h in range(RH):
        dm[:, h, 0] = np.where(t >= s, np.exp(np.maximum(t - s, 0) * lg[h]), 0.0) * scale
        dm[:, h, 1] = np.exp((t + P - s) * lg[h]) * scale
    put("dmask", dm.astype(f))
    do = np.zeros((P, 2, RH))
    for st in range(2):
        for h in range(RH):
            do[:, st, h] = np.exp((NP_ - 1 - st * P - np.arange(P)) * lg[h]) * scale
    put("dout", do.astype(f))
    put("ident", np.eye(P, dtype=f))
    put("mean_d", np.full((P, P), 1.0 / D, f))
    put("mean_gn", np.full((P, P), 1.0 / RDV, f))
    put("ones", np.ones((P, P), f))
    put("col_gn", np.broadcast_to(np.eye(8) / RDV, (P, 8, 8)).astype(f))
    put("col_hg", np.broadcast_to(np.eye(8) / P, (P, 8, 8)).astype(f))
    put("rowsel", np.broadcast_to(np.eye(8)[:, :, None], (8, 8, P)).astype(f))
    put("ltri", (s < t).astype(f))
    put("slot", np.broadcast_to(np.arange(C), (P, C)).astype(f))
    put("exp8", np.broadcast_to(np.arange(8), (P, 8)).astype(f))
    va = np.ones((P, 3), f)
    va[NS:, 2] = 0
    put("valid", va)
    put("reset", np.broadcast_to((np.arange(NP_) % CHUNK != 0), (P, NP_)).astype(f))
    lv = np.zeros((P, 7, P), f)
    for l in range(7):
        m = 1 << l
        lv[:, l] = (s // (2 * m) == t // (2 * m)) & (s % (2 * m) < m) & (t % (2 * m) >= m)
    put("lvl", lv)
    put("eps", np.broadcast_to(np.array([NEPS, GEPS]), (P, 2)).astype(f))
    return c


GAMMA = [float(np.float32(1.0 - 2.0 ** (-5 - h))) for h in range(RH)]

VEC = {"mix": 0, "ffn": 16, "gn": 32, "hgn": 48, "lb": 56}
NVEC = 72


def fills():
    order = []
    add = order.append
    for j in range(4):
        add((("xt", j), 4 + j))
    add((("xt", 4), 0))
    add((("xt", 5), 1))
    add((("ms", 0), 7))
    n = 0

    def tile(kind, i):
        nonlocal n
        add(((kind, i), n % 4))
        n += 1

    for i in range(16):
        tile("qk", i)
    for i in range(16):
        tile("v", i)
        if i:
            add((("vtr", i - 1), 4 + (i - 1) % 2))
    add((("vtr", 15), 5))
    for h in range(RH):
        add((("sc", h), 6))
        add((("kdt", h), 7))
        add((("o", h, 0), 4))
        add((("o", h, 1), 5))
        add((("st", h, 0), 6))
        add((("st", h, 1), 7))
    add((("so", 0), 6))
    for i in range(16):
        tile("g", i)
    for h in range(RH):
        add((("mu", h), (4, 5, 7, 6)[h]))
    add((("var", 0), 4))
    for h in range(RH):
        add((("rs", h), (5, 6, 7, 5)[h]))
    for i in range(8):
        tile("wo", i)
    add((("ms", 1), 7))
    for i in range(FT):
        tile("fg", i)
        tile("fu", i)
    for i in range(8):
        tile("fd", i)
    add((("ms", 2), 7))
    for i in range(8):
        tile("hf", i)
    for i in range(8):
        tile("hq", i)
    for i in range(8):
        tile("hi", i)
        if i:
            add((("itr", i - 1), 4 + (i - 1) % 2))
    add((("itr", 7), 5))
    for i in range(8):
        tile("hg", i)
    for lv in range(8):
        for j in range(4):
            add((("lv", lv, j), 4 * ((lv + 1) % 2) + j))
    for j in range(2):
        add((("cr", j), 4 + j))
    for j in range(4):
        add((("kt", j), (6, 7, 0, 1)[j]))
    for j in range(2):
        add((("hs", j), 2 + j))
    for j in range(4):
        add((("ho", j), 4 + j))
    add((("hso", 0), 0))
    add((("hvar", 0), 1))
    for h in range(HH):
        add((("hrs", h), 2 + h % 4))
    assert n % 4 == 0
    for i in range(8):
        tile("hw", i)
    add((("ms", 3), 7))
    for j in range(12):
        add((("tok", j), j % 6))
    add((("lg", 0), 6))
    add((("rk", 0), 7))
    count = [0] * 8
    out = {}
    for name, b in order:
        assert name not in out
        out[name] = (b, count[b])
        count[b] += 1
    return out, count


def hybrid_step(nc, ins, outs):
    FILL, BANKS = fills()
    with ExitStack() as ctx:
        def sb(name, shape, dt=F32):
            return ctx.enter_context(nc.sbuf_tensor(name, shape, dt))

        def sem(name):
            return ctx.enter_context(nc.semaphore(name))

        ring = sb("ring", [P, RING * PIECE])
        AW = 14256
        arena = sb("arena", [P, AW])
        xT = sb("xT", [P, KD, NT])
        hT = sb("hT", [P, KD, NT])
        cst = sb("cst", [P, NCONST])
        std = sb("std", [P, NT])
        rstd = sb("rstd", [P, NT])
        vec = sb("vec", [P, NVEC])
        lbt = sb("lbt", [P, 8, 8])
        small = sb("small", [P, 320])
        ps = ctx.enter_context(nc.psum_tensor("ps", [P, 8, 512], F32))

        def piece(s):
            return ring[:, s * PIECE:(s + 1) * PIECE]

        def cc(name):
            a, b = CONST[name]
            return cst[:, a:b]

        ident, ones = cc("ident"), cc("ones")
        cos, sin = cc("cos"), cc("sin")
        dmask = cc("dmask").rearrange("p (h t) -> p h t", h=RH)
        dout = cc("dout").rearrange("p (s h) -> p s h", s=2)
        col_gn = cc("col_gn").rearrange("p (h m) -> p h m", h=8)
        col_hg = cc("col_hg").rearrange("p (h m) -> p h m", h=8)
        rowsel = cc("rowsel").rearrange("p (h m) -> p h m", h=8)
        lvl = cc("lvl").bitcast(I32).rearrange("p (l m) -> p l m", l=7)
        eps_n, eps_g = cc("eps")[:, 0:1], cc("eps")[:, 1:2]

        def part(tensor, a, *shape):
            n = int(np.prod(shape))
            v = tensor[:, a:a + n]
            if len(shape) == 2:
                return v.rearrange("p (a b) -> p a b", a=shape[0])
            if len(shape) == 3:
                return v.rearrange("p (a b c) -> p a b c", a=shape[0], b=shape[1])
            return v

        scratch = DRING * PIECE
        x_in = part(arena, 0, 3, D)
        vrow = part(arena, 3 * D, P)
        qT = part(arena, 0, 8, NT)
        kT = part(arena, 2112, 8, NT)
        v_tok = part(arena, 4224, 2, 2048)
        gT = part(arena, 4224, 16, NT)
        oT = part(arena, 8448, 16, NT)
        v_smp = arena[0:NS, 8448 + 8 * NT:8448 + 8 * NT + 2048]
        rot = part(arena, 12672, 4, NT)
        prob = part(arena, 12672, 384)
        sqg = part(arena, 12672, 4, NT)
        tmpT = part(arena, 13728, 2, NT)
        kdec = part(arena, 13728, 2, 256)
        unit = part(ring, scratch, UNITS, 1536)
        s_out = part(ring, scratch + UNITS * 1536, 2, 1024)
        ksmp = part(small, 0, 8, 8)
        hid = part(arena, 0, FT, NT)
        sg = part(arena, FT * NT, 2, NT)
        hq = part(arena, 0, 8, NT)
        hf = part(arena, 2112, 8, NT)
        att = part(arena, 2112, 8, 2, P)
        hsq = part(arena, 2112, 8, NT)
        hk = part(arena, 4224, 8, NT)
        hgt = part(arena, 6336, 8, NT)
        bcum = part(arena, 8448, 8, NP_)
        kd_tok = part(arena, 8448, 16, P)
        i_tok = part(arena, 10496, 2, D)
        cross = part(arena, 12544, 8, P)
        i_smp = arena[0:NS, 12544:12544 + D]
        itmp = part(arena, 13568, 2, NT)
        lev = [part(ring, scratch + 2048 * j, 2048) for j in range(2)]
        hunit = [part(ring, scratch + 4096 + 2048 * j, 2, D) for j in range(2)]
        hs_out = part(ring, scratch, 8, P)
        oH = hT
        fsmp = part(small, 64, 8, 8)
        tots = part(small, 128, 4, 8)
        x_tok = part(arena, 0, 3, D)
        h_tok = part(arena, 3072, 3, D)
        gfin = part(arena, 6144, D)
        gsel = part(arena, 7168, 3, C)
        xe = part(arena, 7456, 8, C)
        act_g = part(arena, 8224, 2, 4 * C)
        hide = part(arena, 8992, 2, 4 * C)
        y_out = part(arena, 9760, D)
        rt = part(arena, 10784, 8 * P)
        RB = 10784
        w_rt = part(arena, RB, 8, 8)
        lg = part(arena, RB + 64, 3, 8)
        prb = part(arena, RB + 88, 3, 8)
        m8 = part(arena, RB + 112, 3, 8)
        ix = arena[:, RB + 136:RB + 160].bitcast(U32).rearrange("p (a b) -> p a b", a=3)
        ixf = part(arena, RB + 160, 3, 8)
        oa = part(arena, RB + 184, 3, 8)
        ob = part(arena, RB + 208, 3, 8)
        mm_ = part(arena, RB + 232, 3, 8)
        rk = part(arena, RB + 256, 4, 8)
        r1 = part(arena, RB + 288, 3, 8)
        reff = part(arena, RB + 312, 3, ROUNDS * 8 + 8)
        wab = part(arena, RB + 440, 3, 4)
        va = part(arena, RB + 452, 2, 3)
        vt = part(arena, RB + 458, 2, 3)
        rowf = part(arena, RB + 464, 2, 3)
        rowi = arena[:, RB + 470:RB + 476].bitcast(U32).rearrange("p (a b) -> p a b", a=2)
        nrf = part(arena, RB + 476, 4)
        nri = arena[:, RB + 480:RB + 481].bitcast(I32)
        red3 = part(arena, RB + 484, 3)
        fsum = part(arena, RB + 488, 3)
        frs = part(arena, RB + 492, 3)
        ya = part(ring, 0, 3, D)
        yb = part(ring, 3072, 3, D)
        yf = part(ring, 6144, 3, D)
        ysq = part(ring, 9216, D)

        v_scr = nc.dram_tensor("v_scr", (NS, 2048), F32)
        i_scr = nc.dram_tensor("i_scr", (NS, D), F32)
        y_scr = nc.dram_tensor("y_scr", (ROUNDS * NE * C, D), F32)

        s_x = sem("tokens_loaded")
        s_c = sem("constants_loaded")
        s_v = sem("vectors_loaded")
        bank_full = [sem(f"bank_full{b}") for b in range(8)]
        bank_free = [sem(f"bank_free{b}") for b in range(8)]
        arrived = [sem(f"piece_arrived{s}") for s in range(DRING)]
        moe_arrived = [sem(f"expert_piece_arrived{s}") for s in range(RING)]
        piece_used = sem("piece_used")
        lb_in = sem("bound_shifted")
        lb_exp = sem("bound_exponentials")
        squares = sem("squares")
        h_ready = sem("h_ready")
        dve_step = sem("dve_step")
        act_step = sem("act_step")
        qk_ready = sem("qk_rotated")
        sq_summed = sem("squares_summed")
        pad_ok = sem("pad_rows_cleared")
        e_in = sem("softmax_shifted")
        fin_in = sem("combined")
        fin_mean = sem("final_mean")
        v_stored = sem("v_stored")
        s_store = [sem(f"ret_state_stored{j}") for j in range(2)]
        unit_s = [sem(f"unit_state_in{j}") for j in range(UNITS)]
        unit_v = [sem(f"unit_v_in{j}") for j in range(UNITS)]
        unit_new = sem("unit_updated")
        unit_pe = sem("unit_multiplied")
        unit_out = [sem(f"unit_stored{j}") for j in range(UNITS)]
        sq_ok = sem("o_squares")
        r8_ok = sem("row_rstd_ready")
        o_ok = sem("o_ready")
        f_ok = sem("forget_ready")
        logf_ok = sem("logf_ready")
        i_stored = sem("i_stored")
        lev_sub = sem("level_exponents")
        lev_exp = sem("level_exp")
        lev_x = sem("level_operands")
        hs_store = sem("hgrn_state_stored")
        hu_in = [sem(f"hunit_state_in{j}") for j in range(2)]
        hu_i = [sem(f"hunit_i_in{j}") for j in range(2)]
        hu_new = sem("hunit_updated")
        hu_pe = sem("hunit_multiplied")
        hu_out = [sem(f"hunit_stored{j}") for j in range(2)]
        rt_in = sem("router_loaded")
        e_ok = sem("softmax_exp")
        mask_ok = sem("choice_ready")
        route_ok = sem("routing_ready")
        sel_ok = sem("selection_ready")
        xg_full = sem("gathered")
        xe_ok = sem("expert_x_ready")
        gate_ok = sem("expert_silu_ready")
        hide_ok = sem("expert_hidden_ready")
        y_free = sem("expert_y_copied")
        y_store = sem("expert_y_stored")
        zero_ok = sem("zeros_ready")
        zero_stored = sem("zeros_stored")
        all_stored = sem("all_y_stored")
        ya_in = sem("rows_gathered")
        fin_sq = sem("final_squares")
        fin_std = sem("final_std")
        fin_ok = sem("final_ready")
        out_done = sem("outputs_stored")

        def bank(name, parts=P):
            return ps[0:parts, FILL[name][0], :]

        def filled(eng, name):
            b, k = FILL[name]
            eng.wait_ge(bank_full[b], k + 1)

        def frees(ins, name):
            ins.then_inc(bank_free[FILL[name][0]], 1)

        def freed(eng, name):
            b, k = FILL[name]
            eng.wait_ge(bank_free[b], k + 1)

        rwi = ins["ret_w_in"][0].rearrange("(k p) n -> p k n", p=P)
        rwo = ins["ret_w_out"][0].rearrange("(k p) n -> p k n", p=P)
        fwg = ins["ffn_w_gate"][0].rearrange("(k p) n -> p k n", p=P)
        fwu = ins["ffn_w_up"][0].rearrange("(k p) n -> p k n", p=P)
        fwd = ins["ffn_w_down"][0].rearrange("(k p) n -> p k n", p=P)
        hwi = ins["hg_w_in"][0].rearrange("(k p) n -> p k n", p=P)
        hwo = ins["hg_w_out"][0].rearrange("(k p) n -> p k n", p=P)
        dense = []
        for j in range(12):
            dense.append((("rwi", j), [(rwi[:, :, 512 * j:512 * j + 512], 8, 512, 0)]))
        for j in range(4):
            dense.append((("rwo", j), [(rwo[:, :, 256 * j:256 * j + 256], 16, 256, 0)]))
        for j in range(11):
            dense.append((("fgu", j), [(fwg[:, :, 256 * j:256 * j + 256], 8, 256, 0),
                                       (fwu[:, :, 256 * j:256 * j + 256], 8, 256, 2048)]))
        for j in range(8):
            a, kh = j // 2, j % 2
            dense.append((("fd", j), [(fwd[:, 11 * kh:11 * kh + 11, 256 * a:256 * a + 256], 11, 256, 0)]))
        HG_ORDER = (1, 0, 2, 3)
        for a, part_ in enumerate(HG_ORDER):
            for j in range(2):
                o = 1024 * part_ + 512 * j
                dense.append((("hwi", 2 * a + j), [(hwi[:, :, o:o + 512], 8, 512, 0)]))
        for j in range(2):
            dense.append((("hwo", j), [(hwo[:, :, 512 * j:512 * j + 512], 8, 512, 0)]))
        NDENSE = len(dense)
        assert NDENSE % DRING == 0
        last_tile = {}
        last_tile.update({("rwi", j): (("qk", 4 * j + 3) if j < 4 else ("v", 4 * j - 13) if j < 8 else ("g", 4 * j - 29))
                          for j in range(12)})
        last_tile.update({("rwo", j): ("wo", 2 * j + 1) for j in range(4)})
        last_tile.update({("fgu", j): ("fu", 2 * j + 1) for j in range(11)})
        last_tile.update({("fd", j): ("fd", 2 * (j // 2) + 1) for j in range(8)})
        last_tile.update({("hwi", j): (("hf", "hq", "hi", "hg")[j // 2], 4 * (j % 2) + 3) for j in range(8)})
        last_tile.update({("hwo", j): ("hw", 4 * j + 3) for j in range(2)})
        where, need, got = {}, {}, [0] * DRING
        for n, (name, loads) in enumerate(dense):
            got[n % DRING] += 16 * len(loads)
            where[name] = n % DRING
            need[name] = got[n % DRING]
        moe_g = ins["moe_w_gate"][0].rearrange("e (k p) n -> p e k n", p=P)
        moe_u = ins["moe_w_up"][0].rearrange("e (k p) n -> p e k n", p=P)
        moe_d = ins["moe_w_down"][0].rearrange("e (k p) n -> p e k n", p=P)
        NCH = FE // 512
        epieces = []
        for c in range(NCH + 1):
            if c < NCH:
                epieces += [("g", c), ("u", c)]
            if c:
                epieces.append(("d", c - 1))
        assert len(epieces) == EP and EP % RING == 0
        epos = {name: t for t, name in enumerate(epieces)}

        def moe_source(e, kind, c):
            if kind == "d":
                return moe_d[:, bass.ds(e, 1), 4 * c:4 * c + 4, :]
            w = moe_g if kind == "g" else moe_u
            return w[:, bass.ds(e, 1), :, 512 * c:512 * c + 512]

        def moe_dest(kind, t):
            v = piece(t % RING)
            if kind == "d":
                return v.rearrange("p (e k n) -> p e k n", e=1, k=4)
            return v.rearrange("p (e k n) -> p e k n", e=1, k=8)

        ret_in = ins["state_retention"][0].rearrange("b h (k p) e -> b h p k e", p=P)
        ret_out = outs["ret_s"][0].rearrange("b h (k p) e -> b h p k e", p=P)
        ret_pout = outs["ret_p"][0, 0].rearrange("h (k p) e -> h p k e", p=P)
        hg_in = ins["state_hgrn"][0].rearrange("b h d e -> b d h e")
        hg_out = outs["hg_s"][0].rearrange("b h d e -> b d h e")
        hg_pout = outs["hg_p"][0, 0].rearrange("h d e -> d h e")

        block = ctx.enter_context(nc.Block())

        @block.sync
        def _(sp):
            for n, (name, loads) in enumerate(dense):
                if n >= DRING:
                    filled(sp, last_tile[dense[n - DRING][0]])
                for src, k, w, off in loads:
                    dst = piece(n % DRING)[:, off:off + k * w].rearrange("p (k n) -> p k n", k=k)
                    sp.dma_start(dst, src).then_inc(arrived[n % DRING], 16)

            for t, (kind, c) in enumerate(epieces):
                if t < DRING:
                    filled(sp, last_tile[dense[NDENSE - DRING + t][0]])
                elif t < RING:
                    filled(sp, ("hrs", 7))
                    sp.wait_ge(hs_store, 16)
                    for j in range(2):
                        sp.wait_ge(hu_out[j], 16 * (NS // 2))
                else:
                    sp.wait_ge(piece_used, t - RING + 1)
                sp.dma_start(moe_dest(kind, t), moe_source(0, kind, c)).then_inc(moe_arrived[t % RING], 16)

            def expert(e, i):
                for t, (kind, c) in enumerate(epieces):
                    sp.wait_ge(piece_used, i * EP + (t - RING + 1))
                    sp.dma_start(moe_dest(kind, t), moe_source(e, kind, c)).then_inc(moe_arrived[t % RING], 16)

            with sp.Fori(1, NE) as e:
                expert(e, e)
            sp.wait_ge(route_ok, 1)
            rounds = sp.value_load(nri[0:1, 0:1], min_val=1, max_val=ROUNDS)
            with sp.If(rounds > 1):
                with sp.Fori(1, rounds) as r:
                    with sp.Fori(0, NE) as e:
                        expert(e, r * NE + e)

        @block.gpsimd
        def _(pool):
            def load_state(u):
                b, h = divmod(u, RH)
                if u >= UNITS:
                    pool.wait_ge(unit_pe, u - UNITS + 1)
                    pool.wait_ge(unit_out[h], 16 * b)
                pool.dma_start(unit[:, h, 0:1024].rearrange("p (k e) -> p k e", k=2), ret_in[b, h])\
                    .then_inc(unit_s[h], 16)

            for u in range(UNITS):
                load_state(u)
            nc.gpsimd.memset(s_out[:, 0, :], 0.0).then_inc(zero_ok, 1)
            pool.wait_ge(zero_ok, 1)
            nz = (ROUNDS - 1) * NE * C // P
            pool.dma_start(y_scr[NE * C:, :].rearrange("(t p) d -> p t d", p=P),
                           s_out[:, 0:1, :].to_broadcast([P, nz, D])).then_inc(zero_stored, 16)
            freed(pool, ("vtr", 14))
            freed(pool, ("vtr", 15))
            pool.dma_start(v_scr[:, :], v_smp).then_inc(v_stored, 16)
            pool.wait_ge(v_stored, 16)
            for u in range(NS * RH + 2):
                if u < NS * RH:
                    b, h = divmod(u, RH)
                    if u >= UNITS:
                        load_state(u)
                    pool.dma_start(unit[:, h, 1024:1536],
                                   v_scr[b, 512 * h:512 * h + 512].partition_broadcast(P))\
                        .then_inc(unit_v[h], 16)
                if u >= 2:
                    w = u - 2
                    b, h = divmod(w, RH)
                    pool.wait_ge(unit_new, w + 1)
                    pool.dma_start(ret_out[b, h], unit[:, h, 0:1024].rearrange("p (k e) -> p k e", k=2))\
                        .then_inc(unit_out[h], 16)

            filled(pool, ("so", 0))
            for h in range(UNITS):
                pool.wait_ge(unit_out[h], 16 * NS)

            def load_h(b):
                if b >= 2:
                    pool.wait_ge(hu_pe, b - 1)
                    pool.wait_ge(hu_out[b % 2], 16 * (b // 2))
                pool.dma_start(hunit[b % 2][:, 0, :].rearrange("p (h e) -> p h e", h=8), hg_in[b])\
                    .then_inc(hu_in[b % 2], 16)

            pool.wait_ge(s_store[0], 32)
            pool.wait_ge(s_store[1], 32)
            load_h(0)
            load_h(1)
            freed(pool, ("itr", 6))
            freed(pool, ("itr", 7))
            pool.dma_start(i_scr[:, :], i_smp).then_inc(i_stored, 16)
            pool.wait_ge(i_stored, 16)
            for b in range(NS + 1):
                if b < NS:
                    if b >= 2:
                        load_h(b)
                    pool.dma_start(hunit[b % 2][:, 1, :], i_scr[b, :].partition_broadcast(P)).then_inc(hu_i[b % 2], 16)
                if b:
                    w = b - 1
                    pool.wait_ge(hu_new, w + 1)
                    pool.dma_start(hg_out[w], hunit[w % 2][:, 0, :].rearrange("p (h e) -> p h e", h=8))\
                        .then_inc(hu_out[w % 2], 16)

            pool.wait_ge(all_stored, 1)
            for w, dst in enumerate((ya, yb)):
                for t in range(3):
                    m = P if t < 2 else NS
                    pool.indirect_dma_start(dst[0:m, t, :], None, y_scr[:, :],
                                            bass.IndirectOffsetOnAxis(ap=rowi[0:m, w, t:t + 1], axis=0))\
                        .then_inc(ya_in, 16)

        @block.scalar
        def _(act):
            A = nc.scalar
            steps = [0]

            def link(i):
                steps[0] += 1
                i.then_inc(act_step, 1)
                act.wait_ge(act_step, steps[0])

            act.dma_start(x_in[:, 0:2, :], ins["x_prompt"][0].rearrange("(t p) d -> p t d", p=P)).then_inc(s_x, 16)
            act.dma_start(x_in[0:NS, 2, :], ins["x_sample"].rearrange("b s d -> (b s) d")).then_inc(s_x, 16)
            act.dma_start(cst[:, :], ins["consts"]).then_inc(s_c, 16)
            for src, r, n in ((ins["norm_mix_g"].rearrange("l (k p) -> (l k) p", p=P), VEC["mix"], 16),
                              (ins["norm_ffn_g"].rearrange("l (k p) -> (l k) p", p=P), VEC["ffn"], 16),
                              (ins["ret_gn_g"].rearrange("l (k p) -> (l k) p", p=P), VEC["gn"], 16),
                              (ins["hg_norm_g"].rearrange("l (k p) -> (l k) p", p=P), VEC["hgn"], 8),
                              (ins["hg_lb_param"].rearrange("l (k p) -> (l k) p", p=P), VEC["lb"], 16)):
                act.dma_start(vrow[r:r + n, :], src).then_inc(s_v, 16)

            def norm(n):
                for hf_ in range(2):
                    if n:
                        freed(act, (("wo", "fd", "hw")[n - 1], 4 * hf_ + 3))
                        filled(act, (("wo", "fd", "hw")[n - 1], 7))
                    else:
                        for j in range(5):
                            freed(act, ("xt", j))
                    A.activation(hT[:, 4 * hf_:4 * hf_ + 4, :], xT[:, 4 * hf_:4 * hf_ + 4, :], ACT.Square)\
                        .then_inc(squares, 1)
                filled(act, ("ms", n))
                frees(A.activation(std[:, :], bank(("ms", n))[:, 0:NT], ACT.Sqrt, bias=eps_n), ("ms", n))

            act.wait_ge(s_c, 16)
            act.wait_ge(lb_in, 1)
            A.activation(lbt[:, 1:3, :], lbt[:, 1:3, :], ACT.Exp).then_inc(lb_exp, 1)
            norm(0)
            for i in range(16):
                filled(act, ("v", i))
                if i >= 2:
                    filled(act, ("vtr", i - 2))
                frees(A.copy(tmpT[:, i % 2, :], bank(("v", i))[:, 0:NT]), ("v", i))
            for h in range(RH):
                filled(act, ("kdt", h))
                if h >= 1:
                    filled(act, ("st", h - 1, 1))
                for st in range(2):
                    i = A.activation(kdec[:, st, :], bank(("kdt", h))[:, 256 * st:256 * st + 256], ACT.Copy,
                                     scale=dout[:, st, h:h + 1])
                frees(i, ("kdt", h))
                for j in range(2):
                    filled(act, ("o", h, j))
                    if h == 2 and j == 0:
                        act.wait_ge(v_stored, 16)
                    frees(A.copy(oT[:, 4 * h + 2 * j:4 * h + 2 * j + 2, 0:NP_],
                                 bank(("o", h, j)).rearrange("p (a t) -> p a t", a=2)), ("o", h, j))
                for j in range(2):
                    filled(act, ("st", h, j))
                    if h == 0 and j == 0:
                        act.wait_ge(zero_stored, 16)
                    if h >= 2 and j == 0:
                        act.wait_ge(s_store[h % 2], 16 * (h // 2))
                    i = A.copy(s_out[:, h % 2, 512 * j:512 * j + 512], bank(("st", h, j)))
                    frees(i, ("st", h, j))
                freed(act, ("st", h, 1))
                act.dma_start(ret_pout[h], s_out[:, h % 2, :].rearrange("p (k e) -> p k e", k=2))\
                    .then_inc(s_store[h % 2], 16)
            for i in range(16):
                filled(act, ("g", i))
                frees(A.activation(gT[:, i, :], bank(("g", i))[:, 0:NT], ACT.Silu), ("g", i))
            for h in range(RH):
                freed(act, ("mu", h))
                if h:
                    act.wait_ge(sq_summed, h)
                A.activation(sqg[:, :, :], oT[:, 4 * h:4 * h + 4, :], ACT.Square).then_inc(sq_ok, 1)
            filled(act, ("var", 0))
            frees(A.activation(std[0:8, :], bank(("var", 0), 8)[:, 0:NT], ACT.Sqrt, bias=eps_g[0:8]), ("var", 0))
            norm(1)
            for i in range(FT):
                filled(act, ("fg", i))
                if i >= 2:
                    freed(act, ("fu", i - 2))
                frees(A.activation(sg[:, i % 2, :], bank(("fg", i))[:, 0:NT], ACT.Silu), ("fg", i))
            norm(2)
            for h in range(HH):
                filled(act, ("hf", h))
                frees(A.activation(hf[:, h, :], bank(("hf", h))[:, 0:NT], ACT.Sigmoid), ("hf", h))
            act.wait_ge(f_ok, 8)
            A.activation(hf[:, :, 0:NP_], hf[:, :, 0:NP_], ACT.Ln).then_inc(logf_ok, 1)
            for h in range(HH):
                filled(act, ("hq", h))
                frees(A.activation(hq[:, h, :], bank(("hq", h))[:, 0:NT], ACT.Silu), ("hq", h))
            for i in range(8):
                filled(act, ("hi", i))
                if i >= 2:
                    filled(act, ("itr", i - 2))
                frees(A.copy(itmp[:, i % 2, :], bank(("hi", i))[:, 0:NT]), ("hi", i))
            for i in range(8):
                filled(act, ("hg", i))
                frees(A.activation(hgt[:, i, :], bank(("hg", i))[:, 0:NT], ACT.Silu), ("hg", i))
            for l in range(9):
                act.wait_ge(lev_sub, l + 1)
                A.activation(lev[l % 2], lev[l % 2], ACT.Exp).then_inc(lev_exp, 1)
            for j in range(4):
                filled(act, ("kt", j))
                frees(A.copy(kd_tok[:, 4 * j:4 * j + 4, :], bank(("kt", j)).rearrange("p (a t) -> p a t", a=4)),
                      ("kt", j))
            for j in range(4):
                filled(act, ("ho", j))
                frees(A.copy(oH[:, 2 * j:2 * j + 2, 0:NP_], bank(("ho", j)).rearrange("p (a t) -> p a t", a=2)),
                      ("ho", j))
            for j in range(2):
                filled(act, ("hs", j))
                frees(A.copy(hs_out[:, 4 * j:4 * j + 4, :], bank(("hs", j)).rearrange("p (a t) -> p a t", a=4)),
                      ("hs", j))
            freed(act, ("hs", 0))
            freed(act, ("hs", 1))
            act.dma_start(hg_pout, hs_out).then_inc(hs_store, 16)
            freed(act, ("hso", 0))
            for j in range(4):
                freed(act, ("ho", j))
            A.activation(hsq, oH[:, :, :], ACT.Square).then_inc(sq_ok, 1)
            filled(act, ("hvar", 0))
            frees(A.activation(std[0:8, :], bank(("hvar", 0), 8)[:, 0:NT], ACT.Sqrt, bias=eps_n[0:8]), ("hvar", 0))
            act.wait_ge(hs_store, 16)
            norm(3)
            act.dma_start(w_rt, ins["moe_router"][0].rearrange("(k p) e -> p k e", p=P)).then_inc(rt_in, 16)
            act.dma_start(gfin, ins["final_norm_g"].partition_broadcast(P)).then_inc(rt_in, 16)
            for j in range(12):
                filled(act, ("tok", j))
                src = bank(("tok", j))
                dst, t, q = (x_tok, j // 2, j % 2) if j < 6 else (h_tok, (j - 6) // 2, j % 2)
                m = P if t < 2 else NS
                if j >= 6 and t == 2:
                    act.wait_ge(pad_ok, 1)
                frees(A.copy(dst[0:m, t, 512 * q:512 * q + 512], src[0:m, :]), ("tok", j))
            act.wait_ge(e_in, 1)
            A.activation(prb, prb, ACT.Exp).then_inc(e_ok, 1)
            act.wait_ge(route_ok, 1)
            rounds = act.value_load(nri[0:1, 0:1], min_val=1, max_val=ROUNDS)
            act.sem_inc(y_free, 1)
            with act.Fori(0, rounds) as r:
                with act.Fori(0, NE) as e:
                    i = r * NE + e
                    for c in range(NCH):
                        act.wait_ge(piece_used, i * EP + (epos["g", c] + 1))
                        act.wait_ge(hide_ok, i * NCH + (1 + max(c - 1, 0)))
                        A.activation(act_g[:, c % 2, :], ps[:, c % 2, 0:4 * C], ACT.Silu).then_inc(gate_ok, 1)
                    act.wait_ge(piece_used, i * EP + EP)
                    A.copy(y_out[0:C, 0:512], ps[0:C, 4, :])
                    A.copy(y_out[0:C, 512:1024], ps[0:C, 5, :]).then_inc(y_free, 1)
                    act.wait_ge(y_free, i + 2)
                    act.dma_start(y_scr[bass.ds(i * C, C), :], y_out[0:C, :]).then_inc(y_store, 16)
                    act.wait_ge(y_store, i * 16 + 16)
            A.copy(frs[:, 0:1], red3[:, 0:1]).then_inc(all_stored, 1)
            for t in range(3):
                m = P if t < 2 else NS
                act.wait_ge(fin_in, t + 1)
                A.activation(ysq[0:m, :], yf[0:m, t, :], ACT.Square, accum_out=fsum[0:m, t:t + 1]).then_inc(fin_sq, 1)
                act.wait_ge(fin_mean, t + 1)
                A.activation(fsum[0:m, t:t + 1], fsum[0:m, t:t + 1], ACT.Sqrt).then_inc(fin_std, 1)
            for t in range(3):
                act.wait_ge(fin_ok, t + 1)
                if t < 2:
                    act.dma_start(outs["y_p"][0, P * t:P * t + P, :], yf[:, t, :]).then_inc(out_done, 16)
                else:
                    act.dma_start(outs["y_s"].rearrange("b s d -> (b s) d"), yf[0:NS, 2, :]).then_inc(out_done, 16)
            act.wait_ge(out_done, 48)
            for s_ in range(2):
                act.wait_ge(s_store[s_], 32)
                act.wait_ge(hu_out[s_], 16 * NS // 2)
            for s_ in range(UNITS):
                act.wait_ge(unit_out[s_], 16 * NS)

        @block.vector
        def _(dve):
            V = nc.vector
            steps = [0]

            def link(i):
                steps[0] += 1
                i.then_inc(dve_step, 1)
                dve.wait_ge(dve_step, steps[0])

            dve.wait_ge(s_c, 16)
            for j in range(4):
                filled(dve, ("xt", j))
                frees(V.tensor_copy(xT[:, 4 * (j % 2):4 * (j % 2) + 4, P * (j // 2):P * (j // 2) + P],
                                    bank(("xt", j)).rearrange("p (a t) -> p a t", a=4)), ("xt", j))
            filled(dve, ("xt", 4))
            frees(V.tensor_copy(xT[:, :, NP_:NT], bank(("xt", 4))[:, 0:64].rearrange("p (a t) -> p a t", a=8)),
                  ("xt", 4))
            filled(dve, ("xt", 5))
            frees(V.tensor_copy(vec[:, :], bank(("xt", 5))[:, 0:NVEC]), ("xt", 5))
            freed(dve, ("xt", 5))
            a0, a1 = vec[:, VEC["lb"]:VEC["lb"] + 8], vec[:, VEC["lb"] + 8:VEC["lb"] + 16]
            link(V.tensor_tensor(lbt[:, 0, :], a0, a1, ALU.max))
            link(V.tensor_tensor(lbt[:, 1, :], a0, lbt[:, 0, :], ALU.subtract))
            V.tensor_tensor(lbt[:, 2, :], a1, lbt[:, 0, :], ALU.subtract).then_inc(lb_in, 1)
            dve.wait_ge(lb_exp, 1)
            link(V.tensor_tensor(lbt[:, 3, :], lbt[:, 1, :], lbt[:, 2, :], ALU.add))
            link(V.reciprocal(lbt[:, 4, :], lbt[:, 3, :]))
            link(V.tensor_tensor(lbt[:, 1, :], lbt[:, 1, :], lbt[:, 4, :], ALU.mult))
            link(V.tensor_tensor(lbt[:, 2, :], lbt[:, 2, :], lbt[:, 4, :], ALU.mult))
            link(V.tensor_tensor(lbt[:, 5, :], lbt[:, 1, :], lbt[:, 2, :], ALU.add))
            link(V.tensor_tensor(lbt[:, 6, :], lbt[:, 5, :], lbt[:, 1, :], ALU.subtract))
            link(V.tensor_scalar(lbt[:, 7, :], lbt[:, 6, :], -1.0, 1.0, ALU.mult, ALU.add))
            lb, oml = lbt[:, 6, :], lbt[:, 7, :]

            def norm(n, gain):
                freed(dve, ("ms", n))
                link(V.reciprocal(rstd[:, :], std[:, :]))
                filled(dve, ("ms", n))
                for k in range(KD):
                    V.scalar_tensor_tensor(out=hT[:, k, :], in0=xT[:, k, :], scalar=vec[:, gain + k:gain + k + 1],
                                           in1=rstd[:, :], op0=ALU.mult, op1=ALU.mult).then_inc(h_ready, 1)

            def residual(kind):
                for i in range(8):
                    filled(dve, (kind, i))
                    frees(V.tensor_tensor(xT[:, i, :], xT[:, i, :], bank((kind, i))[:, 0:NT], ALU.add), (kind, i))
                freed(dve, (kind, 7))

            norm(0, VEC["mix"])
            for a in range(8):
                dst = qT if a < 4 else kT
                t = 2 * (a % 4)
                filled(dve, ("qk", 2 * a))
                filled(dve, ("qk", 2 * a + 1))
                x1, x2 = bank(("qk", 2 * a))[:, 0:NT], bank(("qk", 2 * a + 1))[:, 0:NT]
                if a:
                    dve.wait_ge(qk_ready, a)
                V.tensor_tensor(rot[:, 0, :], x1, cos, ALU.mult)
                V.tensor_tensor(rot[:, 1, :], x2, sin, ALU.mult)
                frees(V.tensor_tensor(rot[:, 2, :], x2, cos, ALU.mult), ("qk", 2 * a + 1))
                frees(V.tensor_tensor(rot[:, 3, :], x1, sin, ALU.mult), ("qk", 2 * a))
                freed(dve, ("qk", 2 * a))
                V.tensor_tensor(dst[:, t, :], rot[:, 0, :], rot[:, 1, :], ALU.subtract)
                V.tensor_tensor(dst[:, t + 1, :], rot[:, 2, :], rot[:, 3, :], ALU.add).then_inc(qk_ready, 1)
            dve.wait_ge(qk_ready, 8)
            link(V.tensor_scalar(ksmp, kT[:, :, NP_:NT], RDK ** -0.5, None, ALU.mult))
            for i in range(16):
                filled(dve, ("vtr", i))
                s = bank(("vtr", i))
                V.tensor_copy(v_tok[:, :, P * i:P * i + P], s[:, 0:256].rearrange("p (a e) -> p a e", a=2))
                frees(V.tensor_copy(v_smp[:, P * i:P * i + P], s[0:NS, 256:384]), ("vtr", i))
            for h in range(RH):
                filled(dve, ("sc", h))
                if h:
                    filled(dve, ("o", h - 1, 1))
                s = bank(("sc", h))
                V.tensor_tensor(prob[:, 0:256], s[:, 0:256], dmask[:, h, :], ALU.mult)
                frees(V.tensor_tensor(prob[:, 256:384], s[:, 256:384], dmask[:, h, 0:P], ALU.mult), ("sc", h))
            for u in range(NS * RH):
                b, h = divmod(u, RH)
                S = unit[:, h, 0:1024]
                dve.wait_ge(unit_s[h], 16 * (b + 1))
                link(V.tensor_scalar(S, S, GAMMA[h], None, ALU.mult))
                dve.wait_ge(unit_v[h], 16 * (b + 1))
                for k in range(2):
                    i = V.scalar_tensor_tensor(out=S[:, 512 * k:512 * k + 512], in0=unit[:, h, 1024:1536],
                                               scalar=ksmp[:, 2 * h + k, b:b + 1], in1=S[:, 512 * k:512 * k + 512],
                                               op0=ALU.mult, op1=ALU.add)
                i.then_inc(unit_new, 1)
            filled(dve, ("so", 0))
            frees(V.tensor_copy(oT[:, :, NP_:NT], bank(("so", 0))[:, 0:P].rearrange("p (a b) -> p a b", a=16)),
                  ("so", 0))
            for h in range(RH):
                filled(dve, ("mu", h))
                o = oT[:, 4 * h:4 * h + 4, :]
                frees(V.tensor_tensor(o, o, bank(("mu", h))[:, 0:NT].unsqueeze(1).to_broadcast([P, 4, NT]),
                                      ALU.subtract), ("mu", h))
            freed(dve, ("var", 0))
            V.reciprocal(rstd[0:8, :], std[0:8, :]).then_inc(r8_ok, 1)
            for h in range(RH):
                filled(dve, ("rs", h))
                if h == 0:
                    freed(dve, ("g", 15))
                for e in range(4):
                    t = 4 * h + e
                    i = V.scalar_tensor_tensor(out=oT[:, t, :], in0=oT[:, t, :],
                                               scalar=vec[:, VEC["gn"] + t:VEC["gn"] + t + 1],
                                               in1=bank(("rs", h))[:, 0:NT], op0=ALU.mult, op1=ALU.mult)
                frees(i, ("rs", h))
                freed(dve, ("rs", h))
                o = oT[:, 4 * h:4 * h + 4, :]
                V.tensor_tensor(o, o, gT[:, 4 * h:4 * h + 4, :], ALU.mult).then_inc(o_ok, 1)
            residual("wo")
            norm(1, VEC["ffn"])
            for i in range(FT):
                filled(dve, ("fu", i))
                freed(dve, ("fg", i))
                frees(V.tensor_tensor(hid[:, i, :], sg[:, i % 2, :], bank(("fu", i))[:, 0:NT], ALU.mult), ("fu", i))
            residual("fd")
            norm(2, VEC["mix"] + 8)
            for h in range(HH):
                freed(dve, ("hf", h))
                link(V.tensor_scalar(hf[:, h, :], hf[:, h, :], oml[:, h:h + 1], lb[:, h:h + 1], ALU.mult, ALU.add))
                V.tensor_scalar(hk[:, h, :], hf[:, h, :], -1.0, 1.0, ALU.mult, ALU.add)
                i = V.tensor_copy(fsmp[:, h, :], hf[:, h, NP_:NT])
                i.then_inc(f_ok, 1)
            dve.wait_ge(logf_ok, 1)
            for h in range(HH):
                i = V.tensor_tensor_scan(bcum[:, h, :], cc("reset"), hf[:, h, 0:NP_], 0.0, ALU.mult, ALU.add)
            link(i)
            bch = bcum.rearrange("p h (c t) -> p h c t", t=CHUNK)
            T = [bch[:, :, c, CHUNK - 1] for c in range(4)]
            V.tensor_copy(tots[:, 2, :], T[3])
            link(V.tensor_tensor(tots[:, 1, :], T[2], T[3], ALU.add))
            link(V.tensor_tensor(tots[:, 0, :], tots[:, 1, :], T[1], ALU.add))

            def reader(l):
                return ("lv", l + 1, 3) if l <= 6 else ("cr", 1)

            def exponents(l):
                if l >= 2:
                    filled(dve, reader(l - 2))
                L = lev[l % 2]
                lc = L.rearrange("p (h c t) -> p h c t", h=8, t=CHUNK)
                tot = lambda a, b: bch[:, :, a:b, CHUNK - 1:CHUNK].to_broadcast([P, 8, b - a, CHUNK])
                if l <= 5:
                    m = 1 << l
                    n = 2048 // (2 * m)
                    bv = bcum.rearrange("p h t -> p (h t)").rearrange("p (n t) -> p n t", t=2 * m)
                    lv = L.rearrange("p (n t) -> p n t", t=2 * m)
                    mid = bv[:, :, m - 1:m].to_broadcast([P, n, m])
                    V.tensor_tensor(lv[:, :, m:], bv[:, :, m:], mid, ALU.subtract)
                    i = V.tensor_tensor(lv[:, :, 0:m], mid, bv[:, :, 0:m], ALU.subtract)
                elif l == 6:
                    for c in (0, 2):
                        V.tensor_tensor(lc[:, :, c:c + 1, :], tot(c, c + 1), bch[:, :, c:c + 1, :], ALU.subtract)
                        i = V.tensor_copy(lc[:, :, c + 1, :], bch[:, :, c + 1, :])
                elif l == 7:
                    link(V.tensor_tensor(lc[:, :, 0:2, :], tot(0, 2), bch[:, :, 0:2, :], ALU.subtract))
                    V.tensor_tensor(lc[:, :, 0, :], lc[:, :, 0, :], tot(1, 2)[:, :, 0, :], ALU.add)
                    V.tensor_copy(lc[:, :, 2, :], bch[:, :, 2, :])
                    i = V.tensor_tensor(lc[:, :, 3, :], bch[:, :, 3, :], tot(2, 3)[:, :, 0, :], ALU.add)
                else:
                    link(V.tensor_tensor(lc, tot(0, 4), bch, ALU.subtract))
                    for c in range(3):
                        i = V.tensor_tensor(lc[:, :, c, :], lc[:, :, c, :],
                                            tots[:, c, :].unsqueeze(2).to_broadcast([P, 8, CHUNK]), ALU.add)
                i.then_inc(lev_sub, 1)

            def operands(l):
                dve.wait_ge(lev_exp, l + 1)
                L = lev[l % 2]
                if l < 8:
                    m = min(1 << l, 128)
                    lv = L.rearrange("p (h n t) -> p h n t", h=8, t=2 * m)
                    kv = hk[:, :, 0:NP_].rearrange("p h (n t) -> p h n t", t=2 * m)
                    qv = hq[:, :, 0:NP_].rearrange("p h (n t) -> p h n t", t=2 * m)
                    V.tensor_tensor(lv[:, :, :, m:], lv[:, :, :, m:], qv[:, :, :, m:], ALU.mult)
                    i = V.tensor_tensor(lv[:, :, :, 0:m], lv[:, :, :, 0:m], kv[:, :, :, 0:m], ALU.mult)
                else:
                    L = L.rearrange("p (h t) -> p h t", h=8)
                    i = V.tensor_tensor(L, L, hk[:, :, 0:NP_], ALU.mult)
                i.then_inc(lev_x, 1)

            def choose(l):
                if l:
                    freed(dve, ("lv", l - 1, 3))
                for j in range(4):
                    filled(dve, ("lv", l, j))
                    src = bank(("lv", l, j)).rearrange("p (a t) -> p a t", a=4)
                    dst = att[:, 2 * j:2 * j + 2, :, :].rearrange("p h a t -> p (h a) t")
                    if l == 0:
                        i = V.tensor_tensor(dst, src, ident.unsqueeze(1).to_broadcast([P, 4, P]), ALU.mult)
                    else:
                        i = V.copy_predicated(dst, lvl[:, l - 1, :].unsqueeze(1).to_broadcast([P, 4, P]), src)
                    frees(i, ("lv", l, j))

            for h in range(UNITS):
                dve.wait_ge(unit_out[h], 16 * NS)
            for j in range(2):
                dve.wait_ge(s_store[j], 32)
            for i in range(8):
                filled(dve, ("itr", i))
                s = bank(("itr", i))
                V.tensor_copy(i_tok[:, :, P * i:P * i + P], s[:, 0:256].rearrange("p (a e) -> p a e", a=2))
                frees(V.tensor_copy(i_smp[:, P * i:P * i + P], s[0:NS, 256:384]), ("itr", i))
            exponents(0)
            choose(0)
            for l in range(9):
                if l < 8:
                    exponents(l + 1)
                operands(l)
                if 1 <= l <= 7:
                    choose(l)
            dve.wait_ge(i_stored, 16)
            for j in range(2):
                filled(dve, ("cr", j))
                frees(V.tensor_copy(cross[:, 4 * j:4 * j + 4, :], bank(("cr", j)).rearrange("p (a t) -> p a t", a=4)),
                      ("cr", j))
            for b in range(NS):
                S = hunit[b % 2][:, 0, :].rearrange("p (h e) -> p h e", h=8)
                I = hunit[b % 2][:, 1, :].rearrange("p (h e) -> p h e", h=8)
                dve.wait_ge(hu_in[b % 2], 16 * (b // 2 + 1))
                V.tensor_tensor(S, S, fsmp[:, :, b:b + 1].to_broadcast([P, 8, P]), ALU.mult)
                dve.wait_ge(hu_i[b % 2], 16 * (b // 2 + 1))
                link(V.tensor_tensor(I, I, hk[:, :, NP_ + b:NP_ + b + 1].to_broadcast([P, 8, P]), ALU.mult))
                V.tensor_tensor(S, S, I, ALU.add).then_inc(hu_new, 1)
            filled(dve, ("hso", 0))
            frees(V.tensor_copy(oH[:, :, NP_:NT], bank(("hso", 0))[:, 0:64].rearrange("p (h b) -> p h b", h=8)),
                  ("hso", 0))
            freed(dve, ("hvar", 0))
            V.reciprocal(rstd[0:8, :], std[0:8, :]).then_inc(r8_ok, 1)
            for h in range(HH):
                filled(dve, ("hrs", h))
                frees(V.scalar_tensor_tensor(out=oH[:, h, :], in0=oH[:, h, :],
                                             scalar=vec[:, VEC["hgn"] + h:VEC["hgn"] + h + 1],
                                             in1=bank(("hrs", h))[:, 0:NT], op0=ALU.mult, op1=ALU.mult), ("hrs", h))
            freed(dve, ("hrs", 7))
            V.tensor_tensor(oH[:, :, :], oH[:, :, :], hgt, ALU.mult).then_inc(o_ok, 1)
            residual("hw")
            norm(3, VEC["ffn"] + 8)
            V.memset(h_tok[:, 2, :], 0.0).then_inc(pad_ok, 1)
            link(V.memset(lg, 0.0))
            filled(dve, ("lg", 0))
            for t in range(3):
                m = P if t < 2 else NS
                i = V.tensor_copy(lg[0:m, t, :], bank(("lg", 0))[0:m, 8 * t:8 * t + 8])
            frees(i, ("lg", 0))
            freed(dve, ("lg", 0))
            link(V.reduce_max(red3, lg, AX.X))
            V.tensor_tensor(prb, lg, red3.unsqueeze(2).to_broadcast([P, 3, 8]), ALU.subtract).then_inc(e_in, 1)
            dve.wait_ge(e_ok, 1)
            link(V.reduce_sum(red3, prb, AX.X))
            link(V.reciprocal(fsum, red3))
            link(V.tensor_tensor(prb, prb, fsum.unsqueeze(2).to_broadcast([P, 3, 8]), ALU.mult))
            for t in range(3):
                link(V.max(m8[:, t, :], prb[:, t, :]))
                i = V.max_index(ix[:, t, :], m8[:, t, :], prb[:, t, :])
            link(i)
            link(V.tensor_copy(ixf, ix))
            valid = cc("valid")
            for t in range(3):
                V.tensor_scalar(oa[:, t, :], cc("exp8"), ixf[:, t, 0:1], valid[:, t:t + 1], ALU.is_equal, ALU.mult)
                i = V.tensor_scalar(ob[:, t, :], cc("exp8"), ixf[:, t, 1:2], valid[:, t:t + 1], ALU.is_equal, ALU.mult)
            link(i)
            V.tensor_tensor(mm_, oa, ob, ALU.add).then_inc(mask_ok, 1)
            link(V.tensor_tensor(wab[:, :, 2], m8[:, :, 0], m8[:, :, 1], ALU.add))
            link(V.reciprocal(wab[:, :, 3], wab[:, :, 2]))
            V.tensor_tensor(wab[:, :, 0], m8[:, :, 0], wab[:, :, 3], ALU.mult)
            V.tensor_tensor(wab[:, :, 1], m8[:, :, 1], wab[:, :, 3], ALU.mult)
            filled(dve, ("rk", 0))
            frees(V.tensor_copy(rk, bank(("rk", 0))[:, 0:32].rearrange("p (a e) -> p a e", a=4)), ("rk", 0))
            freed(dve, ("rk", 0))
            dve.wait_ge(mask_ok, 1)
            link(V.memset(reff, -1.0))
            for r in range(ROUNDS):
                link(V.tensor_scalar(r1, rk[:, 0:3, :], 1.0 - r * C, None, ALU.add))
                link(V.tensor_tensor(r1, r1, mm_, ALU.mult))
                link(V.tensor_scalar(reff[:, :, 8 * r:8 * r + 8], r1, -1.0, None, ALU.add))
            link(V.reduce_max(nrf[:, 0:1], rk[:, 3, :], AX.X))
            link(V.memset(nrf[:, 1:2], 1.0))
            for r in range(1, ROUNDS):
                link(V.tensor_scalar(nrf[:, 2:3], nrf[:, 0:1], float(r * C), None, ALU.is_gt))
                link(V.tensor_tensor(nrf[:, 1:2], nrf[:, 1:2], nrf[:, 2:3], ALU.add))
            link(V.tensor_copy(nri, nrf[:, 1:2]))
            for w, o in enumerate((oa, ob)):
                link(V.tensor_tensor(r1, rk[:, 0:3, :], o, ALU.mult))
                link(V.reduce_sum(va[:, w, :], r1, AX.X))
                link(V.tensor_scalar(rowf[:, w, :], ixf[:, :, w], float(C), None, ALU.mult))
                link(V.tensor_tensor(rowf[:, w, :], rowf[:, w, :], va[:, w, :], ALU.add))
                for r in range(1, ROUNDS):
                    link(V.tensor_scalar(vt[:, w, :], va[:, w, :], float(r * C), float((NE - 1) * C), ALU.is_ge,
                                         ALU.mult))
                    link(V.tensor_tensor(rowf[:, w, :], rowf[:, w, :], vt[:, w, :], ALU.add))
            V.tensor_copy(rowi, rowf).then_inc(route_ok, 1)

            def select(i):
                for t in range(3):
                    s = V.tensor_scalar(gsel[:, t, :], cc("slot"), reff[:, t, bass.ds(i, 1)], None, ALU.is_equal)
                s.then_inc(sel_ok, 1)

            dve.sem_inc(hide_ok, 1)
            select(0)
            dve.wait_ge(route_ok, 1)
            rounds = dve.value_load(nri[0:1, 0:1], min_val=1, max_val=ROUNDS)
            with dve.Fori(0, rounds) as r:
                with dve.Fori(0, NE) as e:
                    i = r * NE + e
                    dve.wait_ge(xg_full, i + 1)
                    for q in range(2):
                        V.tensor_copy(xe[:, 4 * q:4 * q + 4, :],
                                      ps[:, 6 + q, 0:4 * C].rearrange("p (a s) -> p a s", a=4)).then_inc(xe_ok, 1)
                    select(i + 1)
                    for c in range(NCH):
                        dve.wait_ge(piece_used, i * EP + (epos["u", c] + 1))
                        dve.wait_ge(gate_ok, i * NCH + (c + 1))
                        if c >= 2:
                            dve.wait_ge(piece_used, i * EP + (epos["d", c - 2] + 1))
                        V.tensor_tensor(hide[:, c % 2, :], act_g[:, c % 2, :], ps[:, 2 + c % 2, 0:4 * C], ALU.mult)\
                            .then_inc(hide_ok, 1)
            dve.wait_ge(ya_in, 96)
            for t in range(3):
                m = P if t < 2 else NS
                link(V.scalar_tensor_tensor(out=yf[0:m, t, :], in0=ya[0:m, t, :], scalar=wab[0:m, t, 0:1],
                                            in1=x_tok[0:m, t, :], op0=ALU.mult, op1=ALU.add))
                V.scalar_tensor_tensor(out=yf[0:m, t, :], in0=yb[0:m, t, :], scalar=wab[0:m, t, 1:2],
                                       in1=yf[0:m, t, :], op0=ALU.mult, op1=ALU.add).then_inc(fin_in, 1)
                dve.wait_ge(fin_sq, t + 1)
                V.tensor_scalar(fsum[0:m, t:t + 1], fsum[0:m, t:t + 1], 1.0 / D, NEPS, ALU.mult, ALU.add)\
                    .then_inc(fin_mean, 1)
                dve.wait_ge(fin_std, t + 1)
                link(V.reciprocal(frs[0:m, t:t + 1], fsum[0:m, t:t + 1]))
                V.scalar_tensor_tensor(out=yf[0:m, t, :], in0=yf[0:m, t, :], scalar=frs[0:m, t:t + 1],
                                       in1=gfin[0:m, :], op0=ALU.mult, op1=ALU.mult).then_inc(fin_ok, 1)

        @block.tensor
        def _(pe):
            def claim(name):
                b, k = FILL[name]
                if k:
                    pe.wait_ge(bank_free[b], k)

            def close(ins, name):
                ins.then_inc(bank_full[FILL[name][0]], 1)

            def mm(out, lhsT, rhs, first=True, last=True):
                return nc.tensor.matmul(out, lhsT, rhs, start=first, stop=last)

            pe.wait_ge(s_c, 16)
            pe.wait_ge(s_x, 32)
            for j in range(4):
                claim(("xt", j))
                for a in range(4):
                    k = 4 * (j % 2) + a
                    i = nc.tensor.transpose(bank(("xt", j))[:, P * a:P * a + P], x_in[:, j // 2, P * k:P * k + P], ident)
                close(i, ("xt", j))
            for k in range(KD):
                i = nc.tensor.transpose(bank(("xt", 4))[:, NS * k:NS * k + NS], x_in[0:NS, 2, P * k:P * k + P],
                                        ident[0:NS, 0:NS])
            close(i, ("xt", 4))
            pe.wait_ge(s_v, 80)
            close(nc.tensor.transpose(bank(("xt", 5))[:, 0:NVEC], vrow[0:NVEC, :], ident[0:NVEC, 0:NVEC]), ("xt", 5))

            def mean_square(n):
                claim(("ms", n))
                for k in range(KD):
                    if k % 4 == 0:
                        pe.wait_ge(squares, 2 * n + k // 4 + 1)
                    i = mm(bank(("ms", n))[:, 0:NT], cc("mean_d"), hT[:, k, :], k == 0, k == KD - 1)
                close(i, ("ms", n))

            def arrive(name):
                pe.wait_ge(arrived[where[name]], need[name])

            def project(name, w, n_norm=None):
                claim(name)
                for k in range(KD):
                    if n_norm is not None:
                        pe.wait_ge(h_ready, 8 * n_norm + k + 1)
                    i = mm(bank(name)[:, 0:NT], w[:, k, :], hT[:, k, :], k == 0, k == KD - 1)
                close(i, name)

            def pview(name, k, off=0, n=None):
                w = (n or PIECE // k) * k
                return piece(where[name])[:, off:off + w].rearrange("p (k n) -> p k n", k=k)

            def to_tokens(kind, src, dst):
                freed(pe, src)
                claim(dst)
                o = bank(dst)
                for a in range(2):
                    nc.tensor.transpose(o[:, P * a:P * a + P], kind[:, P * a:P * a + P], ident)
                close(nc.tensor.transpose(o[0:NS, 256:384], kind[:, NP_:NT], ident), dst)

            mean_square(0)
            for i in range(16):
                p_ = ("rwi", i // 4)
                if i % 4 == 0:
                    arrive(p_)
                project(("qk", i), pview(p_, 8)[:, :, P * (i % 4):P * (i % 4) + P], 0 if i == 0 else None)
            for i in range(16):
                p_ = ("rwi", 4 + i // 4)
                if i % 4 == 0:
                    arrive(p_)
                project(("v", i), pview(p_, 8)[:, :, P * (i % 4):P * (i % 4) + P])
                if i:
                    to_tokens(tmpT[:, (i - 1) % 2, :], ("v", i - 1), ("vtr", i - 1))
            to_tokens(tmpT[:, 1, :], ("v", 15), ("vtr", 15))
            pe.wait_ge(qk_ready, 8)
            for h in range(RH):
                claim(("sc", h))
                s = bank(("sc", h))
                for k in range(2):
                    mm(s[:, 0:256], kT[:, 2 * h + k, 0:P], qT[:, 2 * h + k, 0:256], k == 0, k == 1)
                for k in range(2):
                    i = mm(s[:, 256:384], kT[:, 2 * h + k, P:256], qT[:, 2 * h + k, P:256], k == 0, k == 1)
                close(i, ("sc", h))
                claim(("kdt", h))
                for st in range(2):
                    for k in range(2):
                        i = nc.tensor.transpose(bank(("kdt", h))[:, 256 * st + P * k:256 * st + P * k + P],
                                                kT[:, 2 * h + k, P * st:P * st + P], ident)
                close(i, ("kdt", h))
                freed(pe, ("sc", h))
                freed(pe, ("vtr", 14))
                freed(pe, ("vtr", 15))
                for j in range(2):
                    claim(("o", h, j))
                    for e in range(2):
                        a = 512 * h + 256 * j + P * e
                        o = bank(("o", h, j))[:, 256 * e:256 * e + 256]
                        mm(o, v_tok[:, 0, a:a + P], prob[:, 0:256], True, False)
                        i = mm(o[:, P:256], v_tok[:, 1, a:a + P], prob[:, 256:384], False, True)
                    close(i, ("o", h, j))
                freed(pe, ("kdt", h))
                for j in range(2):
                    claim(("st", h, j))
                    for st in range(2):
                        i = mm(bank(("st", h, j)), kdec[:, st, P * j:P * j + P], v_tok[:, st, 512 * h:512 * h + 512],
                               st == 0, st == 1)
                    close(i, ("st", h, j))

            def sample_unit(u):
                b, h = divmod(u, RH)
                pe.wait_ge(unit_new, u + 1)
                for e in range(4):
                    for k in range(2):
                        i = mm(bank(("so", 0))[:, NS * (4 * h + e) + b:NS * (4 * h + e) + b + 1],
                               unit[:, h, 512 * k + P * e:512 * k + P * e + P],
                               qT[:, 2 * h + k, NP_ + b:NP_ + b + 1], k == 0, k == 1)
                if u == NS * RH - 1:
                    close(i, ("so", 0))
                else:
                    i.then_inc(unit_pe, 1)

            claim(("so", 0))
            for i in range(16):
                p_ = ("rwi", 8 + i // 4)
                if i % 4 == 0:
                    arrive(p_)
                project(("g", i), pview(p_, 8)[:, :, P * (i % 4):P * (i % 4) + P])
                sample_unit(2 * i)
                sample_unit(2 * i + 1)
            freed(pe, ("so", 0))
            for h in range(RH):
                freed(pe, ("o", h, 0))
                freed(pe, ("o", h, 1))
                claim(("mu", h))
                for e in range(4):
                    i = mm(bank(("mu", h))[:, 0:NT], cc("mean_gn"), oT[:, 4 * h + e, :], e == 0, e == 3)
                close(i, ("mu", h))
            claim(("var", 0))
            for h in range(RH):
                pe.wait_ge(sq_ok, h + 1)
                for e in range(4):
                    i = mm(bank(("var", 0), 8)[:, 0:NT], col_gn[:, h, :], sqg[:, e, :], h + e == 0, h + e == 6)
                if h < 3:
                    i.then_inc(sq_summed, 1)
            close(i, ("var", 0))
            pe.wait_ge(r8_ok, 1)
            for h in range(RH):
                claim(("rs", h))
                close(mm(bank(("rs", h))[:, 0:NT], rowsel[0:8, h, :], rstd[0:8, :]), ("rs", h))
            for j in range(4):
                p_ = ("rwo", j)
                arrive(p_)
                w = pview(p_, 16)
                for a in range(2):
                    name = ("wo", 2 * j + a)
                    claim(name)
                    for k in range(16):
                        if name[1] == 0 and k % 4 == 0:
                            pe.wait_ge(o_ok, k // 4 + 1)
                        i = mm(bank(name)[:, 0:NT], w[:, k, P * a:P * a + P], oT[:, k, :], k == 0, k == 15)
                    close(i, name)
            mean_square(1)
            for j in range(11):
                p_ = ("fgu", j)
                arrive(p_)
                for a in range(2):
                    project(("fg", 2 * j + a), pview(p_, 8, 0, 256)[:, :, P * a:P * a + P], 1 if j + a == 0 else None)
                    project(("fu", 2 * j + a), pview(p_, 8, 2048, 256)[:, :, P * a:P * a + P])
            for a in range(4):
                claim(("fd", 2 * a))
                claim(("fd", 2 * a + 1))
                for kh in range(2):
                    p_ = ("fd", 2 * a + kh)
                    arrive(p_)
                    w = pview(p_, 11, 0, 256)
                    for q in range(2):
                        name = ("fd", 2 * a + q)
                        for k in range(11):
                            kk = 11 * kh + k
                            if name[1] == 0:
                                freed(pe, ("fu", kk))
                            i = mm(bank(name)[:, 0:NT], w[:, k, P * q:P * q + P], hid[:, kk, :], kk == 0, kk == FT - 1)
                        if kh:
                            close(i, name)
            mean_square(2)
            for a, kind in enumerate(("hf", "hq", "hi", "hg")):
                for i in range(8):
                    p_ = ("hwi", 2 * a + i // 4)
                    if i % 4 == 0:
                        arrive(p_)
                    project((kind, i), pview(p_, 8)[:, :, P * (i % 4):P * (i % 4) + P], 2 if a + i == 0 else None)
                    if kind == "hi" and i:
                        to_tokens(itmp[:, (i - 1) % 2, :], ("hi", i - 1), ("itr", i - 1))
                if kind == "hi":
                    to_tokens(itmp[:, 1, :], ("hi", 7), ("itr", 7))
            pe.wait_ge(f_ok, 8)
            freed(pe, ("hq", 7))
            for l in range(8):
                if l:
                    pe.wait_ge(lev_x, l)
                for j in range(4):
                    name = ("lv", l, j)
                    claim(name)
                    for a in range(4):
                        h, t = 2 * j + a // 2, a % 2
                        if l:
                            L = lev[(l - 1) % 2].rearrange("p (h t) -> p h t", h=8)
                            x, y = L[:, h, P * t:P * t + P], L[:, h, P * t:P * t + P]
                        else:
                            x, y = hk[:, h, P * t:P * t + P], hq[:, h, P * t:P * t + P]
                        i = mm(bank(name)[:, P * a:P * a + P], x, y)
                    close(i, name)
            pe.wait_ge(lev_x, 8)
            L = lev[1].rearrange("p (h t) -> p h t", h=8)
            for j in range(2):
                claim(("cr", j))
                for a in range(4):
                    h = 4 * j + a
                    i = mm(bank(("cr", j))[:, P * a:P * a + P], L[:, h, 0:P], L[:, h, P:256])
                close(i, ("cr", j))
            pe.wait_ge(lev_x, 9)
            L = lev[0].rearrange("p (n t) -> p n t", t=P)
            for j in range(4):
                claim(("kt", j))
                for a in range(4):
                    i = nc.tensor.transpose(bank(("kt", j))[:, P * a:P * a + P], L[:, 4 * j + a, :], ident)
                close(i, ("kt", j))
            freed(pe, ("itr", 7))
            freed(pe, ("itr", 6))
            for j in range(2):
                freed(pe, ("kt", 2 * j))
                freed(pe, ("kt", 2 * j + 1))
                claim(("hs", j))
                for a in range(4):
                    h = 4 * j + a
                    for st in range(2):
                        i = mm(bank(("hs", j))[:, P * a:P * a + P], kd_tok[:, 2 * h + st, :],
                               i_tok[:, st, P * h:P * h + P], st == 0, st == 1)
                close(i, ("hs", j))
            freed(pe, ("lv", 7, 3))
            freed(pe, ("cr", 0))
            freed(pe, ("cr", 1))
            for j in range(4):
                claim(("ho", j))
                for a in range(2):
                    h = 2 * j + a
                    o = bank(("ho", j))[:, 256 * a:256 * a + 256]
                    i0, i1 = i_tok[:, 0, P * h:P * h + P], i_tok[:, 1, P * h:P * h + P]
                    mm(o[:, 0:P], i0, att[:, h, 0, :])
                    mm(o[:, P:256], i0, cross[:, h, :], True, False)
                    i = mm(o[:, P:256], i1, att[:, h, 1, :], False, True)
                close(i, ("ho", j))
            claim(("hso", 0))
            for b in range(NS):
                pe.wait_ge(hu_new, b + 1)
                for h in range(HH):
                    i = mm(bank(("hso", 0))[:, NS * h + b:NS * h + b + 1], hunit[b % 2][:, 0, P * h:P * h + P],
                           hq[:, h, NP_ + b:NP_ + b + 1])
                if b < NS - 1:
                    i.then_inc(hu_pe, 1)
            close(i, ("hso", 0))
            pe.wait_ge(sq_ok, RH + 1)
            claim(("hvar", 0))
            for h in range(HH):
                i = mm(bank(("hvar", 0), 8)[:, 0:NT], col_hg[:, h, :], hsq[:, h, :], h == 0, h == 7)
            close(i, ("hvar", 0))
            pe.wait_ge(r8_ok, 2)
            for h in range(HH):
                claim(("hrs", h))
                close(mm(bank(("hrs", h))[:, 0:NT], rowsel[0:8, h, :], rstd[0:8, :]), ("hrs", h))
            pe.wait_ge(o_ok, RH + 1)
            for i_ in range(8):
                p_ = ("hwo", i_ // 4)
                if i_ % 4 == 0:
                    arrive(p_)
                w = pview(p_, 8)
                claim(("hw", i_))
                for k in range(KD):
                    i = mm(bank(("hw", i_))[:, 0:NT], w[:, k, P * (i_ % 4):P * (i_ % 4) + P], oH[:, k, :], k == 0, k == 7)
                close(i, ("hw", i_))
            mean_square(3)
            pe.wait_ge(h_ready, 32)
            for j in range(12):
                src, t, q = (xT, j // 2, j % 2) if j < 6 else (hT, (j - 6) // 2, j % 2)
                m = P if t < 2 else NS
                claim(("tok", j))
                for a in range(4):
                    i = nc.tensor.transpose(bank(("tok", j))[0:m, P * a:P * a + P], src[:, 4 * q + a, P * t:P * t + m],
                                            ident)
                close(i, ("tok", j))
            pe.wait_ge(rt_in, 32)
            claim(("lg", 0))
            for t in range(3):
                m = P if t < 2 else NS
                for k in range(KD):
                    i = mm(bank(("lg", 0))[0:m, 8 * t:8 * t + 8], hT[:, k, P * t:P * t + m], w_rt[:, k, :], k == 0, k == 7)
            close(i, ("lg", 0))
            pe.wait_ge(mask_ok, 1)
            claim(("rk", 0))
            for t in range(4):
                for s in range(min(t + 1, 3)):
                    i = mm(bank(("rk", 0))[:, 8 * t:8 * t + 8], cc("ltri") if s == t else ones, mm_[:, s, :],
                           s == 0, s == min(t, 2))
            close(i, ("rk", 0))
            for j in range(6, 12):
                freed(pe, ("tok", j))
            freed(pe, ("rk", 0))
            pe.wait_ge(route_ok, 1)
            rounds = pe.value_load(nri[0:1, 0:1], min_val=1, max_val=ROUNDS)
            with pe.Fori(0, rounds) as r:
                with pe.Fori(0, NE) as e:
                    n = r * NE + e

                    def expert_arrived(kind, c):
                        t = epos[kind, c]
                        pe.wait_ge(moe_arrived[t % RING], n * (16 * (EP // RING)) + 16 * (t // RING + 1))

                    def up(c):
                        pe.wait_ge(hide_ok, n * NCH + (1 + max(c - 1, 0)))
                        for z, kind in enumerate("gu"):
                            expert_arrived(kind, c)
                            w = piece(epos[kind, c] % RING).rearrange("p (k n) -> p k n", k=8)
                            for j in range(4):
                                for k in range(KD):
                                    i = mm(ps[:, 2 * z + c % 2, C * j:C * j + C], w[:, k, P * j:P * j + P],
                                           xe[:, k, :], k == 0, k == 7)
                            i.then_inc(piece_used, 1)

                    def down(c):
                        expert_arrived("d", c)
                        pe.wait_ge(hide_ok, n * NCH + (c + 2))
                        w = piece(epos["d", c] % RING).rearrange("p (k n) -> p k n", k=4)
                        if c == 0:
                            pe.wait_ge(y_free, n + 1)
                        for j in range(4):
                            for q in range(2):
                                i = mm(ps[0:C, 4 + q, :], hide[:, c % 2, C * j:C * j + C],
                                       w[:, j, 512 * q:512 * q + 512], c + j == 0, c + j == NCH + 2)
                        i.then_inc(piece_used, 1)

                    pe.wait_ge(sel_ok, n + 1)
                    for k in range(KD):
                        for t in range(3):
                            i = mm(ps[:, 6 + k // 4, C * (k % 4):C * (k % 4) + C], h_tok[:, t, P * k:P * k + P],
                                   gsel[:, t, :], t == 0, t == 2)
                    i.then_inc(xg_full, 1)
                    pe.wait_ge(xe_ok, n * 2 + 2)
                    for c in range(NCH + 1):
                        if c < NCH:
                            up(c)
                        if c:
                            down(c - 1)


INPUTS = ["x_prompt", "x_sample", "state_retention", "state_hgrn", "norm_mix_g", "norm_ffn_g", "final_norm_g",
          "ret_w_in", "ret_gn_g", "ret_w_out", "hg_w_in", "hg_lb_param", "hg_norm_g", "hg_w_out", "ffn_w_gate",
          "ffn_w_up", "ffn_w_down", "moe_router", "moe_w_gate", "moe_w_up", "moe_w_down"]
OUTPUTS = [("y_p", (1, NP_, D)), ("y_s", (NS, 1, D)), ("ret_p", (1, 1, RH, RDK, RDV)),
           ("ret_s", (1, NS, RH, RDK, RDV)), ("hg_p", (1, 1, HH, P, P)), ("hg_s", (1, NS, HH, P, P))]


def kernel(**inputs):
    import concourse.bacc as bacc
    from concourse.bass_utils import run_bass_kernel_spmd

    nc = bacc.Bacc("TRN2", target_bir_lowering=False, num_devices=1)
    arrays = {name: np.ascontiguousarray(inputs[name]) for name in INPUTS}
    arrays["consts"] = constants()
    ins = {n: nc.dram_tensor("in_" + n, a.shape, mybir.dt.from_np(a.dtype), kind="ExternalInput").ap()
           for n, a in arrays.items()}
    outs = {n: nc.dram_tensor("out_" + n, s, F32, kind="ExternalOutput").ap() for n, s in OUTPUTS}
    hybrid_step(nc, ins, outs)
    r = run_bass_kernel_spmd(nc, [{"in_" + n: a for n, a in arrays.items()}], core_ids=[0])
    return tuple(r.results[0]["out_" + n] for n, _ in OUTPUTS)
```

```python
from contextlib import ExitStack

import numpy as np

import concourse.bass as bass
from concourse import mybir

ALU = mybir.AluOpType
ACT = mybir.ActivationFunctionType
F32 = mybir.dt.float32
F32R = mybir.dt.float32r
I32 = mybir.dt.int32
U32 = mybir.dt.uint32
AX = mybir.AxisListType

P = 128
D = 1024
KD = D // P
NP_ = 256
NS = 8
NT = NP_ + NS
PAST = 2048
RH, RDK, RDV = 4, 256, 512
HH = 8
FF = 2816
FT = FF // P
NE, FE = 8, 3584
C = 96
ROUNDS = -(-NT // C)
CHUNK = 64
NEPS, GEPS = 1e-6, 1e-5

PIECE = 4096
RING = 7
DRING = 5
EP = 3 * (FE // 512)
WPL = 3
UNITS = 4

CONST = {}
_at = 0
for _n, _w in (("cos", NT), ("sin", NT), ("dmask", RH * 256), ("dout", 2 * RH), ("ident", P), ("mean_d", P),
               ("mean_gn", P), ("ones", P), ("col_gn", 64), ("col_hg", 64), ("rowsel", 8 * P),
               ("ltri", P), ("slot", C), ("exp8", 8), ("valid", 3), ("reset", NP_), ("lvl", 7 * P), ("eps", 2)):
    CONST[_n] = (_at, _at + _w)
    _at += _w
NCONST = _at


def constants():
    c = np.zeros((P, NCONST), np.float32)

    def put(name, v):
        a, b = CONST[name]
        c[:v.shape[0], a:b] = v.reshape(v.shape[0], -1)

    f = np.float32
    half = RDK // 2
    inv = np.power(f(10000.0), -np.arange(half, dtype=f) / f(half)).astype(f)
    pos = np.concatenate([np.arange(NP_), PAST + np.zeros(NS)]).astype(f)
    ang = (pos[None, :] * inv[:, None]).astype(f)
    put("cos", np.cos(ang))
    put("sin", np.sin(ang))
    lg = np.log1p(-np.exp2(-5.0 - np.arange(RH)))
    s, t = np.arange(P)[:, None], np.arange(P)[None, :]
    scale = RDK ** -0.5
    dm = np.zeros((P, RH, 2, P))
    for h in range(RH):
        dm[:, h, 0] = np.where(t >= s, np.exp(np.maximum(t - s, 0) * lg[h]), 0.0) * scale
        dm[:, h, 1] = np.exp((t + P - s) * lg[h]) * scale
    put("dmask", dm.astype(f))
    do = np.zeros((P, 2, RH))
    for st in range(2):
        for h in range(RH):
            do[:, st, h] = np.exp((NP_ - 1 - st * P - np.arange(P)) * lg[h]) * scale
    put("dout", do.astype(f))
    put("ident", np.eye(P, dtype=f))
    put("mean_d", np.full((P, P), 1.0 / D, f))
    put("mean_gn", np.full((P, P), 1.0 / RDV, f))
    put("ones", np.ones((P, P), f))
    put("col_gn", np.broadcast_to(np.eye(8) / RDV, (P, 8, 8)).astype(f))
    put("col_hg", np.broadcast_to(np.eye(8) / P, (P, 8, 8)).astype(f))
    put("rowsel", np.broadcast_to(np.eye(8)[:, :, None], (8, 8, P)).astype(f))
    put("ltri", (s < t).astype(f))
    put("slot", np.broadcast_to(np.arange(C), (P, C)).astype(f))
    put("exp8", np.broadcast_to(np.arange(8), (P, 8)).astype(f))
    va = np.ones((P, 3), f)
    va[NS:, 2] = 0
    put("valid", va)
    put("reset", np.broadcast_to((np.arange(NP_) % CHUNK != 0), (P, NP_)).astype(f))
    lv = np.zeros((P, 7, P), f)
    for l in range(7):
        m = 1 << l
        lv[:, l] = (s // (2 * m) == t // (2 * m)) & (s % (2 * m) < m) & (t % (2 * m) >= m)
    put("lvl", lv)
    put("eps", np.broadcast_to(np.array([NEPS, GEPS]), (P, 2)).astype(f))
    return c


GAMMA = [float(np.float32(1.0 - 2.0 ** (-5 - h))) for h in range(RH)]

VEC = {"mix": 0, "ffn": 16, "gn": 32, "hgn": 48, "lb": 56}
NVEC = 72


RWI_ORDER = (0, 2, 4, 5, 1, 3, 6, 7, 8, 9, 10, 11)
QK_TILES = [[4 * g + i for i in range(4)] + [8 + 4 * g + i for i in range(4)] for g in range(2)]


def fills():
    order = []
    add = order.append
    for j in range(4):
        add((("xt", j), 4 + j))
    add((("xt", 4), 0))
    add((("xt", 5), 1))
    add((("ms", 0), 7))
    n = 0

    def tile(kind, i):
        nonlocal n
        add(((kind, i), n % 4))
        n += 1

    for g in range(2):
        for i in QK_TILES[g]:
            tile("qk", i)
        for i in range(8 * g, 8 * g + 8):
            tile("v", i)
            if i % 8:
                add((("vtr", i - 1), 4 + (i - 1) % 2))
        add((("vtr", 8 * g + 7), 5))
        if g == 1:
            add((("so", 0), 6))
        for h in (2 * g, 2 * g + 1):
            add((("sc", h), 6))
            add((("kdt", h), 7))
            add((("o", h, 0), 4))
            add((("o", h, 1), 5))
            add((("st", h, 0), 6))
            add((("st", h, 1), 7))
    add((("so", 1), 6))
    for i in range(16):
        tile("g", i)
    for h in range(RH):
        add((("mu", h), (4, 5, 7, 6)[h]))
    add((("var", 0), 4))
    for h in range(RH):
        add((("rs", h), (5, 6, 7, 5)[h]))
    for i in range(8):
        tile("wo", i)
    add((("ms", 1), 7))
    for i in range(FT):
        tile("fg", i)
        tile("fu", i)
    for i in range(8):
        tile("fd", i)
    add((("ms", 2), 7))
    for i in range(8):
        tile("hf", i)
    for i in range(8):
        tile("hi", i)
        if i:
            add((("itr", i - 1), 4 + (i - 1) % 2))
    add((("itr", 7), 5))
    for i in range(8):
        tile("hq", i)
    add((("hso", 0), 3))
    for lv in range(8):
        for j in range(4):
            add((("lv", lv, j), 4 + j))
        add((("hg", lv), lv % 3))
    for j in range(2):
        add((("cr", j), 4 + j))
    for j in range(4):
        add((("kt", j), (6, 7, 0, 1)[j]))
    for j in range(2):
        add((("hs", j), (2, 0)[j]))
    for j in range(4):
        add((("ho", j), 4 + j))
    add((("hvar", 0), 1))
    for h in range(HH):
        add((("hrs", h), 2 + h % 4))
    assert n % 4 == 0
    for i in range(8):
        tile("hw", i)
    add((("ms", 3), 7))
    for j in range(12):
        add((("tok", j), j % 6))
    add((("lg", 0), 6))
    add((("rk", 0), 7))
    count = [0] * 8
    out = {}
    for name, b in order:
        assert name not in out
        out[name] = (b, count[b])
        count[b] += 1
    return out, count


def hybrid_step(nc, ins, outs):
    FILL, BANKS = fills()
    with ExitStack() as ctx:
        def sb(name, shape, dt=F32, scope=ctx):
            return scope.enter_context(nc.sbuf_tensor(name, shape, dt))

        def sem(name):
            return ctx.enter_context(nc.semaphore(name))

        ring = sb("ring", [P, RING * PIECE])
        cst = sb("cst", [P, NCONST])
        vec = sb("vec", [P, NVEC])
        lbt = sb("lbt", [P, 8, 8])
        small = sb("small", [P, 320])
        with ExitStack() as dense_memory:
            arena = sb("arena", [P, 14256], scope=dense_memory)
            x_mem = sb("xT", [P, KD * NT], scope=dense_memory)
            h_mem = sb("hT", [P, KD * NT], scope=dense_memory)
            std = sb("std", [P, NT], scope=dense_memory)
            rstd = sb("rstd", [P, NT], scope=dense_memory)
        earena = sb("expert_arena", [P, 11288])
        hide_parts = sb("hide_parts", [P, 2 * 2 * 4 * C], F32R)
        w_parts = sb("down_weight_parts", [P, 2 * WPL * D], F32R)
        ps = ctx.enter_context(nc.psum_tensor("ps", [P, 8, 512], F32))

        def piece(s):
            return ring[:, s * PIECE:(s + 1) * PIECE]

        def cc(name):
            a, b = CONST[name]
            return cst[:, a:b]

        ident, ones = cc("ident"), cc("ones")
        cos, sin = cc("cos"), cc("sin")
        dmask = cc("dmask").rearrange("p (h t) -> p h t", h=RH)
        dout = cc("dout").rearrange("p (s h) -> p s h", s=2)
        col_gn = cc("col_gn").rearrange("p (h m) -> p h m", h=8)
        col_hg = cc("col_hg").rearrange("p (h m) -> p h m", h=8)
        rowsel = cc("rowsel").rearrange("p (h m) -> p h m", h=8)
        lvl = cc("lvl").bitcast(I32).rearrange("p (l m) -> p l m", l=7)
        eps_n, eps_g = cc("eps")[:, 0:1], cc("eps")[:, 1:2]

        def part(tensor, a, *shape):
            n = int(np.prod(shape))
            v = tensor[:, a:a + n]
            if len(shape) == 2:
                return v.rearrange("p (a b) -> p a b", a=shape[0])
            if len(shape) == 3:
                return v.rearrange("p (a b c) -> p a b c", a=shape[0], b=shape[1])
            return v

        xT = part(x_mem, 0, KD, NT)
        hT = part(h_mem, 0, KD, NT)
        scratch = DRING * PIECE
        x_in = part(arena, 0, 3, D)
        vrow = part(arena, 3 * D, P)
        qT = part(arena, 0, 8, NT)
        kT = part(arena, 2112, 8, NT)
        v_tok = part(arena, 4224, 2, 2048)
        gT = part(arena, 4224, 16, NT)
        oT = part(arena, 8448, 16, NT)
        v_smp = arena[0:NS, 8448 + 8 * NT:8448 + 8 * NT + 2048]
        rot = part(arena, 12672, 4, NT)
        prob = part(arena, 12672, 384)
        sqg = part(arena, 12672, 4, NT)
        tmpT = part(arena, 13728, 2, NT)
        kdec = part(arena, 13728, 2, 256)
        unit = part(ring, scratch, UNITS, 1536)
        s_out = part(ring, scratch + UNITS * 1536, 2, 1024)
        ksmp = part(small, 0, 8, 8)
        hid = part(arena, 0, FT, NT)
        sg = part(arena, FT * NT, 2, NT)
        hq = part(arena, 0, 8, NT)
        hf = part(arena, 2112, 8, NT)
        att = part(arena, 2112, 8, 2, P)
        hsq = part(arena, 2112, 8, NT)
        hk = part(arena, 4224, 8, NT)
        hgt = part(arena, 6336, 8, NT)
        bcum = part(arena, 8448, 8, NP_)
        kd_tok = part(arena, 8448, 16, P)
        i_tok = part(arena, 10496, 2, D)
        cross = part(arena, 12544, 8, P)
        i_smp = arena[0:NS, 12544:12544 + D]
        itmp = part(arena, 13568, 2, NT)
        lev = [part(ring, scratch + 2048 * j, 2048) for j in range(2)]
        hunit = [part(ring, scratch + 4096 + 2048 * j, 2, D) for j in range(2)]
        hs_out = part(ring, scratch, 8, P)
        oH = hT
        fsmp = part(small, 64, 8, 8)
        tots = part(small, 128, 4, 8)
        x_tok = part(earena, 0, 3, D)
        h_tok = part(earena, 3072, 3, D)
        gfin = part(earena, 6144, D)
        gsel = part(earena, 7168, 3, C)
        xe = part(earena, 7456, 8, C)
        act_g = part(earena, 8224, 2, 4 * C)
        hide = part(earena, 8992, 2, 4 * C)
        y_out = part(earena, 9760, D)
        hide_hi = part(hide_parts, 0, 2, 4 * C)
        hide_lo = part(hide_parts, 8 * C, 2, 4 * C)
        w_hi = part(w_parts, 0, WPL, D)
        w_lo = part(w_parts, WPL * D, WPL, D)
        RB = 10784
        w_rt = part(earena, RB, 8, 8)
        lg = part(earena, RB + 64, 3, 8)
        prb = part(earena, RB + 88, 3, 8)
        m8 = part(earena, RB + 112, 3, 8)
        ix = earena[:, RB + 136:RB + 160].bitcast(U32).rearrange("p (a b) -> p a b", a=3)
        ixf = part(earena, RB + 160, 3, 8)
        oa = part(earena, RB + 184, 3, 8)
        ob = part(earena, RB + 208, 3, 8)
        mm_ = part(earena, RB + 232, 3, 8)
        rk = part(earena, RB + 256, 4, 8)
        r1 = part(earena, RB + 288, 3, 8)
        reff = part(earena, RB + 312, 3, ROUNDS * 8 + 8)
        wab = part(earena, RB + 440, 3, 4)
        va = part(earena, RB + 452, 2, 3)
        vt = part(earena, RB + 458, 2, 3)
        rowf = part(earena, RB + 464, 2, 3)
        rowi = earena[:, RB + 470:RB + 476].bitcast(U32).rearrange("p (a b) -> p a b", a=2)
        nrf = part(earena, RB + 476, 4)
        nri = earena[:, RB + 480:RB + 481].bitcast(I32)
        red3 = part(earena, RB + 484, 3)
        fsum = part(earena, RB + 488, 3)
        frs = part(earena, RB + 492, 3)
        ya = part(ring, 0, 3, D)
        yb = part(ring, 3072, 3, D)
        yf = part(ring, 6144, 3, D)
        ysq = part(ring, 9216, D)

        v_scr = nc.dram_tensor("v_scr", (NS, 2048), F32)
        i_scr = nc.dram_tensor("i_scr", (NS, D), F32)
        y_scr = nc.dram_tensor("y_scr", (ROUNDS * NE * C, D), F32)

        s_x = sem("tokens_loaded")
        s_c = sem("constants_loaded")
        s_v = sem("vectors_loaded")
        bank_full = [sem(f"bank_full{b}") for b in range(8)]
        bank_free = [sem(f"bank_free{b}") for b in range(8)]
        arrived = [sem(f"piece_arrived{s}") for s in range(DRING)]
        moe_arrived = [sem(f"expert_piece_arrived{s}") for s in range(RING)]
        piece_used = sem("piece_used")
        lb_in = sem("bound_shifted")
        lb_exp = sem("bound_exponentials")
        squares = sem("squares")
        h_ready = sem("h_ready")
        dve_step = sem("dve_step")
        act_step = sem("act_step")
        pool_step = sem("pool_step")
        hgate_ok = sem("hgrn_gate_ready")
        qk_ready = sem("qk_rotated")
        sq_summed = sem("squares_summed")
        pad_ok = sem("pad_rows_cleared")
        e_in = sem("softmax_shifted")
        fin_in = sem("combined")
        fin_mean = sem("final_mean")
        v_stored = sem("v_stored")
        s_store = [sem(f"ret_state_stored{j}") for j in range(2)]
        unit_s = [sem(f"unit_state_in{j}") for j in range(UNITS)]
        unit_v = [sem(f"unit_v_in{j}") for j in range(UNITS)]
        unit_new = sem("unit_updated")
        unit_pe = sem("unit_multiplied")
        unit_out = [sem(f"unit_stored{j}") for j in range(UNITS)]
        sq_ok = sem("o_squares")
        r8_ok = sem("row_rstd_ready")
        o_ok = sem("o_ready")
        f_ok = sem("forget_ready")
        logf_ok = sem("logf_ready")
        i_stored = sem("i_stored")
        lev_sub = sem("level_exponents")
        lev_exp = sem("level_exp")
        lev_x = sem("level_operands")
        hs_store = sem("hgrn_state_stored")
        hu_in = [sem(f"hunit_state_in{j}") for j in range(2)]
        hu_i = [sem(f"hunit_i_in{j}") for j in range(2)]
        hu_new = sem("hunit_updated")
        hu_pe = sem("hunit_multiplied")
        hu_out = [sem(f"hunit_stored{j}") for j in range(2)]
        rt_in = sem("router_loaded")
        e_ok = sem("softmax_exp")
        mask_ok = sem("choice_ready")
        route_ok = sem("routing_ready")
        sel_ok = sem("selection_ready")
        xg_full = sem("gathered")
        xe_ok = sem("expert_x_ready")
        gate_ok = sem("expert_silu_ready")
        hide_ok = sem("expert_hidden_ready")
        hide_hi_ok = sem("expert_hidden_high")
        hide_lo_ok = sem("expert_hidden_low")
        w_hi_ok = sem("down_weights_high")
        w_lo_ok = sem("down_weights_low")
        w_used = sem("down_weights_used")
        y_free = sem("expert_y_copied")
        y_store = sem("expert_y_stored")
        zero_ok = sem("zeros_ready")
        zero_stored = sem("zeros_stored")
        all_stored = sem("all_y_stored")
        ya_in = sem("rows_gathered")
        fin_sq = sem("final_squares")
        fin_std = sem("final_std")
        fin_ok = sem("final_ready")
        out_done = sem("outputs_stored")

        def bank(name, parts=P):
            return ps[0:parts, FILL[name][0], :]

        def filled(eng, name):
            b, k = FILL[name]
            eng.wait_ge(bank_full[b], k + 1)

        def frees(ins, name):
            ins.then_inc(bank_free[FILL[name][0]], 1)

        def freed(eng, name):
            b, k = FILL[name]
            eng.wait_ge(bank_free[b], k + 1)

        rwi = ins["ret_w_in"][0].rearrange("(k p) n -> p k n", p=P)
        rwo = ins["ret_w_out"][0].rearrange("(k p) n -> p k n", p=P)
        fwg = ins["ffn_w_gate"][0].rearrange("(k p) n -> p k n", p=P)
        fwu = ins["ffn_w_up"][0].rearrange("(k p) n -> p k n", p=P)
        fwd = ins["ffn_w_down"][0].rearrange("(k p) n -> p k n", p=P)
        hwi = ins["hg_w_in"][0].rearrange("(k p) n -> p k n", p=P)
        hwo = ins["hg_w_out"][0].rearrange("(k p) n -> p k n", p=P)
        dense = []
        for j in RWI_ORDER:
            dense.append((("rwi", j), [(rwi[:, :, 512 * j:512 * j + 512], 8, 512, 0)]))
        for j in range(4):
            dense.append((("rwo", j), [(rwo[:, :, 256 * j:256 * j + 256], 16, 256, 0)]))
        for j in range(11):
            dense.append((("fgu", j), [(fwg[:, :, 256 * j:256 * j + 256], 8, 256, 0),
                                       (fwu[:, :, 256 * j:256 * j + 256], 8, 256, 2048)]))
        for j in range(8):
            a, kh = j // 2, j % 2
            dense.append((("fd", j), [(fwd[:, 11 * kh:11 * kh + 11, 256 * a:256 * a + 256], 11, 256, 0)]))
        HG_ORDER = (1, 2, 0, 3)
        for a, part_ in enumerate(HG_ORDER):
            for j in range(2):
                o = 1024 * part_ + 512 * j
                dense.append((("hwi", 2 * a + j), [(hwi[:, :, o:o + 512], 8, 512, 0)]))
        for j in range(2):
            dense.append((("hwo", j), [(hwo[:, :, 512 * j:512 * j + 512], 8, 512, 0)]))
        NDENSE = len(dense)
        assert NDENSE % DRING == 0
        last_tile = {}
        last_tile.update({("rwi", j): (("qk", 4 * j + 3) if j < 4 else ("v", 4 * j - 13) if j < 8 else ("g", 4 * j - 29))
                          for j in range(12)})
        last_tile.update({("rwo", j): ("wo", 2 * j + 1) for j in range(4)})
        last_tile.update({("fgu", j): ("fu", 2 * j + 1) for j in range(11)})
        last_tile.update({("fd", j): ("fd", 2 * (j // 2) + 1) for j in range(8)})
        last_tile.update({("hwi", j): (("hf", "hi", "hq", "hg")[j // 2], 4 * (j % 2) + 3) for j in range(8)})
        last_tile.update({("hwo", j): ("hw", 4 * j + 3) for j in range(2)})
        where, need, got = {}, {}, [0] * DRING
        for n, (name, loads) in enumerate(dense):
            got[n % DRING] += 16 * len(loads)
            where[name] = n % DRING
            need[name] = got[n % DRING]
        moe_g = ins["moe_w_gate"][0].rearrange("e (k p) n -> p e k n", p=P)
        moe_u = ins["moe_w_up"][0].rearrange("e (k p) n -> p e k n", p=P)
        moe_d = ins["moe_w_down"][0].rearrange("e (k p) n -> p e k n", p=P)
        NCH = FE // 512
        epieces = []
        for c in range(NCH + 1):
            if c < NCH:
                epieces += [("g", c), ("u", c)]
            if c:
                epieces.append(("d", c - 1))
        assert len(epieces) == EP and EP % RING == 0
        epos = {name: t for t, name in enumerate(epieces)}

        def moe_source(e, kind, c):
            if kind == "d":
                return moe_d[:, bass.ds(e, 1), 4 * c:4 * c + 4, :]
            w = moe_g if kind == "g" else moe_u
            return w[:, bass.ds(e, 1), :, 512 * c:512 * c + 512]

        def moe_dest(kind, t):
            v = piece(t % RING)
            if kind == "d":
                return v.rearrange("p (e k n) -> p e k n", e=1, k=4)
            return v.rearrange("p (e k n) -> p e k n", e=1, k=8)

        ret_in = ins["state_retention"][0].rearrange("b h (k p) e -> b h p k e", p=P)
        ret_out = outs["ret_s"][0].rearrange("b h (k p) e -> b h p k e", p=P)
        ret_pout = outs["ret_p"][0, 0].rearrange("h (k p) e -> h p k e", p=P)
        hg_in = ins["state_hgrn"][0].rearrange("b h d e -> b d h e")
        hg_out = outs["hg_s"][0].rearrange("b h d e -> b d h e")
        hg_pout = outs["hg_p"][0, 0].rearrange("h d e -> d h e")

        block = ctx.enter_context(nc.Block())

        def unit_of(u):
            g, v = divmod(u, 16)
            return v // 2, 2 * g + v % 2

        @block.sync
        def _(sp):
            sp.wait_ge(s_x, 32)
            sp.wait_ge(s_c, 16)
            for n, (name, loads) in enumerate(dense):
                if n >= DRING:
                    filled(sp, last_tile[dense[n - DRING][0]])
                for src, k, w, off in loads:
                    dst = piece(n % DRING)[:, off:off + k * w].rearrange("p (k n) -> p k n", k=k)
                    sp.dma_start(dst, src).then_inc(arrived[n % DRING], 16)

            def reused(e, t):
                prev = t - RING
                if prev < 0:
                    e, prev = e - 1, prev + EP
                kind, c = epieces[prev]
                if kind == "d":
                    sp.wait_ge(w_lo_ok, e * (4 * NCH) + 4 * (c + 1))
                else:
                    sp.wait_ge(piece_used, e * (2 * NCH) + (2 * c + (kind == "u") + 1))

            for t, (kind, c) in enumerate(epieces):
                if t < DRING:
                    filled(sp, last_tile[dense[NDENSE - DRING + t][0]])
                elif t < RING:
                    filled(sp, ("hrs", 7))
                    sp.wait_ge(hs_store, 16)
                    freed(sp, ("kt", 3))
                    for j in range(2):
                        sp.wait_ge(hu_out[j], 16 * (NS // 2))
                else:
                    reused(0, t)
                sp.dma_start(moe_dest(kind, t), moe_source(0, kind, c)).then_inc(moe_arrived[t % RING], 16)

            def expert(e, i):
                for t, (kind, c) in enumerate(epieces):
                    reused(i, t)
                    sp.dma_start(moe_dest(kind, t), moe_source(e, kind, c)).then_inc(moe_arrived[t % RING], 16)

            with sp.Fori(1, NE) as e:
                expert(e, e)
            sp.wait_ge(route_ok, 1)
            rounds = sp.value_load(nri[0:1, 0:1], min_val=1, max_val=ROUNDS)
            with sp.If(rounds > 1):
                with sp.Fori(1, rounds) as r:
                    with sp.Fori(0, NE) as e:
                        expert(e, r * NE + e)

        @block.gpsimd
        def _(pool):
            def load_state(u):
                b, h = unit_of(u)
                j = u % UNITS
                if u >= UNITS:
                    w = u - UNITS
                    if w % 16 == 15:
                        filled(pool, ("so", w // 16))
                    else:
                        pool.wait_ge(unit_pe, w + 1 - w // 16)
                    pool.wait_ge(unit_out[j], 16 * (u // UNITS))
                pool.dma_start(unit[:, j, 0:1024].rearrange("p (k e) -> p k e", k=2), ret_in[b, h])\
                    .then_inc(unit_s[j], 16)

            for u in range(UNITS):
                load_state(u)
            for u in range(NS * RH + 2):
                if u < NS * RH:
                    b, h = unit_of(u)
                    j = u % UNITS
                    if u >= UNITS:
                        load_state(u)
                    if u % 16 == 0:
                        g = u // 16
                        freed(pool, ("vtr", 8 * g + 6))
                        freed(pool, ("vtr", 8 * g + 7))
                        pool.dma_start(v_scr[:, D * g:D * g + D], v_smp[:, D * g:D * g + D]).then_inc(v_stored, 16)
                        pool.wait_ge(v_stored, 16 * (g + 1))
                    pool.dma_start(unit[:, j, 1024:1536], v_scr[b, 512 * h:512 * h + 512].partition_broadcast(P))\
                        .then_inc(unit_v[j], 16)
                if u >= 2:
                    w = u - 2
                    b, h = unit_of(w)
                    pool.wait_ge(unit_new, w + 1)
                    pool.dma_start(ret_out[b, h], unit[:, w % UNITS, 0:1024].rearrange("p (k e) -> p k e", k=2))\
                        .then_inc(unit_out[w % UNITS], 16)

            filled(pool, ("so", 1))
            for h in range(UNITS):
                pool.wait_ge(unit_out[h], 16 * NS)
            pool.wait_ge(s_store[0], 32)
            pool.wait_ge(s_store[1], 32)
            nc.gpsimd.memset(hunit[1][:, 1, :], 0.0).then_inc(zero_ok, 1)
            pool.wait_ge(zero_ok, 1)
            nz = (ROUNDS - 1) * NE * C // P
            pool.dma_start(y_scr[NE * C:, :].rearrange("(t p) d -> p t d", p=P),
                           hunit[1][:, 1:2, :].to_broadcast([P, nz, D])).then_inc(zero_stored, 16)

            def load_h(b):
                if b >= 2:
                    pool.wait_ge(hu_pe, b - 1)
                    pool.wait_ge(hu_out[b % 2], 16 * (b // 2))
                pool.dma_start(hunit[b % 2][:, 0, :].rearrange("p (h e) -> p h e", h=8), hg_in[b])\
                    .then_inc(hu_in[b % 2], 16)

            load_h(0)
            load_h(1)
            freed(pool, ("itr", 6))
            freed(pool, ("itr", 7))
            pool.dma_start(i_scr[:, :], i_smp).then_inc(i_stored, 16)
            pool.wait_ge(i_stored, 16)
            pool.wait_ge(f_ok, 8)
            pool.wait_ge(zero_stored, 16)
            steps = [0]

            def link(i):
                steps[0] += 1
                i.then_inc(pool_step, 1)
                pool.wait_ge(pool_step, steps[0])

            def load_i(b):
                pool.dma_start(hunit[b % 2][:, 1, :], i_scr[b, :].partition_broadcast(P)).then_inc(hu_i[b % 2], 16)

            load_i(0)
            load_i(1)
            G = nc.gpsimd
            for b in range(NS):
                S = hunit[b % 2][:, 0, :].rearrange("p (h e) -> p h e", h=8)
                I = hunit[b % 2][:, 1, :].rearrange("p (h e) -> p h e", h=8)
                pool.wait_ge(hu_in[b % 2], 16 * (b // 2 + 1))
                G.tensor_tensor(S, S, fsmp[:, :, b:b + 1].to_broadcast([P, 8, P]), ALU.mult)
                pool.wait_ge(hu_i[b % 2], 16 * (b // 2 + 1))
                link(G.tensor_tensor(I, I, hk[:, :, NP_ + b:NP_ + b + 1].to_broadcast([P, 8, P]), ALU.mult))
                G.tensor_tensor(S, S, I, ALU.add).then_inc(hu_new, 1)
                pool.wait_ge(hu_new, b + 1)
                pool.dma_start(hg_out[b], hunit[b % 2][:, 0, :].rearrange("p (h e) -> p h e", h=8))\
                    .then_inc(hu_out[b % 2], 16)
                if b + 2 < NS:
                    load_i(b + 2)
                    load_h(b + 2)

            pool.wait_ge(all_stored, 1)
            for w, dst in enumerate((ya, yb)):
                for t in range(3):
                    m = P if t < 2 else NS
                    pool.indirect_dma_start(dst[0:m, t, :], None, y_scr[:, :],
                                            bass.IndirectOffsetOnAxis(ap=rowi[0:m, w, t:t + 1], axis=0))\
                        .then_inc(ya_in, 16)

        @block.scalar
        def _(act):
            A = nc.scalar
            steps = [0]

            def link(i):
                steps[0] += 1
                i.then_inc(act_step, 1)
                act.wait_ge(act_step, steps[0])

            act.dma_start(x_in[:, 0:2, :], ins["x_prompt"][0].rearrange("(t p) d -> p t d", p=P)).then_inc(s_x, 16)
            act.dma_start(x_in[0:NS, 2, :], ins["x_sample"].rearrange("b s d -> (b s) d")).then_inc(s_x, 16)
            act.dma_start(cst[:, :], ins["consts"]).then_inc(s_c, 16)
            for src, r, n in ((ins["norm_mix_g"].rearrange("l (k p) -> (l k) p", p=P), VEC["mix"], 16),
                              (ins["norm_ffn_g"].rearrange("l (k p) -> (l k) p", p=P), VEC["ffn"], 16),
                              (ins["ret_gn_g"].rearrange("l (k p) -> (l k) p", p=P), VEC["gn"], 16),
                              (ins["hg_norm_g"].rearrange("l (k p) -> (l k) p", p=P), VEC["hgn"], 8),
                              (ins["hg_lb_param"].rearrange("l (k p) -> (l k) p", p=P), VEC["lb"], 16)):
                act.dma_start(vrow[r:r + n, :], src).then_inc(s_v, 16)

            def norm(n):
                for hf_ in range(2):
                    if n:
                        freed(act, (("wo", "fd", "hw")[n - 1], 4 * hf_ + 3))
                        filled(act, (("wo", "fd", "hw")[n - 1], 7))
                    else:
                        for j in range(5):
                            freed(act, ("xt", j))
                    A.activation(hT[:, 4 * hf_:4 * hf_ + 4, :], xT[:, 4 * hf_:4 * hf_ + 4, :], ACT.Square)\
                        .then_inc(squares, 1)
                filled(act, ("ms", n))
                frees(A.activation(std[:, :], bank(("ms", n))[:, 0:NT], ACT.Sqrt, bias=eps_n), ("ms", n))

            act.wait_ge(s_c, 16)
            act.wait_ge(lb_in, 1)
            A.activation(lbt[:, 1:3, :], lbt[:, 1:3, :], ACT.Exp).then_inc(lb_exp, 1)
            norm(0)
            for g in range(2):
                for i in range(8 * g, 8 * g + 8):
                    filled(act, ("v", i))
                    if i % 8 >= 2:
                        filled(act, ("vtr", i - 2))
                    elif g:
                        filled(act, ("st", 1, 1))
                    frees(A.copy(tmpT[:, i % 2, :], bank(("v", i))[:, 0:NT]), ("v", i))
                for h in (2 * g, 2 * g + 1):
                    filled(act, ("kdt", h))
                    if h >= 1:
                        filled(act, ("st", h - 1, 1))
                    for st in range(2):
                        i = A.activation(kdec[:, st, :], bank(("kdt", h))[:, 256 * st:256 * st + 256], ACT.Copy,
                                         scale=dout[:, st, h:h + 1])
                    frees(i, ("kdt", h))
                    for j in range(2):
                        filled(act, ("o", h, j))
                        if h == 2 and j == 0:
                            act.wait_ge(v_stored, 32)
                        frees(A.copy(oT[:, 4 * h + 2 * j:4 * h + 2 * j + 2, 0:NP_],
                                     bank(("o", h, j)).rearrange("p (a t) -> p a t", a=2)), ("o", h, j))
                    for j in range(2):
                        filled(act, ("st", h, j))
                        if h >= 2 and j == 0:
                            act.wait_ge(s_store[h % 2], 16 * (h // 2))
                        i = A.copy(s_out[:, h % 2, 512 * j:512 * j + 512], bank(("st", h, j)))
                        frees(i, ("st", h, j))
                    freed(act, ("st", h, 1))
                    act.dma_start(ret_pout[h], s_out[:, h % 2, :].rearrange("p (k e) -> p k e", k=2))\
                        .then_inc(s_store[h % 2], 16)
            for i in range(16):
                filled(act, ("g", i))
                frees(A.activation(gT[:, i, :], bank(("g", i))[:, 0:NT], ACT.Silu), ("g", i))
            for h in range(RH):
                freed(act, ("mu", h))
                if h:
                    act.wait_ge(sq_summed, h)
                A.activation(sqg[:, :, :], oT[:, 4 * h:4 * h + 4, :], ACT.Square).then_inc(sq_ok, 1)
            filled(act, ("var", 0))
            frees(A.activation(std[0:8, :], bank(("var", 0), 8)[:, 0:NT], ACT.Sqrt, bias=eps_g[0:8]), ("var", 0))
            norm(1)
            for i in range(FT):
                filled(act, ("fg", i))
                if i >= 2:
                    freed(act, ("fu", i - 2))
                frees(A.activation(sg[:, i % 2, :], bank(("fg", i))[:, 0:NT], ACT.Silu), ("fg", i))
            norm(2)
            for h in range(HH):
                filled(act, ("hf", h))
                frees(A.activation(hf[:, h, :], bank(("hf", h))[:, 0:NT], ACT.Sigmoid), ("hf", h))
            act.wait_ge(f_ok, 8)
            A.activation(hf[:, :, 0:NP_], hf[:, :, 0:NP_], ACT.Ln).then_inc(logf_ok, 1)
            for i in range(8):
                filled(act, ("hi", i))
                if i >= 2:
                    filled(act, ("itr", i - 2))
                frees(A.copy(itmp[:, i % 2, :], bank(("hi", i))[:, 0:NT]), ("hi", i))
            for h in range(HH):
                filled(act, ("hq", h))
                frees(A.activation(hq[:, h, :], bank(("hq", h))[:, 0:NT], ACT.Silu), ("hq", h))
            for l in range(9):
                act.wait_ge(lev_sub, l + 1)
                A.activation(lev[l % 2], lev[l % 2], ACT.Exp).then_inc(lev_exp, 1)
                if l:
                    filled(act, ("hg", l - 1))
                    frees(A.copy(hgt[:, l - 1, :], bank(("hg", l - 1))[:, 0:NT]), ("hg", l - 1))
            freed(act, ("hg", 7))
            A.activation(hgt, hgt, ACT.Silu).then_inc(hgate_ok, 1)
            for j in range(4):
                filled(act, ("kt", j))
                frees(A.copy(kd_tok[:, 4 * j:4 * j + 4, :], bank(("kt", j)).rearrange("p (a t) -> p a t", a=4)),
                      ("kt", j))
            for j in range(4):
                filled(act, ("ho", j))
                frees(A.copy(oH[:, 2 * j:2 * j + 2, 0:NP_], bank(("ho", j)).rearrange("p (a t) -> p a t", a=2)),
                      ("ho", j))
            for j in range(2):
                filled(act, ("hs", j))
                frees(A.copy(hs_out[:, 4 * j:4 * j + 4, :], bank(("hs", j)).rearrange("p (a t) -> p a t", a=4)),
                      ("hs", j))
            freed(act, ("hs", 0))
            freed(act, ("hs", 1))
            act.dma_start(hg_pout, hs_out).then_inc(hs_store, 16)
            freed(act, ("hso", 0))
            for j in range(4):
                freed(act, ("ho", j))
            A.activation(hsq, oH[:, :, :], ACT.Square).then_inc(sq_ok, 1)
            filled(act, ("hvar", 0))
            frees(A.activation(std[0:8, :], bank(("hvar", 0), 8)[:, 0:NT], ACT.Sqrt, bias=eps_n[0:8]), ("hvar", 0))
            act.wait_ge(hs_store, 16)
            norm(3)
            act.dma_start(w_rt, ins["moe_router"][0].rearrange("(k p) e -> p k e", p=P)).then_inc(rt_in, 16)
            act.dma_start(gfin, ins["final_norm_g"].partition_broadcast(P)).then_inc(rt_in, 16)
            for j in range(12):
                filled(act, ("tok", j))
                src = bank(("tok", j))
                dst, t, q = (x_tok, j // 2, j % 2) if j < 6 else (h_tok, (j - 6) // 2, j % 2)
                m = P if t < 2 else NS
                if j >= 6 and t == 2:
                    act.wait_ge(pad_ok, 1)
                frees(A.copy(dst[0:m, t, 512 * q:512 * q + 512], src[0:m, :]), ("tok", j))
            act.wait_ge(e_in, 1)
            A.activation(prb, prb, ACT.Exp).then_inc(e_ok, 1)
            act.wait_ge(route_ok, 1)
            rounds = act.value_load(nri[0:1, 0:1], min_val=1, max_val=ROUNDS)
            act.sem_inc(y_free, 1)
            with act.Fori(0, rounds) as r:
                with act.Fori(0, NE) as e:
                    i = r * NE + e
                    for c in range(NCH + 1):
                        if c < NCH:
                            act.wait_ge(piece_used, i * (2 * NCH) + (2 * c + 1))
                            act.wait_ge(hide_ok, i * NCH + (1 + max(c - 1, 0)))
                            A.activation(act_g[:, c % 2, :], ps[:, c % 2, 0:4 * C], ACT.Silu).then_inc(gate_ok, 1)
                        if c:
                            t = epos["d", c - 1]
                            act.wait_ge(moe_arrived[t % RING], i * (16 * (EP // RING)) + 16 * (t // RING + 1))
                            for j in range(4):
                                g = 4 * (c - 1) + j
                                act.wait_ge(w_used, i * (4 * NCH) + (g - WPL + 3 if g >= WPL else 2))
                                A.copy(w_hi[:, g % WPL, :], piece(t % RING)[:, D * j:D * j + D]).then_inc(w_hi_ok, 1)
                        if c < NCH:
                            act.wait_ge(hide_ok, i * NCH + (c + 2))
                            if c == 0:
                                act.wait_ge(w_used, i * (4 * NCH) + 2)
                            A.copy(hide_hi[:, c % 2, :], hide[:, c % 2, :]).then_inc(hide_hi_ok, 1)
                    act.wait_ge(w_used, i * (4 * NCH) + (4 * NCH + 2))
                    A.copy(y_out[0:C, 0:512], ps[0:C, 4, :])
                    A.copy(y_out[0:C, 512:1024], ps[0:C, 5, :]).then_inc(y_free, 1)
                    act.wait_ge(y_free, i + 2)
                    act.dma_start(y_scr[bass.ds(i * C, C), :], y_out[0:C, :]).then_inc(y_store, 16)
                    act.wait_ge(y_store, i * 16 + 16)
            A.copy(frs[:, 0:1], red3[:, 0:1]).then_inc(all_stored, 1)
            for t in range(3):
                m = P if t < 2 else NS
                act.wait_ge(fin_in, t + 1)
                A.activation(ysq[0:m, :], yf[0:m, t, :], ACT.Square, accum_out=fsum[0:m, t:t + 1]).then_inc(fin_sq, 1)
                act.wait_ge(fin_mean, t + 1)
                A.activation(fsum[0:m, t:t + 1], fsum[0:m, t:t + 1], ACT.Sqrt).then_inc(fin_std, 1)
            for t in range(3):
                act.wait_ge(fin_ok, t + 1)
                if t < 2:
                    act.dma_start(outs["y_p"][0, P * t:P * t + P, :], yf[:, t, :]).then_inc(out_done, 16)
                else:
                    act.dma_start(outs["y_s"].rearrange("b s d -> (b s) d"), yf[0:NS, 2, :]).then_inc(out_done, 16)
            act.wait_ge(out_done, 48)
            for s_ in range(2):
                act.wait_ge(s_store[s_], 32)
                act.wait_ge(hu_out[s_], 16 * NS // 2)
            for s_ in range(UNITS):
                act.wait_ge(unit_out[s_], 16 * NS)

        @block.vector
        def _(dve):
            V = nc.vector
            steps = [0]

            def link(i):
                steps[0] += 1
                i.then_inc(dve_step, 1)
                dve.wait_ge(dve_step, steps[0])

            dve.wait_ge(s_c, 16)
            for j in range(4):
                filled(dve, ("xt", j))
                frees(V.tensor_copy(xT[:, 4 * (j % 2):4 * (j % 2) + 4, P * (j // 2):P * (j // 2) + P],
                                    bank(("xt", j)).rearrange("p (a t) -> p a t", a=4)), ("xt", j))
            filled(dve, ("xt", 4))
            frees(V.tensor_copy(xT[:, :, NP_:NT], bank(("xt", 4))[:, 0:64].rearrange("p (a t) -> p a t", a=8)),
                  ("xt", 4))
            filled(dve, ("xt", 5))
            frees(V.tensor_copy(vec[:, :], bank(("xt", 5))[:, 0:NVEC]), ("xt", 5))
            freed(dve, ("xt", 5))
            a0, a1 = vec[:, VEC["lb"]:VEC["lb"] + 8], vec[:, VEC["lb"] + 8:VEC["lb"] + 16]
            link(V.tensor_tensor(lbt[:, 0, :], a0, a1, ALU.max))
            link(V.tensor_tensor(lbt[:, 1, :], a0, lbt[:, 0, :], ALU.subtract))
            V.tensor_tensor(lbt[:, 2, :], a1, lbt[:, 0, :], ALU.subtract).then_inc(lb_in, 1)
            dve.wait_ge(lb_exp, 1)
            link(V.tensor_tensor(lbt[:, 3, :], lbt[:, 1, :], lbt[:, 2, :], ALU.add))
            link(V.reciprocal(lbt[:, 4, :], lbt[:, 3, :]))
            link(V.tensor_tensor(lbt[:, 1, :], lbt[:, 1, :], lbt[:, 4, :], ALU.mult))
            link(V.tensor_tensor(lbt[:, 2, :], lbt[:, 2, :], lbt[:, 4, :], ALU.mult))
            link(V.tensor_tensor(lbt[:, 5, :], lbt[:, 1, :], lbt[:, 2, :], ALU.add))
            link(V.tensor_tensor(lbt[:, 6, :], lbt[:, 5, :], lbt[:, 1, :], ALU.subtract))
            link(V.tensor_scalar(lbt[:, 7, :], lbt[:, 6, :], -1.0, 1.0, ALU.mult, ALU.add))
            lb, oml = lbt[:, 6, :], lbt[:, 7, :]

            def norm(n, gain):
                freed(dve, ("ms", n))
                link(V.reciprocal(rstd[:, :], std[:, :]))
                filled(dve, ("ms", n))
                for k in range(KD):
                    V.scalar_tensor_tensor(out=hT[:, k, :], in0=xT[:, k, :], scalar=vec[:, gain + k:gain + k + 1],
                                           in1=rstd[:, :], op0=ALU.mult, op1=ALU.mult).then_inc(h_ready, 1)

            def residual(kind):
                for i in range(8):
                    filled(dve, (kind, i))
                    frees(V.tensor_tensor(xT[:, i, :], xT[:, i, :], bank((kind, i))[:, 0:NT], ALU.add), (kind, i))
                freed(dve, (kind, 7))

            norm(0, VEC["mix"])
            def rotate(a):
                dst = qT if a < 4 else kT
                t = 2 * (a % 4)
                filled(dve, ("qk", 2 * a))
                filled(dve, ("qk", 2 * a + 1))
                x1, x2 = bank(("qk", 2 * a))[:, 0:NT], bank(("qk", 2 * a + 1))[:, 0:NT]
                if rotated[0]:
                    dve.wait_ge(qk_ready, rotated[0])
                V.tensor_tensor(rot[:, 0, :], x1, cos, ALU.mult)
                V.tensor_tensor(rot[:, 1, :], x2, sin, ALU.mult)
                frees(V.tensor_tensor(rot[:, 2, :], x2, cos, ALU.mult), ("qk", 2 * a + 1))
                frees(V.tensor_tensor(rot[:, 3, :], x1, sin, ALU.mult), ("qk", 2 * a))
                freed(dve, ("qk", 2 * a))
                V.tensor_tensor(dst[:, t, :], rot[:, 0, :], rot[:, 1, :], ALU.subtract)
                V.tensor_tensor(dst[:, t + 1, :], rot[:, 2, :], rot[:, 3, :], ALU.add).then_inc(qk_ready, 1)
                rotated[0] += 1

            def v_rows(i):
                filled(dve, ("vtr", i))
                s = bank(("vtr", i))
                V.tensor_copy(v_tok[:, :, P * i:P * i + P], s[:, 0:256].rearrange("p (a e) -> p a e", a=2))
                frees(V.tensor_copy(v_smp[:, P * i:P * i + P], s[0:NS, 256:384]), ("vtr", i))

            def update(u):
                b, h = unit_of(u)
                j = u % UNITS
                S = unit[:, j, 0:1024]
                dve.wait_ge(unit_s[j], 16 * (u // UNITS + 1))
                link(V.tensor_scalar(S, S, GAMMA[h], None, ALU.mult))
                dve.wait_ge(unit_v[j], 16 * (u // UNITS + 1))
                for k in range(2):
                    i = V.scalar_tensor_tensor(out=S[:, 512 * k:512 * k + 512], in0=unit[:, j, 1024:1536],
                                               scalar=ksmp[:, 2 * h + k, b:b + 1], in1=S[:, 512 * k:512 * k + 512],
                                               op0=ALU.mult, op1=ALU.add)
                i.then_inc(unit_new, 1)

            def sample_o(g):
                filled(dve, ("so", g))
                frees(V.tensor_copy(oT[:, 8 * g:8 * g + 8, NP_:NT],
                                    bank(("so", g))[:, 0:64].rearrange("p (a b) -> p a b", a=8)), ("so", g))

            rotated = [0]
            for g in range(2):
                if g:
                    filled(dve, ("o", 1, 1))
                for n, a in enumerate((2 * g, 2 * g + 1, 4 + 2 * g, 5 + 2 * g)):
                    rotate(a)
                    if g:
                        update(2 * n)
                        update(2 * n + 1)
                dve.wait_ge(qk_ready, 4 * (g + 1))
                link(V.tensor_scalar(ksmp[:, 4 * g:4 * g + 4, :], kT[:, 4 * g:4 * g + 4, NP_:NT], RDK ** -0.5, None,
                                     ALU.mult))
                for n in range(8):
                    v_rows(8 * g + n)
                    if g:
                        update(8 + n)
                if g:
                    sample_o(0)
                for h in (2 * g, 2 * g + 1):
                    filled(dve, ("sc", h))
                    if h:
                        filled(dve, ("o", h - 1, 1))
                    s = bank(("sc", h))
                    V.tensor_tensor(prob[:, 0:256], s[:, 0:256], dmask[:, h, :], ALU.mult)
                    frees(V.tensor_tensor(prob[:, 256:384], s[:, 256:384], dmask[:, h, 0:P], ALU.mult), ("sc", h))
            for u in range(16, 32):
                update(u)
            sample_o(1)
            for h in range(RH):
                filled(dve, ("mu", h))
                o = oT[:, 4 * h:4 * h + 4, :]
                frees(V.tensor_tensor(o, o, bank(("mu", h))[:, 0:NT].unsqueeze(1).to_broadcast([P, 4, NT]),
                                      ALU.subtract), ("mu", h))
            freed(dve, ("var", 0))
            V.reciprocal(rstd[0:8, :], std[0:8, :]).then_inc(r8_ok, 1)
            for h in range(RH):
                filled(dve, ("rs", h))
                if h == 0:
                    freed(dve, ("g", 15))
                for e in range(4):
                    t = 4 * h + e
                    i = V.scalar_tensor_tensor(out=oT[:, t, :], in0=oT[:, t, :],
                                               scalar=vec[:, VEC["gn"] + t:VEC["gn"] + t + 1],
                                               in1=bank(("rs", h))[:, 0:NT], op0=ALU.mult, op1=ALU.mult)
                frees(i, ("rs", h))
                freed(dve, ("rs", h))
                o = oT[:, 4 * h:4 * h + 4, :]
                V.tensor_tensor(o, o, gT[:, 4 * h:4 * h + 4, :], ALU.mult).then_inc(o_ok, 1)
            residual("wo")
            norm(1, VEC["ffn"])
            for i in range(FT):
                filled(dve, ("fu", i))
                freed(dve, ("fg", i))
                frees(V.tensor_tensor(hid[:, i, :], sg[:, i % 2, :], bank(("fu", i))[:, 0:NT], ALU.mult), ("fu", i))
            residual("fd")
            norm(2, VEC["mix"] + 8)
            for h in range(HH):
                freed(dve, ("hf", h))
                link(V.tensor_scalar(hf[:, h, :], hf[:, h, :], oml[:, h:h + 1], lb[:, h:h + 1], ALU.mult, ALU.add))
                V.tensor_scalar(hk[:, h, :], hf[:, h, :], -1.0, 1.0, ALU.mult, ALU.add)
                i = V.tensor_copy(fsmp[:, h, :], hf[:, h, NP_:NT])
                i.then_inc(f_ok, 1)
            dve.wait_ge(logf_ok, 1)
            for h in range(HH):
                i = V.tensor_tensor_scan(bcum[:, h, :], cc("reset"), hf[:, h, 0:NP_], 0.0, ALU.mult, ALU.add)
            link(i)
            bch = bcum.rearrange("p h (c t) -> p h c t", t=CHUNK)
            T = [bch[:, :, c, CHUNK - 1] for c in range(4)]
            V.tensor_copy(tots[:, 2, :], T[3])
            link(V.tensor_tensor(tots[:, 1, :], T[2], T[3], ALU.add))
            link(V.tensor_tensor(tots[:, 0, :], tots[:, 1, :], T[1], ALU.add))

            def reader(l):
                return ("lv", l + 1, 3) if l <= 6 else ("cr", 1)

            def exponents(l):
                if l >= 2:
                    filled(dve, reader(l - 2))
                L = lev[l % 2]
                lc = L.rearrange("p (h c t) -> p h c t", h=8, t=CHUNK)
                tot = lambda a, b: bch[:, :, a:b, CHUNK - 1:CHUNK].to_broadcast([P, 8, b - a, CHUNK])
                if l <= 5:
                    m = 1 << l
                    n = 2048 // (2 * m)
                    bv = bcum.rearrange("p h t -> p (h t)").rearrange("p (n t) -> p n t", t=2 * m)
                    lv = L.rearrange("p (n t) -> p n t", t=2 * m)
                    mid = bv[:, :, m - 1:m].to_broadcast([P, n, m])
                    V.tensor_tensor(lv[:, :, m:], bv[:, :, m:], mid, ALU.subtract)
                    i = V.tensor_tensor(lv[:, :, 0:m], mid, bv[:, :, 0:m], ALU.subtract)
                elif l == 6:
                    for c in (0, 2):
                        V.tensor_tensor(lc[:, :, c:c + 1, :], tot(c, c + 1), bch[:, :, c:c + 1, :], ALU.subtract)
                        i = V.tensor_copy(lc[:, :, c + 1, :], bch[:, :, c + 1, :])
                elif l == 7:
                    link(V.tensor_tensor(lc[:, :, 0:2, :], tot(0, 2), bch[:, :, 0:2, :], ALU.subtract))
                    V.tensor_tensor(lc[:, :, 0, :], lc[:, :, 0, :], tot(1, 2)[:, :, 0, :], ALU.add)
                    V.tensor_copy(lc[:, :, 2, :], bch[:, :, 2, :])
                    i = V.tensor_tensor(lc[:, :, 3, :], bch[:, :, 3, :], tot(2, 3)[:, :, 0, :], ALU.add)
                else:
                    link(V.tensor_tensor(lc, tot(0, 4), bch, ALU.subtract))
                    for c in range(3):
                        i = V.tensor_tensor(lc[:, :, c, :], lc[:, :, c, :],
                                            tots[:, c, :].unsqueeze(2).to_broadcast([P, 8, CHUNK]), ALU.add)
                i.then_inc(lev_sub, 1)

            def operands(l):
                dve.wait_ge(lev_exp, l + 1)
                L = lev[l % 2]
                if l < 8:
                    m = min(1 << l, 128)
                    lv = L.rearrange("p (h n t) -> p h n t", h=8, t=2 * m)
                    kv = hk[:, :, 0:NP_].rearrange("p h (n t) -> p h n t", t=2 * m)
                    qv = hq[:, :, 0:NP_].rearrange("p h (n t) -> p h n t", t=2 * m)
                    V.tensor_tensor(lv[:, :, :, m:], lv[:, :, :, m:], qv[:, :, :, m:], ALU.mult)
                    i = V.tensor_tensor(lv[:, :, :, 0:m], lv[:, :, :, 0:m], kv[:, :, :, 0:m], ALU.mult)
                else:
                    L = L.rearrange("p (h t) -> p h t", h=8)
                    i = V.tensor_tensor(L, L, hk[:, :, 0:NP_], ALU.mult)
                i.then_inc(lev_x, 1)

            def choose(l):
                if l:
                    freed(dve, ("lv", l - 1, 3))
                for j in range(4):
                    filled(dve, ("lv", l, j))
                    src = bank(("lv", l, j)).rearrange("p (a t) -> p a t", a=4)
                    dst = att[:, 2 * j:2 * j + 2, :, :].rearrange("p h a t -> p (h a) t")
                    if l == 0:
                        i = V.tensor_tensor(dst, src, ident.unsqueeze(1).to_broadcast([P, 4, P]), ALU.mult)
                    else:
                        i = V.copy_predicated(dst, lvl[:, l - 1, :].unsqueeze(1).to_broadcast([P, 4, P]), src)
                    frees(i, ("lv", l, j))

            for h in range(UNITS):
                dve.wait_ge(unit_out[h], 16 * NS)
            for j in range(2):
                dve.wait_ge(s_store[j], 32)
            for i in range(8):
                filled(dve, ("itr", i))
                s = bank(("itr", i))
                V.tensor_copy(i_tok[:, :, P * i:P * i + P], s[:, 0:256].rearrange("p (a e) -> p a e", a=2))
                frees(V.tensor_copy(i_smp[:, P * i:P * i + P], s[0:NS, 256:384]), ("itr", i))
            exponents(0)
            choose(0)
            for l in range(9):
                if l < 8:
                    exponents(l + 1)
                operands(l)
                if 1 <= l <= 7:
                    choose(l)
            filled(dve, ("hso", 0))
            frees(V.tensor_copy(oH[:, :, NP_:NT], bank(("hso", 0))[:, 0:64].rearrange("p (h b) -> p h b", h=8)),
                  ("hso", 0))
            dve.wait_ge(i_stored, 16)
            for j in range(2):
                filled(dve, ("cr", j))
                frees(V.tensor_copy(cross[:, 4 * j:4 * j + 4, :], bank(("cr", j)).rearrange("p (a t) -> p a t", a=4)),
                      ("cr", j))
            freed(dve, ("hvar", 0))
            V.reciprocal(rstd[0:8, :], std[0:8, :]).then_inc(r8_ok, 1)
            for h in range(HH):
                filled(dve, ("hrs", h))
                frees(V.scalar_tensor_tensor(out=oH[:, h, :], in0=oH[:, h, :],
                                             scalar=vec[:, VEC["hgn"] + h:VEC["hgn"] + h + 1],
                                             in1=bank(("hrs", h))[:, 0:NT], op0=ALU.mult, op1=ALU.mult), ("hrs", h))
            freed(dve, ("hrs", 7))
            dve.wait_ge(hgate_ok, 1)
            V.tensor_tensor(oH[:, :, :], oH[:, :, :], hgt, ALU.mult).then_inc(o_ok, 1)
            residual("hw")
            norm(3, VEC["ffn"] + 8)
            V.memset(h_tok[:, 2, :], 0.0).then_inc(pad_ok, 1)
            link(V.memset(lg, 0.0))
            filled(dve, ("lg", 0))
            for t in range(3):
                m = P if t < 2 else NS
                i = V.tensor_copy(lg[0:m, t, :], bank(("lg", 0))[0:m, 8 * t:8 * t + 8])
            frees(i, ("lg", 0))
            freed(dve, ("lg", 0))
            link(V.reduce_max(red3, lg, AX.X))
            V.tensor_tensor(prb, lg, red3.unsqueeze(2).to_broadcast([P, 3, 8]), ALU.subtract).then_inc(e_in, 1)
            dve.wait_ge(e_ok, 1)
            link(V.reduce_sum(red3, prb, AX.X))
            link(V.reciprocal(fsum, red3))
            link(V.tensor_tensor(prb, prb, fsum.unsqueeze(2).to_broadcast([P, 3, 8]), ALU.mult))
            for t in range(3):
                link(V.max(m8[:, t, :], prb[:, t, :]))
                i = V.max_index(ix[:, t, :], m8[:, t, :], prb[:, t, :])
            link(i)
            link(V.tensor_copy(ixf, ix))
            valid = cc("valid")
            for t in range(3):
                V.tensor_scalar(oa[:, t, :], cc("exp8"), ixf[:, t, 0:1], valid[:, t:t + 1], ALU.is_equal, ALU.mult)
                i = V.tensor_scalar(ob[:, t, :], cc("exp8"), ixf[:, t, 1:2], valid[:, t:t + 1], ALU.is_equal, ALU.mult)
            link(i)
            V.tensor_tensor(mm_, oa, ob, ALU.add).then_inc(mask_ok, 1)
            link(V.tensor_tensor(wab[:, :, 2], m8[:, :, 0], m8[:, :, 1], ALU.add))
            link(V.reciprocal(wab[:, :, 3], wab[:, :, 2]))
            V.tensor_tensor(wab[:, :, 0], m8[:, :, 0], wab[:, :, 3], ALU.mult)
            V.tensor_tensor(wab[:, :, 1], m8[:, :, 1], wab[:, :, 3], ALU.mult)
            filled(dve, ("rk", 0))
            frees(V.tensor_copy(rk, bank(("rk", 0))[:, 0:32].rearrange("p (a e) -> p a e", a=4)), ("rk", 0))
            freed(dve, ("rk", 0))
            dve.wait_ge(mask_ok, 1)
            link(V.memset(reff, -1.0))
            for r in range(ROUNDS):
                link(V.tensor_scalar(r1, rk[:, 0:3, :], 1.0 - r * C, None, ALU.add))
                link(V.tensor_tensor(r1, r1, mm_, ALU.mult))
                link(V.tensor_scalar(reff[:, :, 8 * r:8 * r + 8], r1, -1.0, None, ALU.add))
            link(V.reduce_max(nrf[:, 0:1], rk[:, 3, :], AX.X))
            link(V.memset(nrf[:, 1:2], 1.0))
            for r in range(1, ROUNDS):
                link(V.tensor_scalar(nrf[:, 2:3], nrf[:, 0:1], float(r * C), None, ALU.is_gt))
                link(V.tensor_tensor(nrf[:, 1:2], nrf[:, 1:2], nrf[:, 2:3], ALU.add))
            link(V.tensor_copy(nri, nrf[:, 1:2]))
            for w, o in enumerate((oa, ob)):
                link(V.tensor_tensor(r1, rk[:, 0:3, :], o, ALU.mult))
                link(V.reduce_sum(va[:, w, :], r1, AX.X))
                link(V.tensor_scalar(rowf[:, w, :], ixf[:, :, w], float(C), None, ALU.mult))
                link(V.tensor_tensor(rowf[:, w, :], rowf[:, w, :], va[:, w, :], ALU.add))
                for r in range(1, ROUNDS):
                    link(V.tensor_scalar(vt[:, w, :], va[:, w, :], float(r * C), float((NE - 1) * C), ALU.is_ge,
                                         ALU.mult))
                    link(V.tensor_tensor(rowf[:, w, :], rowf[:, w, :], vt[:, w, :], ALU.add))
            V.tensor_copy(rowi, rowf).then_inc(route_ok, 1)

            def select(i):
                for t in range(3):
                    s = V.tensor_scalar(gsel[:, t, :], cc("slot"), reff[:, t, bass.ds(i, 1)], None, ALU.is_equal)
                s.then_inc(sel_ok, 1)

            dve.sem_inc(hide_ok, 1)
            select(0)
            dve.wait_ge(route_ok, 1)
            rounds = dve.value_load(nri[0:1, 0:1], min_val=1, max_val=ROUNDS)
            with dve.Fori(0, rounds) as r:
                with dve.Fori(0, NE) as e:
                    i = r * NE + e
                    dve.wait_ge(xg_full, i + 1)
                    for q in range(2):
                        V.tensor_copy(xe[:, 4 * q:4 * q + 4, :],
                                      ps[:, 6 + q, 0:4 * C].rearrange("p (a s) -> p a s", a=4)).then_inc(xe_ok, 1)
                    select(i + 1)

                    def low_parts(c, js):
                        for j in js:
                            dve.wait_ge(w_hi_ok, i * (4 * NCH) + (4 * c + j + 1))
                            V.tensor_tensor(w_lo[:, (4 * c + j) % WPL, :], piece(epos["d", c] % RING)[:, D * j:D * j + D],
                                            w_hi[:, (4 * c + j) % WPL, :].bitcast(F32), ALU.subtract).then_inc(w_lo_ok, 1)

                    for c in range(NCH + 1):
                        if c:
                            low_parts(c - 1, (0, 1))
                        if c < NCH:
                            dve.wait_ge(piece_used, i * (2 * NCH) + (2 * c + 2))
                            dve.wait_ge(gate_ok, i * NCH + (c + 1))
                            V.tensor_tensor(hide[:, c % 2, :], act_g[:, c % 2, :], ps[:, 2 + c % 2, 0:4 * C], ALU.mult)\
                                .then_inc(hide_ok, 1)
                        if c:
                            low_parts(c - 1, (2, 3))
                        if c < NCH:
                            dve.wait_ge(hide_hi_ok, i * NCH + (c + 1))
                            V.tensor_tensor(hide_lo[:, c % 2, :], hide[:, c % 2, :],
                                            hide_hi[:, c % 2, :].bitcast(F32), ALU.subtract).then_inc(hide_lo_ok, 1)
            dve.wait_ge(ya_in, 96)
            for t in range(3):
                m = P if t < 2 else NS
                link(V.scalar_tensor_tensor(out=yf[0:m, t, :], in0=ya[0:m, t, :], scalar=wab[0:m, t, 0:1],
                                            in1=x_tok[0:m, t, :], op0=ALU.mult, op1=ALU.add))
                V.scalar_tensor_tensor(out=yf[0:m, t, :], in0=yb[0:m, t, :], scalar=wab[0:m, t, 1:2],
                                       in1=yf[0:m, t, :], op0=ALU.mult, op1=ALU.add).then_inc(fin_in, 1)
                dve.wait_ge(fin_sq, t + 1)
                V.tensor_scalar(fsum[0:m, t:t + 1], fsum[0:m, t:t + 1], 1.0 / D, NEPS, ALU.mult, ALU.add)\
                    .then_inc(fin_mean, 1)
                dve.wait_ge(fin_std, t + 1)
                link(V.reciprocal(frs[0:m, t:t + 1], fsum[0:m, t:t + 1]))
                V.scalar_tensor_tensor(out=yf[0:m, t, :], in0=yf[0:m, t, :], scalar=frs[0:m, t:t + 1],
                                       in1=gfin[0:m, :], op0=ALU.mult, op1=ALU.mult).then_inc(fin_ok, 1)

        @block.tensor
        def _(pe):
            def claim(name):
                b, k = FILL[name]
                if k:
                    pe.wait_ge(bank_free[b], k)

            def close(ins, name):
                ins.then_inc(bank_full[FILL[name][0]], 1)

            def mm(out, lhsT, rhs, first=True, last=True):
                return nc.tensor.matmul(out, lhsT, rhs, start=first, stop=last)

            pe.wait_ge(s_c, 16)
            pe.wait_ge(s_x, 32)
            for j in range(4):
                claim(("xt", j))
                for a in range(4):
                    k = 4 * (j % 2) + a
                    i = nc.tensor.transpose(bank(("xt", j))[:, P * a:P * a + P], x_in[:, j // 2, P * k:P * k + P], ident)
                close(i, ("xt", j))
            for k in range(KD):
                i = nc.tensor.transpose(bank(("xt", 4))[:, NS * k:NS * k + NS], x_in[0:NS, 2, P * k:P * k + P],
                                        ident[0:NS, 0:NS])
            close(i, ("xt", 4))
            pe.wait_ge(s_v, 80)
            close(nc.tensor.transpose(bank(("xt", 5))[:, 0:NVEC], vrow[0:NVEC, :], ident[0:NVEC, 0:NVEC]), ("xt", 5))

            def mean_square(n):
                claim(("ms", n))
                for k in range(KD):
                    if k % 4 == 0:
                        pe.wait_ge(squares, 2 * n + k // 4 + 1)
                    i = mm(bank(("ms", n))[:, 0:NT], cc("mean_d"), hT[:, k, :], k == 0, k == KD - 1)
                close(i, ("ms", n))

            def arrive(name):
                pe.wait_ge(arrived[where[name]], need[name])

            def project(name, w, n_norm=None):
                claim(name)
                for k in range(KD):
                    if n_norm is not None:
                        pe.wait_ge(h_ready, 8 * n_norm + k + 1)
                    i = mm(bank(name)[:, 0:NT], w[:, k, :], hT[:, k, :], k == 0, k == KD - 1)
                close(i, name)

            def pview(name, k, off=0, n=None):
                w = (n or PIECE // k) * k
                return piece(where[name])[:, off:off + w].rearrange("p (k n) -> p k n", k=k)

            def to_tokens(kind, src, dst):
                freed(pe, src)
                claim(dst)
                o = bank(dst)
                for a in range(2):
                    nc.tensor.transpose(o[:, P * a:P * a + P], kind[:, P * a:P * a + P], ident)
                close(nc.tensor.transpose(o[0:NS, 256:384], kind[:, NP_:NT], ident), dst)

            mean_square(0)
            def attention(h):
                claim(("sc", h))
                s = bank(("sc", h))
                for k in range(2):
                    mm(s[:, 0:256], kT[:, 2 * h + k, 0:P], qT[:, 2 * h + k, 0:256], k == 0, k == 1)
                for k in range(2):
                    i = mm(s[:, 256:384], kT[:, 2 * h + k, P:256], qT[:, 2 * h + k, P:256], k == 0, k == 1)
                close(i, ("sc", h))
                claim(("kdt", h))
                for st in range(2):
                    for k in range(2):
                        i = nc.tensor.transpose(bank(("kdt", h))[:, 256 * st + P * k:256 * st + P * k + P],
                                                kT[:, 2 * h + k, P * st:P * st + P], ident)
                close(i, ("kdt", h))
                freed(pe, ("sc", h))
                for j in range(2):
                    claim(("o", h, j))
                    for e in range(2):
                        a = 512 * h + 256 * j + P * e
                        o = bank(("o", h, j))[:, 256 * e:256 * e + 256]
                        mm(o, v_tok[:, 0, a:a + P], prob[:, 0:256], True, False)
                        i = mm(o[:, P:256], v_tok[:, 1, a:a + P], prob[:, 256:384], False, True)
                    close(i, ("o", h, j))
                freed(pe, ("kdt", h))
                for j in range(2):
                    claim(("st", h, j))
                    for st in range(2):
                        i = mm(bank(("st", h, j)), kdec[:, st, P * j:P * j + P], v_tok[:, st, 512 * h:512 * h + 512],
                               st == 0, st == 1)
                    close(i, ("st", h, j))

            def sample_unit(u):
                b, h = unit_of(u)
                g = u // 16
                pe.wait_ge(unit_new, u + 1)
                for e in range(4):
                    t = 4 * (h - 2 * g) + e
                    for k in range(2):
                        i = mm(bank(("so", g))[:, NS * t + b:NS * t + b + 1],
                               unit[:, u % UNITS, 512 * k + P * e:512 * k + P * e + P],
                               qT[:, 2 * h + k, NP_ + b:NP_ + b + 1], k == 0, k == 1)
                if u % 16 == 15:
                    close(i, ("so", g))
                else:
                    i.then_inc(unit_pe, 1)

            LAG = 3
            for g in range(2):
                if g:
                    claim(("so", 0))
                for n, i in enumerate(QK_TILES[g]):
                    p_ = ("rwi", i // 4)
                    if n % 4 == 0:
                        arrive(p_)
                    project(("qk", i), pview(p_, 8)[:, :, P * (i % 4):P * (i % 4) + P], 0 if i == 0 else None)
                    if g and n >= LAG:
                        sample_unit(n - LAG)
                for n in range(8):
                    i = 8 * g + n
                    p_ = ("rwi", 4 + i // 4)
                    if n % 4 == 0:
                        arrive(p_)
                    project(("v", i), pview(p_, 8)[:, :, P * (i % 4):P * (i % 4) + P])
                    if n:
                        to_tokens(tmpT[:, (i - 1) % 2, :], ("v", i - 1), ("vtr", i - 1))
                    if g:
                        sample_unit(8 + n - LAG)
                to_tokens(tmpT[:, 1, :], ("v", 8 * g + 7), ("vtr", 8 * g + 7))
                if g:
                    for u in range(16 - LAG, 16):
                        sample_unit(u)
                pe.wait_ge(qk_ready, 4 * (g + 1))
                freed(pe, ("vtr", 8 * g + 6))
                freed(pe, ("vtr", 8 * g + 7))
                attention(2 * g)
                attention(2 * g + 1)
            claim(("so", 1))
            for i in range(16):
                p_ = ("rwi", 8 + i // 4)
                if i % 4 == 0:
                    arrive(p_)
                project(("g", i), pview(p_, 8)[:, :, P * (i % 4):P * (i % 4) + P])
                if i >= LAG:
                    sample_unit(16 + i - LAG)
            for u in range(32 - LAG, 32):
                sample_unit(u)
            freed(pe, ("so", 1))
            for h in range(RH):
                freed(pe, ("o", h, 0))
                freed(pe, ("o", h, 1))
                claim(("mu", h))
                for e in range(4):
                    i = mm(bank(("mu", h))[:, 0:NT], cc("mean_gn"), oT[:, 4 * h + e, :], e == 0, e == 3)
                close(i, ("mu", h))
            claim(("var", 0))
            for h in range(RH):
                pe.wait_ge(sq_ok, h + 1)
                for e in range(4):
                    i = mm(bank(("var", 0), 8)[:, 0:NT], col_gn[:, h, :], sqg[:, e, :], h + e == 0, h + e == 6)
                if h < 3:
                    i.then_inc(sq_summed, 1)
            close(i, ("var", 0))
            pe.wait_ge(r8_ok, 1)
            for h in range(RH):
                claim(("rs", h))
                close(mm(bank(("rs", h))[:, 0:NT], rowsel[0:8, h, :], rstd[0:8, :]), ("rs", h))
            for j in range(4):
                p_ = ("rwo", j)
                arrive(p_)
                w = pview(p_, 16)
                for a in range(2):
                    name = ("wo", 2 * j + a)
                    claim(name)
                    for k in range(16):
                        if name[1] == 0 and k % 4 == 0:
                            pe.wait_ge(o_ok, k // 4 + 1)
                        i = mm(bank(name)[:, 0:NT], w[:, k, P * a:P * a + P], oT[:, k, :], k == 0, k == 15)
                    close(i, name)
            mean_square(1)
            for j in range(11):
                p_ = ("fgu", j)
                arrive(p_)
                for a in range(2):
                    project(("fg", 2 * j + a), pview(p_, 8, 0, 256)[:, :, P * a:P * a + P], 1 if j + a == 0 else None)
                    project(("fu", 2 * j + a), pview(p_, 8, 2048, 256)[:, :, P * a:P * a + P])
            for a in range(4):
                claim(("fd", 2 * a))
                claim(("fd", 2 * a + 1))
                for kh in range(2):
                    p_ = ("fd", 2 * a + kh)
                    arrive(p_)
                    w = pview(p_, 11, 0, 256)
                    for q in range(2):
                        name = ("fd", 2 * a + q)
                        for k in range(11):
                            kk = 11 * kh + k
                            if name[1] == 0:
                                freed(pe, ("fu", kk))
                            i = mm(bank(name)[:, 0:NT], w[:, k, P * q:P * q + P], hid[:, kk, :], kk == 0, kk == FT - 1)
                        if kh:
                            close(i, name)
            mean_square(2)
            for a, kind in enumerate(("hf", "hi", "hq")):
                for i in range(8):
                    p_ = ("hwi", 2 * a + i // 4)
                    if i % 4 == 0:
                        arrive(p_)
                    project((kind, i), pview(p_, 8)[:, :, P * (i % 4):P * (i % 4) + P], 2 if a + i == 0 else None)
                    if kind == "hi" and i:
                        to_tokens(itmp[:, (i - 1) % 2, :], ("hi", i - 1), ("itr", i - 1))
                if kind == "hi":
                    to_tokens(itmp[:, 1, :], ("hi", 7), ("itr", 7))
            claim(("hso", 0))
            pe.wait_ge(f_ok, 8)
            freed(pe, ("hq", 7))
            for l in range(8):
                if l:
                    pe.wait_ge(lev_x, l)
                for j in range(4):
                    name = ("lv", l, j)
                    claim(name)
                    for a in range(4):
                        h, t = 2 * j + a // 2, a % 2
                        if l:
                            L = lev[(l - 1) % 2].rearrange("p (h t) -> p h t", h=8)
                            x, y = L[:, h, P * t:P * t + P], L[:, h, P * t:P * t + P]
                        else:
                            x, y = hk[:, h, P * t:P * t + P], hq[:, h, P * t:P * t + P]
                        i = mm(bank(name)[:, P * a:P * a + P], x, y)
                    close(i, name)
                p_ = ("hwi", 6 + l // 4)
                if l % 4 == 0:
                    arrive(p_)
                project(("hg", l), pview(p_, 8)[:, :, P * (l % 4):P * (l % 4) + P])
                pe.wait_ge(hu_new, l + 1)
                for h in range(HH):
                    i = mm(bank(("hso", 0))[:, NS * h + l:NS * h + l + 1], hunit[l % 2][:, 0, P * h:P * h + P],
                           hq[:, h, NP_ + l:NP_ + l + 1])
                if l < NS - 1:
                    i.then_inc(hu_pe, 1)
                else:
                    close(i, ("hso", 0))
            pe.wait_ge(lev_x, 8)
            L = lev[1].rearrange("p (h t) -> p h t", h=8)
            for j in range(2):
                claim(("cr", j))
                for a in range(4):
                    h = 4 * j + a
                    i = mm(bank(("cr", j))[:, P * a:P * a + P], L[:, h, 0:P], L[:, h, P:256])
                close(i, ("cr", j))
            pe.wait_ge(lev_x, 9)
            L = lev[0].rearrange("p (n t) -> p n t", t=P)
            for j in range(4):
                claim(("kt", j))
                for a in range(4):
                    i = nc.tensor.transpose(bank(("kt", j))[:, P * a:P * a + P], L[:, 4 * j + a, :], ident)
                close(i, ("kt", j))
            freed(pe, ("itr", 7))
            freed(pe, ("itr", 6))
            for j in range(2):
                freed(pe, ("kt", 2 * j))
                freed(pe, ("kt", 2 * j + 1))
                claim(("hs", j))
                for a in range(4):
                    h = 4 * j + a
                    for st in range(2):
                        i = mm(bank(("hs", j))[:, P * a:P * a + P], kd_tok[:, 2 * h + st, :],
                               i_tok[:, st, P * h:P * h + P], st == 0, st == 1)
                close(i, ("hs", j))
            freed(pe, ("lv", 7, 3))
            freed(pe, ("cr", 0))
            freed(pe, ("cr", 1))
            for j in range(4):
                claim(("ho", j))
                for a in range(2):
                    h = 2 * j + a
                    o = bank(("ho", j))[:, 256 * a:256 * a + 256]
                    i0, i1 = i_tok[:, 0, P * h:P * h + P], i_tok[:, 1, P * h:P * h + P]
                    mm(o[:, 0:P], i0, att[:, h, 0, :])
                    mm(o[:, P:256], i0, cross[:, h, :], True, False)
                    i = mm(o[:, P:256], i1, att[:, h, 1, :], False, True)
                close(i, ("ho", j))
            pe.wait_ge(sq_ok, RH + 1)
            claim(("hvar", 0))
            for h in range(HH):
                i = mm(bank(("hvar", 0), 8)[:, 0:NT], col_hg[:, h, :], hsq[:, h, :], h == 0, h == 7)
            close(i, ("hvar", 0))
            pe.wait_ge(r8_ok, 2)
            for h in range(HH):
                claim(("hrs", h))
                close(mm(bank(("hrs", h))[:, 0:NT], rowsel[0:8, h, :], rstd[0:8, :]), ("hrs", h))
            pe.wait_ge(o_ok, RH + 1)
            for i_ in range(8):
                p_ = ("hwo", i_ // 4)
                if i_ % 4 == 0:
                    arrive(p_)
                w = pview(p_, 8)
                claim(("hw", i_))
                for k in range(KD):
                    i = mm(bank(("hw", i_))[:, 0:NT], w[:, k, P * (i_ % 4):P * (i_ % 4) + P], oH[:, k, :], k == 0, k == 7)
                close(i, ("hw", i_))
            mean_square(3)
            pe.wait_ge(h_ready, 32)
            for j in range(12):
                src, t, q = (xT, j // 2, j % 2) if j < 6 else (hT, (j - 6) // 2, j % 2)
                m = P if t < 2 else NS
                claim(("tok", j))
                for a in range(4):
                    i = nc.tensor.transpose(bank(("tok", j))[0:m, P * a:P * a + P], src[:, 4 * q + a, P * t:P * t + m],
                                            ident)
                close(i, ("tok", j))
            pe.wait_ge(rt_in, 32)
            claim(("lg", 0))
            for t in range(3):
                m = P if t < 2 else NS
                for k in range(KD):
                    i = mm(bank(("lg", 0))[0:m, 8 * t:8 * t + 8], hT[:, k, P * t:P * t + m], w_rt[:, k, :], k == 0, k == 7)
            close(i, ("lg", 0))
            pe.wait_ge(mask_ok, 1)
            claim(("rk", 0))
            for t in range(4):
                for s in range(min(t + 1, 3)):
                    i = mm(bank(("rk", 0))[:, 8 * t:8 * t + 8], cc("ltri") if s == t else ones, mm_[:, s, :],
                           s == 0, s == min(t, 2))
            close(i, ("rk", 0))
            for j in range(6, 12):
                freed(pe, ("tok", j))
            freed(pe, ("rk", 0))
            pe.wait_ge(route_ok, 1)
            rounds = pe.value_load(nri[0:1, 0:1], min_val=1, max_val=ROUNDS)
            pe.sem_inc(w_used, 2)
            with pe.Fori(0, rounds) as r:
                with pe.Fori(0, NE) as e:
                    n = r * NE + e

                    def expert_arrived(kind, c):
                        t = epos[kind, c]
                        pe.wait_ge(moe_arrived[t % RING], n * (16 * (EP // RING)) + 16 * (t // RING + 1))

                    def up(c):
                        pe.wait_ge(hide_ok, n * NCH + (1 + max(c - 1, 0)))
                        for z, kind in enumerate("gu"):
                            expert_arrived(kind, c)
                            w = piece(epos[kind, c] % RING).rearrange("p (k n) -> p k n", k=8)
                            for j in range(4):
                                for k in range(KD):
                                    i = mm(ps[:, 2 * z + c % 2, C * j:C * j + C], w[:, k, P * j:P * j + P],
                                           xe[:, k, :], k == 0, k == 7)
                            i.then_inc(piece_used, 1)

                    def down(c):
                        pe.wait_ge(hide_lo_ok, n * NCH + (c + 1))
                        if c == 0:
                            pe.wait_ge(y_free, n + 1)
                        for j in range(4):
                            x_hi = hide_hi[:, c % 2, C * j:C * j + C]
                            x_lo = hide_lo[:, c % 2, C * j:C * j + C]
                            pe.wait_ge(w_hi_ok, n * (4 * NCH) + (4 * c + j + 1))
                            for q in range(2):
                                w = w_hi[:, (4 * c + j) % WPL, 512 * q:512 * q + 512]
                                mm(ps[0:C, 4 + q, :], x_hi, w, c + j == 0, False)
                                mm(ps[0:C, 4 + q, :], x_lo, w, False, False)
                            pe.wait_ge(w_lo_ok, n * (4 * NCH) + (4 * c + j + 1))
                            for q in range(2):
                                i = mm(ps[0:C, 4 + q, :], x_hi, w_lo[:, (4 * c + j) % WPL, 512 * q:512 * q + 512],
                                       False, c + j == NCH + 2)
                            i.then_inc(w_used, 1)

                    pe.wait_ge(sel_ok, n + 1)
                    for k in range(KD):
                        for t in range(3):
                            i = mm(ps[:, 6 + k // 4, C * (k % 4):C * (k % 4) + C], h_tok[:, t, P * k:P * k + P],
                                   gsel[:, t, :], t == 0, t == 2)
                    i.then_inc(xg_full, 1)
                    pe.wait_ge(xe_ok, n * 2 + 2)
                    for c in range(NCH + 1):
                        if c < NCH:
                            up(c)
                        if c:
                            down(c - 1)


INPUTS = ["x_prompt", "x_sample", "state_retention", "state_hgrn", "norm_mix_g", "norm_ffn_g", "final_norm_g",
          "ret_w_in", "ret_gn_g", "ret_w_out", "hg_w_in", "hg_lb_param", "hg_norm_g", "hg_w_out", "ffn_w_gate",
          "ffn_w_up", "ffn_w_down", "moe_router", "moe_w_gate", "moe_w_up", "moe_w_down"]
OUTPUTS = [("y_p", (1, NP_, D)), ("y_s", (NS, 1, D)), ("ret_p", (1, 1, RH, RDK, RDV)),
           ("ret_s", (1, NS, RH, RDK, RDV)), ("hg_p", (1, 1, HH, P, P)), ("hg_s", (1, NS, HH, P, P))]


def kernel(**inputs):
    import concourse.bacc as bacc
    from concourse.bass_utils import run_bass_kernel_spmd

    nc = bacc.Bacc("TRN2", target_bir_lowering=False, num_devices=1)
    arrays = {name: np.ascontiguousarray(inputs[name]) for name in INPUTS}
    arrays["consts"] = constants()
    ins = {n: nc.dram_tensor("in_" + n, a.shape, mybir.dt.from_np(a.dtype), kind="ExternalInput").ap()
           for n, a in arrays.items()}
    outs = {n: nc.dram_tensor("out_" + n, s, F32, kind="ExternalOutput").ap() for n, s in OUTPUTS}
    hybrid_step(nc, ins, outs)
    r = run_bass_kernel_spmd(nc, [{"in_" + n: a for n, a in arrays.items()}], core_ids=[0])
    return tuple(r.results[0]["out_" + n] for n, _ in OUTPUTS)
```

```python
from contextlib import ExitStack

import numpy as np

import concourse.bass as bass
from concourse import mybir

ALU = mybir.AluOpType
ACT = mybir.ActivationFunctionType
F32 = mybir.dt.float32
F32R = mybir.dt.float32r
I32 = mybir.dt.int32
U32 = mybir.dt.uint32
AX = mybir.AxisListType

P = 128
D = 1024
KD = D // P
NP_ = 256
NS = 8
NT = NP_ + NS
PAST = 2048
RH, RDK, RDV = 4, 256, 512
HH = 8
FF = 2816
FT = FF // P
NE, FE = 8, 3584
C = 96
ROUNDS = -(-NT // C)
CHUNK = 64
NEPS, GEPS = 1e-6, 1e-5

PIECE = 4096
RING = 7
DRING = 5
EP = 3 * (FE // 512)
FPL = 4
WPL = 3
UNITS = 4

CONST = {}
_at = 0
for _n, _w in (("ident", P), ("mean_d", P), ("eps", 2),
               ("cos", NT), ("sin", NT), ("dmask", RH * 256), ("dout", 2 * RH), ("mean_gn", P), ("ones", P), ("col_gn", 64), ("col_hg", 64), ("rowsel", 8 * P),
               ("ltri", P), ("slot", C), ("exp8", 8), ("valid", 3), ("reset", NP_), ("lvl", 7 * P)):
    CONST[_n] = (_at, _at + _w)
    _at += _w
NCONST = _at
FIRST = CONST["cos"][0]


def constants():
    c = np.zeros((P, NCONST), np.float32)

    def put(name, v):
        a, b = CONST[name]
        c[:v.shape[0], a:b] = v.reshape(v.shape[0], -1)

    f = np.float32
    half = RDK // 2
    inv = np.power(f(10000.0), -np.arange(half, dtype=f) / f(half)).astype(f)
    pos = np.concatenate([np.arange(NP_), PAST + np.zeros(NS)]).astype(f)
    ang = (pos[None, :] * inv[:, None]).astype(f)
    put("cos", np.cos(ang))
    put("sin", np.sin(ang))
    lg = np.log1p(-np.exp2(-5.0 - np.arange(RH)))
    s, t = np.arange(P)[:, None], np.arange(P)[None, :]
    scale = RDK ** -0.5
    dm = np.zeros((P, RH, 2, P))
    for h in range(RH):
        dm[:, h, 0] = np.where(t >= s, np.exp(np.maximum(t - s, 0) * lg[h]), 0.0) * scale
        dm[:, h, 1] = np.exp((t + P - s) * lg[h]) * scale
    put("dmask", dm.astype(f))
    do = np.zeros((P, 2, RH))
    for st in range(2):
        for h in range(RH):
            do[:, st, h] = np.exp((NP_ - 1 - st * P - np.arange(P)) * lg[h]) * scale
    put("dout", do.astype(f))
    put("ident", np.eye(P, dtype=f))
    put("mean_d", np.full((P, P), 1.0 / D, f))
    put("mean_gn", np.full((P, P), 1.0 / RDV, f))
    put("ones", np.ones((P, P), f))
    put("col_gn", np.broadcast_to(np.eye(8) / RDV, (P, 8, 8)).astype(f))
    put("col_hg", np.broadcast_to(np.eye(8) / P, (P, 8, 8)).astype(f))
    put("rowsel", np.broadcast_to(np.eye(8)[:, :, None], (8, 8, P)).astype(f))
    put("ltri", (s < t).astype(f))
    put("slot", np.broadcast_to(np.arange(C), (P, C)).astype(f))
    put("exp8", np.broadcast_to(np.arange(8), (P, 8)).astype(f))
    va = np.ones((P, 3), f)
    va[NS:, 2] = 0
    put("valid", va)
    put("reset", np.broadcast_to((np.arange(NP_) % CHUNK != 0), (P, NP_)).astype(f))
    lv = np.zeros((P, 7, P), f)
    for l in range(7):
        m = 1 << l
        lv[:, l] = (s // (2 * m) == t // (2 * m)) & (s % (2 * m) < m) & (t % (2 * m) >= m)
    put("lvl", lv)
    put("eps", np.broadcast_to(np.array([NEPS, GEPS]), (P, 2)).astype(f))
    return c


GAMMA = [float(np.float32(1.0 - 2.0 ** (-5 - h))) for h in range(RH)]

VEC = {"mix": 0, "ffn": 16, "gn": 32, "hgn": 48, "lb": 56}
NVEC = 72


RWI_ORDER = (0, 2, 4, 5, 1, 3, 6, 7, 8, 9, 10, 11)
QK_TILES = [[2 * h, 2 * h + 1, 8 + 2 * h, 9 + 2 * h] for h in range(RH)]
UNIT_START, UNIT_LAG = 9, 2


def units_after(tile):
    return [u for u in range(NS * RH) if UNIT_START + u * 11 // 10 == tile]


def fills():
    order = []
    add = order.append
    for j in range(4):
        add((("xt", j), 4 + j))
    add((("xt", 4), 0))
    add((("xt", 5), 1))
    add((("ms", 0), 7))
    n = 0

    def tile(kind, i):
        nonlocal n
        add(((kind, i), n % 4))
        n += 1

    m = 0

    def ret_tile(kind, i):
        nonlocal m
        add(((kind, i), m % 3))
        m += 1

    for h in range(RH):
        if h == 1:
            add((("so", 0), 3))
        for i in QK_TILES[h]:
            ret_tile("qk", i)
        for i in range(4 * h, 4 * h + 4):
            ret_tile("v", i)
            if i % 4:
                add((("vtr", i - 1), 4 + (i - 1) % 2))
        add((("vtr", 4 * h + 3), 5))
        add((("sc", h), 6))
        add((("kdt", h), 7))
        add((("o", h, 0), 4))
        add((("o", h, 1), 5))
        add((("st", h, 0), 6))
        add((("st", h, 1), 7))
    for i in range(16):
        ret_tile("g", i)
    for h in range(RH):
        add((("mu", h), (4, 5, 7, 6)[h]))
    add((("var", 0), 4))
    for h in range(RH):
        add((("rs", h), (5, 6, 7, 5)[h]))
    for i in range(8):
        tile("wo", i)
    add((("ms", 1), 7))
    for i in range(FT):
        tile("fg", i)
        tile("fu", i)
    for i in range(8):
        tile("fd", i)
    add((("ms", 2), 7))
    for i in range(8):
        tile("hf", i)
    for i in range(8):
        tile("hi", i)
        if i:
            add((("itr", i - 1), 4 + (i - 1) % 2))
    add((("itr", 7), 5))
    for i in range(8):
        tile("hq", i)
    add((("hso", 0), 3))
    for lv in range(8):
        for j in range(4):
            add((("lv", lv, j), 4 + j))
        add((("hg", lv), lv % 3))
    for j in range(2):
        add((("cr", j), 4 + j))
    for j in range(4):
        add((("kt", j), (6, 7, 0, 1)[j]))
    for j in range(2):
        add((("hs", j), (2, 0)[j]))
    for j in range(4):
        add((("ho", j), 4 + j))
    add((("hvar", 0), 1))
    for h in range(HH):
        add((("hrs", h), 2 + h % 4))
    assert n % 4 == 0
    for i in range(8):
        tile("hw", i)
    add((("ms", 3), 7))
    for j in range(12):
        add((("tok", j), j % 6))
    add((("lg", 0), 6))
    add((("rk", 0), 7))
    count = [0] * 8
    out = {}
    for name, b in order:
        assert name not in out
        out[name] = (b, count[b])
        count[b] += 1
    return out, count


def hybrid_step(nc, ins, outs):
    FILL, BANKS = fills()
    with ExitStack() as ctx:
        def sb(name, shape, dt=F32, scope=ctx):
            return scope.enter_context(nc.sbuf_tensor(name, shape, dt))

        def sem(name):
            return ctx.enter_context(nc.semaphore(name))

        cst = sb("cst", [P, NCONST])
        vec = sb("vec", [P, NVEC])
        lbt = sb("lbt", [P, 8, 8])
        small = sb("small", [P, 320])
        with ExitStack() as mixers:
            ring = sb("ring", [P, RING * PIECE], scope=mixers)
            x_mem = sb("xT", [P, KD * NT], scope=mixers)
            arena = sb("arena", [P, 14256], scope=mixers)
            h_mem = sb("hT", [P, KD * NT], scope=mixers)
            std = sb("std", [P, NT], scope=mixers)
            rstd = sb("rstd", [P, NT], scope=mixers)
        with ExitStack() as swiglu:
            sb("ring_in_swiglu", [P, DRING * PIECE], scope=swiglu)
            fw_parts = sb("swiglu_weight_parts", [P, 2 * FPL * D], F32R, scope=swiglu)
            sb("xT_in_swiglu", [P, KD * NT], scope=swiglu)
            hid_parts = sb("hidden_parts", [P, 2 * FT * NT], F32R, scope=swiglu)
            h_parts = sb("h_parts", [P, 2 * KD * NT], F32R, scope=swiglu)
            f_tmp = sb("swiglu_products", [P, 4 * NT], scope=swiglu)
        sb("ring_in_experts", [P, RING * PIECE])
        w_parts = sb("down_weight_parts", [P, 2 * WPL * D], F32R)
        hide_parts = sb("hide_parts", [P, 2 * 2 * 4 * C], F32R)
        earena = sb("expert_arena", [P, 11304])
        ps = ctx.enter_context(nc.psum_tensor("ps", [P, 8, 512], F32))

        def piece(s):
            return ring[:, s * PIECE:(s + 1) * PIECE]

        def cc(name):
            a, b = CONST[name]
            return cst[:, a:b]

        ident, ones = cc("ident"), cc("ones")
        cos, sin = cc("cos"), cc("sin")
        dmask = cc("dmask").rearrange("p (h t) -> p h t", h=RH)
        dout = cc("dout").rearrange("p (s h) -> p s h", s=2)
        col_gn = cc("col_gn").rearrange("p (h m) -> p h m", h=8)
        col_hg = cc("col_hg").rearrange("p (h m) -> p h m", h=8)
        rowsel = cc("rowsel").rearrange("p (h m) -> p h m", h=8)
        lvl = cc("lvl").bitcast(I32).rearrange("p (l m) -> p l m", l=7)
        eps_n, eps_g = cc("eps")[:, 0:1], cc("eps")[:, 1:2]

        def part(tensor, a, *shape):
            n = int(np.prod(shape))
            v = tensor[:, a:a + n]
            if len(shape) == 2:
                return v.rearrange("p (a b) -> p a b", a=shape[0])
            if len(shape) == 3:
                return v.rearrange("p (a b c) -> p a b c", a=shape[0], b=shape[1])
            return v

        xT = part(x_mem, 0, KD, NT)
        hT = part(h_mem, 0, KD, NT)
        scratch = DRING * PIECE
        x_in = part(arena, 0, 3, D)
        vrow = part(arena, 3 * D, P)
        qT = part(arena, 0, 8, NT)
        kT = part(arena, 2112, 8, NT)
        v_tok = part(arena, 4224, 2, 2048)
        gT = part(arena, 4224, 16, NT)
        oT = part(arena, 8448, 16, NT)
        v_smp = [[(arena[0:NS, 8448 + 12 * NT:8448 + 12 * NT + RDV], 0)],
                 [(std[0:NS, 0:256], 0), (rstd[0:NS, 0:256], 256)]]
        rot = part(arena, 12672, 4, NT)
        prob = part(arena, 12672, 384)
        sqg = part(arena, 12672, 4, NT)
        tmpT = part(arena, 13728, 2, NT)
        kdec = part(arena, 13728, 2, 256)
        unit = part(ring, scratch, UNITS, 1536)
        s_out = part(ring, scratch + UNITS * 1536, 2, 1024)
        ksmp = part(small, 0, 8, 8)
        h_full = part(arena, 0, KD, NT)
        h_hi = part(h_parts, 0, KD, NT)
        h_lo = part(h_parts, KD * NT, KD, NT)
        hid_hi = part(hid_parts, 0, FT, NT)
        hid_lo = part(hid_parts, FT * NT, FT, NT)
        sg = part(f_tmp, 0, 2, NT)
        hid = part(f_tmp, 2 * NT, 2, NT)
        fw_hi = part(fw_parts, 0, FPL, D)
        fw_lo = part(fw_parts, FPL * D, FPL, D)
        hq = part(arena, 0, 8, NT)
        hf = part(arena, 2112, 8, NT)
        att = part(arena, 2112, 8, 2, P)
        hsq = part(arena, 2112, 8, NT)
        hk = part(arena, 4224, 8, NT)
        hgt = part(arena, 6336, 8, NT)
        bcum = part(arena, 8448, 8, NP_)
        kd_tok = part(arena, 8448, 16, P)
        i_tok = part(arena, 10496, 2, D)
        cross = part(arena, 12544, 8, P)
        i_smp = arena[0:NS, 12544:12544 + D]
        itmp = part(arena, 13568, 2, NT)
        lev = [part(ring, scratch + 2048 * j, 2048) for j in range(2)]
        hunit = [part(ring, scratch + 4096 + 2048 * j, 2, D) for j in range(2)]
        hs_out = part(ring, scratch, 8, P)
        oH = hT
        fsmp = part(small, 64, 8, 8)
        tots = part(small, 128, 4, 8)
        x_tok = part(earena, 0, 3, D)
        h_tok = part(earena, 3072, 3, D)
        gfin = part(earena, 6144, D)
        gsel = part(earena, 7168, 3, C)
        xe = part(earena, 7456, 8, C)
        act_g = part(earena, 8224, 2, 4 * C)
        hide = part(earena, 8992, 2, 4 * C)
        y_out = part(earena, 9760, D)
        hide_hi = part(hide_parts, 0, 2, 4 * C)
        hide_lo = part(hide_parts, 8 * C, 2, 4 * C)
        w_hi = part(w_parts, 0, WPL, D)
        w_lo = part(w_parts, WPL * D, WPL, D)
        RB = 10800
        w_rt = part(earena, RB, 8, 8)
        lg = part(earena, RB + 64, 3, 8)
        prb = part(earena, RB + 88, 3, 8)
        m8 = part(earena, RB + 112, 3, 8)
        ix = earena[:, RB + 136:RB + 160].bitcast(U32).rearrange("p (a b) -> p a b", a=3)
        ixf = part(earena, RB + 160, 3, 8)
        oa = part(earena, RB + 184, 3, 8)
        ob = part(earena, RB + 208, 3, 8)
        mm_ = part(earena, RB + 232, 3, 8)
        rk = part(earena, RB + 256, 4, 8)
        r1 = part(earena, RB + 288, 3, 8)
        reff = part(earena, RB + 312, 3, ROUNDS * 8 + 8)
        wab = part(earena, RB + 440, 3, 4)
        va = part(earena, RB + 452, 2, 3)
        vt = part(earena, RB + 458, 2, 3)
        rowf = part(earena, RB + 464, 2, 3)
        rowi = earena[:, RB + 470:RB + 476].bitcast(U32).rearrange("p (a b) -> p a b", a=2)
        nrf = part(earena, RB + 476, 4)
        nri = earena[:, RB + 480:RB + 481].bitcast(I32)
        red3 = part(earena, RB + 484, 3)
        fsum = part(earena, RB + 488, 3)
        frs = part(earena, RB + 492, 3)
        ya = part(ring, 0, 3, D)
        yb = part(ring, 3072, 3, D)
        yf = part(ring, 6144, 3, D)
        ysq = part(ring, 9216, D)

        v_scr = nc.dram_tensor("v_scr", (NS, 2048), F32)
        i_scr = nc.dram_tensor("i_scr", (NS, D), F32)
        y_scr = nc.dram_tensor("y_scr", (ROUNDS * NE * C, D), F32)

        s_x = sem("tokens_loaded")
        s_c = sem("constants_loaded")
        s_c2 = sem("further_constants_loaded")
        s_v = sem("vectors_loaded")
        bank_full = [sem(f"bank_full{b}") for b in range(8)]
        bank_free = [sem(f"bank_free{b}") for b in range(8)]
        arrived = [sem(f"piece_arrived{s}") for s in range(DRING)]
        moe_arrived = [sem(f"expert_piece_arrived{s}") for s in range(RING)]
        piece_used = sem("piece_used")
        lb_in = sem("bound_shifted")
        lb_exp = sem("bound_exponentials")
        squares = sem("squares")
        h_ready = sem("h_ready")
        dve_step = sem("dve_step")
        act_step = sem("act_step")
        pool_step = sem("pool_step")
        hgate_ok = sem("hgrn_gate_ready")
        qk_ready = sem("qk_rotated")
        h_full_ok = sem("h_before_split")
        h_hi_ok = sem("h_high")
        hid_hi_ok = sem("hidden_high")
        hid_ok = sem("hidden_low")
        fw_hi_ok = sem("swiglu_weights_high")
        fw_lo_ok = sem("swiglu_weights_low")
        fw_used = sem("swiglu_weights_used")
        sq_summed = sem("squares_summed")
        pad_ok = sem("pad_rows_cleared")
        e_in = sem("softmax_shifted")
        fin_in = sem("combined")
        v_stored = sem("v_stored")
        s_store = [sem(f"ret_state_stored{j}") for j in range(2)]
        unit_s = [sem(f"unit_state_in{j}") for j in range(UNITS)]
        unit_v = [sem(f"unit_v_in{j}") for j in range(UNITS)]
        unit_new = sem("unit_updated")
        unit_pe = sem("unit_multiplied")
        unit_out = [sem(f"unit_stored{j}") for j in range(UNITS)]
        sq_ok = sem("o_squares")
        r8_ok = sem("row_rstd_ready")
        o_ok = sem("o_ready")
        f_ok = sem("forget_ready")
        logf_ok = sem("logf_ready")
        i_stored = sem("i_stored")
        lev_sub = sem("level_exponents")
        lev_exp = sem("level_exp")
        lev_x = sem("level_operands")
        hs_store = sem("hgrn_state_stored")
        hu_in = [sem(f"hunit_state_in{j}") for j in range(2)]
        hu_i = [sem(f"hunit_i_in{j}") for j in range(2)]
        hu_new = sem("hunit_updated")
        hu_pe = sem("hunit_multiplied")
        hu_out = [sem(f"hunit_stored{j}") for j in range(2)]
        rt_in = sem("router_loaded")
        e_ok = sem("softmax_exp")
        mask_ok = sem("choice_ready")
        route_ok = sem("rounds_ready")
        rows_ok = sem("output_rows_ready")
        sel_ok = sem("selection_ready")
        xg_full = sem("gathered")
        xe_ok = sem("expert_x_ready")
        gate_ok = sem("expert_silu_ready")
        hide_ok = sem("expert_hidden_ready")
        hide_hi_ok = sem("expert_hidden_high")
        hide_lo_ok = sem("expert_hidden_low")
        w_hi_ok = sem("down_weights_high")
        w_lo_ok = sem("down_weights_low")
        w_used = sem("down_weights_used")
        y_free = sem("expert_y_copied")
        y_store = sem("expert_y_stored")
        zero_ok = sem("zeros_ready")
        zero_stored = sem("zeros_stored")
        all_stored = sem("all_y_stored")
        ya_in = [sem(f"rows_gathered{t}") for t in range(3)]
        fin_sq = sem("final_squares")
        fin_std = sem("final_std")
        fin_ok = sem("final_ready")
        out_done = sem("outputs_stored")

        def bank(name, parts=P):
            return ps[0:parts, FILL[name][0], :]

        def filled(eng, name):
            b, k = FILL[name]
            eng.wait_ge(bank_full[b], k + 1)

        def frees(ins, name):
            ins.then_inc(bank_free[FILL[name][0]], 1)

        def freed(eng, name):
            b, k = FILL[name]
            eng.wait_ge(bank_free[b], k + 1)

        rwi = ins["ret_w_in"][0].rearrange("(k p) n -> p k n", p=P)
        rwo = ins["ret_w_out"][0].rearrange("(k p) n -> p k n", p=P)
        fwg = ins["ffn_w_gate"][0].rearrange("(k p) n -> p k n", p=P)
        fwu = ins["ffn_w_up"][0].rearrange("(k p) n -> p k n", p=P)
        fwd = ins["ffn_w_down"][0].rearrange("(k p) n -> p k n", p=P)
        hwi = ins["hg_w_in"][0].rearrange("(k p) n -> p k n", p=P)
        hwo = ins["hg_w_out"][0].rearrange("(k p) n -> p k n", p=P)
        dense = []
        for j in RWI_ORDER:
            dense.append((("rwi", j), [(rwi[:, :, 512 * j:512 * j + 512], 8, 512, 0)]))
        for j in range(4):
            dense.append((("rwo", j), [(rwo[:, :, 256 * j:256 * j + 256], 16, 256, 0)]))
        for j in range(11):
            dense.append((("fgu", j), [(fwg[:, :, 256 * j:256 * j + 256], 8, 256, 0),
                                       (fwu[:, :, 256 * j:256 * j + 256], 8, 256, 2048)]))
        for j in range(8):
            a, kh = j // 2, j % 2
            dense.append((("fd", j), [(fwd[:, 11 * kh:11 * kh + 11, 256 * a:256 * a + 256], 11, 256, 0)]))
        HG_ORDER = (1, 2, 0, 3)
        for a, part_ in enumerate(HG_ORDER):
            for j in range(2):
                o = 1024 * part_ + 512 * j
                dense.append((("hwi", 2 * a + j), [(hwi[:, :, o:o + 512], 8, 512, 0)]))
        for j in range(2):
            dense.append((("hwo", j), [(hwo[:, :, 512 * j:512 * j + 512], 8, 512, 0)]))
        NDENSE = len(dense)
        assert NDENSE % DRING == 0
        last_tile = {}
        last_tile.update({("rwi", j): (("qk", 4 * j + 3) if j < 4 else ("v", 4 * j - 13) if j < 8 else ("g", 4 * j - 29))
                          for j in range(12)})
        last_tile.update({("rwo", j): ("wo", 2 * j + 1) for j in range(4)})
        last_tile.update({("fgu", j): ("fu", 2 * j + 1) for j in range(11)})
        last_tile.update({("fd", j): ("fd", 2 * (j // 2) + 1) for j in range(8)})
        last_tile.update({("hwi", j): (("hf", "hi", "hq", "hg")[j // 2], 4 * (j % 2) + 3) for j in range(8)})
        last_tile.update({("hwo", j): ("hw", 4 * j + 3) for j in range(2)})
        where, need, got = {}, {}, [0] * DRING
        for n, (name, loads) in enumerate(dense):
            got[n % DRING] += 16 * len(loads)
            where[name] = n % DRING
            need[name] = got[n % DRING]
        blocks = []
        for i in range(FT):
            blocks.append((("fg", i), ("fgu", i // 2), 0, 8, P * (i % 2), 0, 8, 0))
            blocks.append((("fu", i), ("fgu", i // 2), 2048, 8, P * (i % 2), 0, 8, 0))
        for a in range(4):
            for kh in range(2):
                for q in range(2):
                    for k0, k1 in ((0, 6), (6, 11)):
                        blocks.append((("fd", 2 * a + q), ("fd", 2 * a + kh), 0, 11, P * q, k0, k1, 11 * kh))
        NB = len(blocks)

        def block_raw(n):
            _, p_, off, nk, col, k0, k1, _ = blocks[n]
            v = piece(where[p_])[:, off:off + nk * 256].rearrange("p (k n) -> p k n", k=nk)
            return v[:, k0:k1, col:col + P]

        def block_part(tensor, n):
            _, _, _, _, _, k0, k1, _ = blocks[n]
            return tensor[:, n % FPL, 0:P * (k1 - k0)].rearrange("p (k n) -> p k n", k=k1 - k0)

        def block_closes(n):
            kind, _ = blocks[n][0]
            return kind != "fd" or blocks[n][6] + blocks[n][7] == FT

        moe_g = ins["moe_w_gate"][0].rearrange("e (k p) n -> p e k n", p=P)
        moe_u = ins["moe_w_up"][0].rearrange("e (k p) n -> p e k n", p=P)
        moe_d = ins["moe_w_down"][0].rearrange("e (k p) n -> p e k n", p=P)
        NCH = FE // 512
        epieces = []
        for c in range(NCH + 1):
            if c < NCH:
                epieces += [("g", c), ("u", c)]
            if c:
                epieces.append(("d", c - 1))
        assert len(epieces) == EP and EP % RING == 0
        epos = {name: t for t, name in enumerate(epieces)}

        def moe_source(e, kind, c):
            if kind == "d":
                return moe_d[:, bass.ds(e, 1), 4 * c:4 * c + 4, :]
            w = moe_g if kind == "g" else moe_u
            return w[:, bass.ds(e, 1), :, 512 * c:512 * c + 512]

        def moe_dest(kind, t):
            v = piece(t % RING)
            if kind == "d":
                return v.rearrange("p (e k n) -> p e k n", e=1, k=4)
            return v.rearrange("p (e k n) -> p e k n", e=1, k=8)

        ret_in = ins["state_retention"][0].rearrange("b h (k p) e -> b h p k e", p=P)
        ret_out = outs["ret_s"][0].rearrange("b h (k p) e -> b h p k e", p=P)
        ret_pout = outs["ret_p"][0, 0].rearrange("h (k p) e -> h p k e", p=P)
        hg_in = ins["state_hgrn"][0].rearrange("b h d e -> b d h e")
        hg_out = outs["hg_s"][0].rearrange("b h d e -> b d h e")
        hg_pout = outs["hg_p"][0, 0].rearrange("h d e -> d h e")

        block = ctx.enter_context(nc.Block())

        V_STORES = (16, 48, 64, 96)

        def unit_of(u):
            return u % NS, u // NS

        @block.sync
        def _(sp):
            sp.wait_ge(s_x, 32)
            sp.wait_ge(s_c, 16)
            for n, (name, loads) in enumerate(dense):
                if n >= DRING:
                    filled(sp, last_tile[dense[n - DRING][0]])
                for src, k, w, off in loads:
                    dst = piece(n % DRING)[:, off:off + k * w].rearrange("p (k n) -> p k n", k=k)
                    sp.dma_start(dst, src).then_inc(arrived[n % DRING], 16)
                if n == 0:
                    sp.dma_start(cst[:, FIRST:], ins["consts"][:, FIRST:]).then_inc(s_c2, 16)

            def reused(e, t):
                prev = t - RING
                if prev < 0:
                    e, prev = e - 1, prev + EP
                kind, c = epieces[prev]
                if kind == "d":
                    sp.wait_ge(w_lo_ok, e * (4 * NCH) + 4 * (c + 1))
                else:
                    sp.wait_ge(piece_used, e * (2 * NCH) + (2 * c + (kind == "u") + 1))

            for t, (kind, c) in enumerate(epieces):
                if t < DRING:
                    filled(sp, last_tile[dense[NDENSE - DRING + t][0]])
                elif t < RING:
                    filled(sp, ("hrs", 7))
                    sp.wait_ge(hs_store, 16)
                    freed(sp, ("kt", 3))
                    for j in range(2):
                        sp.wait_ge(hu_out[j], 16 * (NS // 2))
                else:
                    reused(0, t)
                sp.dma_start(moe_dest(kind, t), moe_source(0, kind, c)).then_inc(moe_arrived[t % RING], 16)

            def expert(e, i):
                for t, (kind, c) in enumerate(epieces):
                    reused(i, t)
                    sp.dma_start(moe_dest(kind, t), moe_source(e, kind, c)).then_inc(moe_arrived[t % RING], 16)

            with sp.Fori(1, NE) as e:
                expert(e, e)
            sp.wait_ge(route_ok, 1)
            rounds = sp.value_load(nri[0:1, 0:1], min_val=1, max_val=ROUNDS)
            with sp.If(rounds > 1):
                with sp.Fori(1, rounds) as r:
                    with sp.Fori(0, NE) as e:
                        expert(e, r * NE + e)

        @block.gpsimd
        def _(pool):
            def load_state(u):
                b, h = unit_of(u)
                j = u % UNITS
                if u >= UNITS:
                    w = u - UNITS
                    pool.wait_ge(unit_pe, w + 1)
                    pool.wait_ge(unit_out[j], 16 * (u // UNITS))
                pool.dma_start(unit[:, j, 0:1024].rearrange("p (k e) -> p k e", k=2), ret_in[b, h])\
                    .then_inc(unit_s[j], 16)

            for u in range(UNITS):
                load_state(u)
            for u in range(NS * RH + 2):
                if u < NS * RH:
                    b, h = unit_of(u)
                    j = u % UNITS
                    if u >= UNITS:
                        load_state(u)
                    if b == 0:
                        freed(pool, ("vtr", 4 * h + 2))
                        freed(pool, ("vtr", 4 * h + 3))
                        for rows, o in v_smp[h % 2]:
                            w = rows.shape[-1]
                            pool.dma_start(v_scr[:, RDV * h + o:RDV * h + o + w], rows).then_inc(v_stored, 16)
                        pool.wait_ge(v_stored, V_STORES[h])
                    pool.dma_start(unit[:, j, 1024:1536], v_scr[b, 512 * h:512 * h + 512].partition_broadcast(P))\
                        .then_inc(unit_v[j], 16)
                if u >= 2:
                    w = u - 2
                    b, h = unit_of(w)
                    pool.wait_ge(unit_new, w + 1)
                    pool.dma_start(ret_out[b, h], unit[:, w % UNITS, 0:1024].rearrange("p (k e) -> p k e", k=2))\
                        .then_inc(unit_out[w % UNITS], 16)

            filled(pool, ("so", 0))
            for h in range(UNITS):
                pool.wait_ge(unit_out[h], 16 * NS)
            pool.wait_ge(s_store[0], 32)
            pool.wait_ge(s_store[1], 32)
            filled(pool, ("fd", 7))
            nc.gpsimd.memset(hunit[1][:, 1, :], 0.0).then_inc(zero_ok, 1)
            pool.wait_ge(zero_ok, 1)
            nz = (ROUNDS - 1) * NE * C // P
            pool.dma_start(y_scr[NE * C:, :].rearrange("(t p) d -> p t d", p=P),
                           hunit[1][:, 1:2, :].to_broadcast([P, nz, D])).then_inc(zero_stored, 16)

            def load_h(b):
                if b >= 2:
                    pool.wait_ge(hu_pe, b - 1)
                    pool.wait_ge(hu_out[b % 2], 16 * (b // 2))
                pool.dma_start(hunit[b % 2][:, 0, :].rearrange("p (h e) -> p h e", h=8), hg_in[b])\
                    .then_inc(hu_in[b % 2], 16)

            load_h(0)
            load_h(1)
            freed(pool, ("itr", 6))
            freed(pool, ("itr", 7))
            pool.dma_start(i_scr[:, :], i_smp).then_inc(i_stored, 16)
            pool.wait_ge(i_stored, 16)
            pool.wait_ge(f_ok, 8)
            steps = [0]

            def link(i):
                steps[0] += 1
                i.then_inc(pool_step, 1)
                pool.wait_ge(pool_step, steps[0])

            def load_i(b):
                pool.dma_start(hunit[b % 2][:, 1, :], i_scr[b, :].partition_broadcast(P)).then_inc(hu_i[b % 2], 16)

            load_i(0)
            pool.wait_ge(zero_stored, 16)
            load_i(1)
            G = nc.gpsimd
            for b in range(NS):
                S = hunit[b % 2][:, 0, :].rearrange("p (h e) -> p h e", h=8)
                I = hunit[b % 2][:, 1, :].rearrange("p (h e) -> p h e", h=8)
                pool.wait_ge(hu_in[b % 2], 16 * (b // 2 + 1))
                G.tensor_tensor(S, S, fsmp[:, :, b:b + 1].to_broadcast([P, 8, P]), ALU.mult)
                pool.wait_ge(hu_i[b % 2], 16 * (b // 2 + 1))
                link(G.tensor_tensor(I, I, hk[:, :, NP_ + b:NP_ + b + 1].to_broadcast([P, 8, P]), ALU.mult))
                if 1 <= b < NS - 1:
                    load_h(b + 1)
                G.tensor_tensor(S, S, I, ALU.add).then_inc(hu_new, 1)
                pool.wait_ge(hu_new, b + 1)
                pool.dma_start(hg_out[b], hunit[b % 2][:, 0, :].rearrange("p (h e) -> p h e", h=8))\
                    .then_inc(hu_out[b % 2], 16)
                if b + 2 < NS:
                    load_i(b + 2)

            pool.wait_ge(all_stored, 1)
            pool.wait_ge(rows_ok, 1)
            for t in range(3):
                m = P if t < 2 else NS
                for w, dst in enumerate((ya, yb)):
                    pool.indirect_dma_start(dst[0:m, t, :], None, y_scr[:, :],
                                            bass.IndirectOffsetOnAxis(ap=rowi[0:m, w, t:t + 1], axis=0))\
                        .then_inc(ya_in[t], 16)

        @block.scalar
        def _(act):
            A = nc.scalar
            steps = [0]

            def link(i):
                steps[0] += 1
                i.then_inc(act_step, 1)
                act.wait_ge(act_step, steps[0])

            act.dma_start(x_in[:, 0:2, :], ins["x_prompt"][0].rearrange("(t p) d -> p t d", p=P)).then_inc(s_x, 16)
            act.dma_start(x_in[0:NS, 2, :], ins["x_sample"].rearrange("b s d -> (b s) d")).then_inc(s_x, 16)
            act.dma_start(cst[:, 0:FIRST], ins["consts"][:, 0:FIRST]).then_inc(s_c, 16)
            for src, r, n in ((ins["norm_mix_g"].rearrange("l (k p) -> (l k) p", p=P), VEC["mix"], 16),
                              (ins["norm_ffn_g"].rearrange("l (k p) -> (l k) p", p=P), VEC["ffn"], 16),
                              (ins["ret_gn_g"].rearrange("l (k p) -> (l k) p", p=P), VEC["gn"], 16),
                              (ins["hg_norm_g"].rearrange("l (k p) -> (l k) p", p=P), VEC["hgn"], 8),
                              (ins["hg_lb_param"].rearrange("l (k p) -> (l k) p", p=P), VEC["lb"], 16)):
                act.dma_start(vrow[r:r + n, :], src).then_inc(s_v, 16)

            def norm(n):
                for hf_ in range(2):
                    if n:
                        freed(act, (("wo", "fd", "hw")[n - 1], 4 * hf_ + 3))
                        filled(act, (("wo", "fd", "hw")[n - 1], 7))
                    else:
                        for j in range(5):
                            freed(act, ("xt", j))
                    A.activation(hT[:, 4 * hf_:4 * hf_ + 4, :], xT[:, 4 * hf_:4 * hf_ + 4, :], ACT.Square)\
                        .then_inc(squares, 1)
                filled(act, ("ms", n))
                frees(A.activation(std[:, :], bank(("ms", n))[:, 0:NT], ACT.Sqrt, bias=eps_n), ("ms", n))

            act.wait_ge(s_c, 16)
            act.wait_ge(lb_in, 1)
            A.activation(lbt[:, 1:3, :], lbt[:, 1:3, :], ACT.Exp).then_inc(lb_exp, 1)
            norm(0)
            for h in range(RH):
                for i in range(4 * h, 4 * h + 4):
                    filled(act, ("v", i))
                    if i % 4 >= 2:
                        filled(act, ("vtr", i - 2))
                    elif h:
                        filled(act, ("st", h - 1, 1))
                    frees(A.copy(tmpT[:, i % 2, :], bank(("v", i))[:, 0:NT]), ("v", i))
                if h == 0:
                    act.wait_ge(s_c2, 16)
                filled(act, ("kdt", h))
                if h >= 1:
                    filled(act, ("st", h - 1, 1))
                for st in range(2):
                    i = A.activation(kdec[:, st, :], bank(("kdt", h))[:, 256 * st:256 * st + 256], ACT.Copy,
                                     scale=dout[:, st, h:h + 1])
                frees(i, ("kdt", h))
                for j in range(2):
                    filled(act, ("o", h, j))
                    if h == 3 and j == 0:
                        act.wait_ge(v_stored, V_STORES[2])
                    frees(A.copy(oT[:, 4 * h + 2 * j:4 * h + 2 * j + 2, 0:NP_],
                                 bank(("o", h, j)).rearrange("p (a t) -> p a t", a=2)), ("o", h, j))
                for j in range(2):
                    filled(act, ("st", h, j))
                    if h >= 2 and j == 0:
                        act.wait_ge(s_store[h % 2], 16 * (h // 2))
                    i = A.copy(s_out[:, h % 2, 512 * j:512 * j + 512], bank(("st", h, j)))
                    frees(i, ("st", h, j))
                freed(act, ("st", h, 1))
                act.dma_start(ret_pout[h], s_out[:, h % 2, :].rearrange("p (k e) -> p k e", k=2))\
                    .then_inc(s_store[h % 2], 16)
            for i in range(16):
                filled(act, ("g", i))
                frees(A.activation(gT[:, i, :], bank(("g", i))[:, 0:NT], ACT.Silu), ("g", i))
            for h in range(RH):
                freed(act, ("mu", h))
                if h:
                    act.wait_ge(sq_summed, h)
                A.activation(sqg[:, :, :], oT[:, 4 * h:4 * h + 4, :], ACT.Square).then_inc(sq_ok, 1)
            filled(act, ("var", 0))
            frees(A.activation(std[0:8, :], bank(("var", 0), 8)[:, 0:NT], ACT.Sqrt, bias=eps_g[0:8]), ("var", 0))

            def high_part(n):
                act.wait_ge(arrived[where[blocks[n][1]]], need[blocks[n][1]])
                if n >= FPL:
                    if block_closes(n - FPL):
                        filled(act, blocks[n - FPL][0])
                    else:
                        act.wait_ge(fw_used, sum(not block_closes(m) for m in range(n - FPL + 1)))
                A.copy(block_part(fw_hi, n), block_raw(n)).then_inc(fw_hi_ok, 1)

            for h in range(UNITS):
                act.wait_ge(unit_out[h], 16 * NS)
            for j in range(2):
                act.wait_ge(s_store[j], 32)
            for n in range(FPL):
                high_part(n)
            norm(1)
            for k in range(KD):
                act.wait_ge(h_full_ok, k + 1)
                A.copy(h_hi[:, k, :], h_full[:, k, :]).then_inc(h_hi_ok, 1)
            for n in range(NB):
                kind, i = blocks[n][0]
                if kind == "fg":
                    filled(act, ("fg", i))
                    if i >= 2:
                        freed(act, ("fu", i - 2))
                    frees(A.activation(sg[:, i % 2, :], bank(("fg", i))[:, 0:NT], ACT.Silu), ("fg", i))
                if n + FPL < NB:
                    high_part(n + FPL)
                if kind == "fu":
                    freed(act, ("fu", i))
                    A.copy(hid_hi[:, i, :], hid[:, i % 2, :]).then_inc(hid_hi_ok, 1)
            norm(2)
            for h in range(HH):
                filled(act, ("hf", h))
                frees(A.activation(hf[:, h, :], bank(("hf", h))[:, 0:NT], ACT.Sigmoid), ("hf", h))
            act.wait_ge(f_ok, 8)
            A.activation(hf[:, :, 0:NP_], hf[:, :, 0:NP_], ACT.Ln).then_inc(logf_ok, 1)
            for i in range(8):
                filled(act, ("hi", i))
                if i >= 2:
                    filled(act, ("itr", i - 2))
                frees(A.copy(itmp[:, i % 2, :], bank(("hi", i))[:, 0:NT]), ("hi", i))
            for h in range(HH):
                filled(act, ("hq", h))
                frees(A.activation(hq[:, h, :], bank(("hq", h))[:, 0:NT], ACT.Silu), ("hq", h))
            for l in range(9):
                act.wait_ge(lev_sub, l + 1)
                A.activation(lev[l % 2], lev[l % 2], ACT.Exp).then_inc(lev_exp, 1)
                if l:
                    filled(act, ("hg", l - 1))
                    frees(A.copy(hgt[:, l - 1, :], bank(("hg", l - 1))[:, 0:NT]), ("hg", l - 1))
            freed(act, ("hg", 7))
            A.activation(hgt, hgt, ACT.Silu).then_inc(hgate_ok, 1)
            for j in range(4):
                filled(act, ("kt", j))
                frees(A.copy(kd_tok[:, 4 * j:4 * j + 4, :], bank(("kt", j)).rearrange("p (a t) -> p a t", a=4)),
                      ("kt", j))
            for j in range(4):
                filled(act, ("ho", j))
                frees(A.copy(oH[:, 2 * j:2 * j + 2, 0:NP_], bank(("ho", j)).rearrange("p (a t) -> p a t", a=2)),
                      ("ho", j))
            for j in range(2):
                filled(act, ("hs", j))
                frees(A.copy(hs_out[:, 4 * j:4 * j + 4, :], bank(("hs", j)).rearrange("p (a t) -> p a t", a=4)),
                      ("hs", j))
            freed(act, ("hs", 0))
            freed(act, ("hs", 1))
            act.dma_start(hg_pout, hs_out).then_inc(hs_store, 16)
            freed(act, ("hso", 0))
            for j in range(4):
                freed(act, ("ho", j))
            A.activation(hsq, oH[:, :, :], ACT.Square).then_inc(sq_ok, 1)
            filled(act, ("hvar", 0))
            frees(A.activation(std[0:8, :], bank(("hvar", 0), 8)[:, 0:NT], ACT.Sqrt, bias=eps_n[0:8]), ("hvar", 0))
            act.wait_ge(hs_store, 16)
            norm(3)
            act.wait_ge(h_ready, 32)
            act.dma_start(w_rt, ins["moe_router"][0].rearrange("(k p) e -> p k e", p=P)).then_inc(rt_in, 16)
            act.dma_start(gfin, ins["final_norm_g"].partition_broadcast(P)).then_inc(rt_in, 16)
            for j in range(12):
                filled(act, ("tok", j))
                src = bank(("tok", j))
                dst, t, q = (x_tok, j // 2, j % 2) if j < 6 else (h_tok, (j - 6) // 2, j % 2)
                m = P if t < 2 else NS
                if j >= 6 and t == 2:
                    act.wait_ge(pad_ok, 1)
                frees(A.copy(dst[0:m, t, 512 * q:512 * q + 512], src[0:m, :]), ("tok", j))
            act.wait_ge(e_in, 1)
            A.activation(prb, prb, ACT.Exp).then_inc(e_ok, 1)
            act.wait_ge(route_ok, 1)
            rounds = act.value_load(nri[0:1, 0:1], min_val=1, max_val=ROUNDS)
            act.sem_inc(y_free, 1)
            with act.Fori(0, rounds) as r:
                with act.Fori(0, NE) as e:
                    i = r * NE + e
                    for c in range(NCH + 1):
                        if c < NCH:
                            act.wait_ge(piece_used, i * (2 * NCH) + (2 * c + 1))
                            act.wait_ge(hide_ok, i * NCH + (1 + max(c - 1, 0)))
                            A.activation(act_g[:, c % 2, :], ps[:, c % 2, 0:4 * C], ACT.Silu).then_inc(gate_ok, 1)
                        if c:
                            t = epos["d", c - 1]
                            act.wait_ge(moe_arrived[t % RING], i * (16 * (EP // RING)) + 16 * (t // RING + 1))
                            for j in range(4):
                                g = 4 * (c - 1) + j
                                act.wait_ge(w_used, i * (4 * NCH) + (g - WPL + 3 if g >= WPL else 2))
                                A.copy(w_hi[:, g % WPL, :], piece(t % RING)[:, D * j:D * j + D]).then_inc(w_hi_ok, 1)
                        if c < NCH:
                            act.wait_ge(hide_ok, i * NCH + (c + 2))
                            if c == 0:
                                act.wait_ge(w_used, i * (4 * NCH) + 2)
                            A.copy(hide_hi[:, c % 2, :], hide[:, c % 2, :]).then_inc(hide_hi_ok, 1)
                    act.wait_ge(w_used, i * (4 * NCH) + (4 * NCH + 2))
                    A.copy(y_out[0:C, 0:512], ps[0:C, 4, :])
                    A.copy(y_out[0:C, 512:1024], ps[0:C, 5, :]).then_inc(y_free, 1)
                    act.wait_ge(y_free, i + 2)
                    act.dma_start(y_scr[bass.ds(i * C, C), :], y_out[0:C, :]).then_inc(y_store, 16)
                    act.wait_ge(y_store, i * 16 + 16)
            A.copy(frs[:, 0:1], red3[:, 0:1]).then_inc(all_stored, 1)
            for t in range(3):
                m = P if t < 2 else NS
                act.wait_ge(fin_in, t + 1)
                A.activation(ysq[0:m, :], yf[0:m, t, :], ACT.Square, accum_out=fsum[0:m, t:t + 1]).then_inc(fin_sq, 1)
                act.wait_ge(fin_sq, t + 1)
                A.activation(fsum[0:m, t:t + 1], fsum[0:m, t:t + 1], ACT.Sqrt, bias=eps_n[0:m], scale=1.0 / D)\
                    .then_inc(fin_std, 1)
            for t in range(3):
                act.wait_ge(fin_ok, t + 1)
                if t < 2:
                    act.dma_start(outs["y_p"][0, P * t:P * t + P, :], yf[:, t, :]).then_inc(out_done, 16)
                else:
                    act.dma_start(outs["y_s"].rearrange("b s d -> (b s) d"), yf[0:NS, 2, :]).then_inc(out_done, 16)
            act.wait_ge(out_done, 48)
            for s_ in range(2):
                act.wait_ge(s_store[s_], 32)
                act.wait_ge(hu_out[s_], 16 * NS // 2)
            for s_ in range(UNITS):
                act.wait_ge(unit_out[s_], 16 * NS)

        @block.vector
        def _(dve):
            V = nc.vector
            steps = [0]

            def link(i):
                steps[0] += 1
                i.then_inc(dve_step, 1)
                dve.wait_ge(dve_step, steps[0])

            dve.wait_ge(s_c, 16)
            for j in range(4):
                filled(dve, ("xt", j))
                frees(V.tensor_copy(xT[:, 4 * (j % 2):4 * (j % 2) + 4, P * (j // 2):P * (j // 2) + P],
                                    bank(("xt", j)).rearrange("p (a t) -> p a t", a=4)), ("xt", j))
            filled(dve, ("xt", 4))
            frees(V.tensor_copy(xT[:, :, NP_:NT], bank(("xt", 4))[:, 0:64].rearrange("p (a t) -> p a t", a=8)),
                  ("xt", 4))
            filled(dve, ("xt", 5))
            frees(V.tensor_copy(vec[:, :], bank(("xt", 5))[:, 0:NVEC]), ("xt", 5))
            freed(dve, ("xt", 5))
            a0, a1 = vec[:, VEC["lb"]:VEC["lb"] + 8], vec[:, VEC["lb"] + 8:VEC["lb"] + 16]
            link(V.tensor_tensor(lbt[:, 0, :], a0, a1, ALU.max))
            link(V.tensor_tensor(lbt[:, 1, :], a0, lbt[:, 0, :], ALU.subtract))
            V.tensor_tensor(lbt[:, 2, :], a1, lbt[:, 0, :], ALU.subtract).then_inc(lb_in, 1)
            dve.wait_ge(lb_exp, 1)
            link(V.tensor_tensor(lbt[:, 3, :], lbt[:, 1, :], lbt[:, 2, :], ALU.add))
            link(V.reciprocal(lbt[:, 4, :], lbt[:, 3, :]))
            link(V.tensor_tensor(lbt[:, 1, :], lbt[:, 1, :], lbt[:, 4, :], ALU.mult))
            link(V.tensor_tensor(lbt[:, 2, :], lbt[:, 2, :], lbt[:, 4, :], ALU.mult))
            link(V.tensor_tensor(lbt[:, 5, :], lbt[:, 1, :], lbt[:, 2, :], ALU.add))
            link(V.tensor_tensor(lbt[:, 6, :], lbt[:, 5, :], lbt[:, 1, :], ALU.subtract))
            link(V.tensor_scalar(lbt[:, 7, :], lbt[:, 6, :], -1.0, 1.0, ALU.mult, ALU.add))
            lb, oml = lbt[:, 6, :], lbt[:, 7, :]

            def norm(n, gain):
                freed(dve, ("ms", n))
                link(V.reciprocal(rstd[:, :], std[:, :]))
                filled(dve, ("ms", n))
                for k in range(KD):
                    V.scalar_tensor_tensor(out=hT[:, k, :], in0=xT[:, k, :], scalar=vec[:, gain + k:gain + k + 1],
                                           in1=rstd[:, :], op0=ALU.mult, op1=ALU.mult).then_inc(h_ready, 1)

            def residual(kind):
                for i in range(8):
                    filled(dve, (kind, i))
                    frees(V.tensor_tensor(xT[:, i, :], xT[:, i, :], bank((kind, i))[:, 0:NT], ALU.add), (kind, i))
                freed(dve, (kind, 7))

            norm(0, VEC["mix"])
            dve.wait_ge(s_c2, 16)
            def rotate(a):
                dst = qT if a < 4 else kT
                t = 2 * (a % 4)
                filled(dve, ("qk", 2 * a))
                filled(dve, ("qk", 2 * a + 1))
                x1, x2 = bank(("qk", 2 * a))[:, 0:NT], bank(("qk", 2 * a + 1))[:, 0:NT]
                if rotated[0]:
                    dve.wait_ge(qk_ready, rotated[0])
                V.tensor_tensor(rot[:, 0, :], x1, cos, ALU.mult)
                V.tensor_tensor(rot[:, 1, :], x2, sin, ALU.mult)
                frees(V.tensor_tensor(rot[:, 2, :], x2, cos, ALU.mult), ("qk", 2 * a + 1))
                frees(V.tensor_tensor(rot[:, 3, :], x1, sin, ALU.mult), ("qk", 2 * a))
                freed(dve, ("qk", 2 * a))
                V.tensor_tensor(dst[:, t, :], rot[:, 0, :], rot[:, 1, :], ALU.subtract)
                V.tensor_tensor(dst[:, t + 1, :], rot[:, 2, :], rot[:, 3, :], ALU.add).then_inc(qk_ready, 1)
                rotated[0] += 1

            def v_rows(i):
                filled(dve, ("vtr", i))
                s = bank(("vtr", i))
                V.tensor_copy(v_tok[:, :, P * i:P * i + P], s[:, 0:256].rearrange("p (a e) -> p a e", a=2))
                if i >= 8 and i % 4 == 0:
                    dve.wait_ge(v_stored, V_STORES[i // 4 - 2])
                parts_ = v_smp[i // 4 % 2]
                rows, o = parts_[(i % 4) * len(parts_) // 4]
                e = P * (i % 4) - o
                frees(V.tensor_copy(rows[:, e:e + P], s[0:NS, 256:384]), ("vtr", i))

            def update(u):
                b, h = unit_of(u)
                j = u % UNITS
                S = unit[:, j, 0:1024]
                dve.wait_ge(unit_s[j], 16 * (u // UNITS + 1))
                link(V.tensor_scalar(S, S, GAMMA[h], None, ALU.mult))
                dve.wait_ge(unit_v[j], 16 * (u // UNITS + 1))
                for k in range(2):
                    i = V.scalar_tensor_tensor(out=S[:, 512 * k:512 * k + 512], in0=unit[:, j, 1024:1536],
                                               scalar=ksmp[:, 2 * h + k, b:b + 1], in1=S[:, 512 * k:512 * k + 512],
                                               op0=ALU.mult, op1=ALU.add)
                i.then_inc(unit_new, 1)

            rotated = [0]
            for h in range(RH):
                if h:
                    filled(dve, ("o", h - 1, 1))
                for n, a in enumerate((h, 4 + h)):
                    rotate(a)
                    for tile_ in (8 * h + 2 * n, 8 * h + 2 * n + 1):
                        for u in units_after(tile_):
                            update(u)
                dve.wait_ge(qk_ready, 2 * (h + 1))
                link(V.tensor_scalar(ksmp[:, 2 * h:2 * h + 2, :], kT[:, 2 * h:2 * h + 2, NP_:NT], RDK ** -0.5, None,
                                     ALU.mult))
                for n in range(4):
                    v_rows(4 * h + n)
                    for u in units_after(8 * h + 4 + n):
                        update(u)
                filled(dve, ("sc", h))
                if h:
                    filled(dve, ("o", h - 1, 1))
                s = bank(("sc", h))
                V.tensor_tensor(prob[:, 0:256], s[:, 0:256], dmask[:, h, :], ALU.mult)
                frees(V.tensor_tensor(prob[:, 256:384], s[:, 256:384], dmask[:, h, 0:P], ALU.mult), ("sc", h))
            for tile_ in range(32, 48):
                for u in units_after(tile_):
                    update(u)
            filled(dve, ("so", 0))
            frees(V.tensor_copy(oT[:, :, NP_:NT], bank(("so", 0))[:, 0:P].rearrange("p (a b) -> p a b", a=16)),
                  ("so", 0))
            for h in range(RH):
                filled(dve, ("mu", h))
                o = oT[:, 4 * h:4 * h + 4, :]
                frees(V.tensor_tensor(o, o, bank(("mu", h))[:, 0:NT].unsqueeze(1).to_broadcast([P, 4, NT]),
                                      ALU.subtract), ("mu", h))
            freed(dve, ("var", 0))
            V.reciprocal(rstd[0:8, :], std[0:8, :]).then_inc(r8_ok, 1)
            for h in range(RH):
                filled(dve, ("rs", h))
                if h == 0:
                    freed(dve, ("g", 15))
                for e in range(4):
                    t = 4 * h + e
                    i = V.scalar_tensor_tensor(out=oT[:, t, :], in0=oT[:, t, :],
                                               scalar=vec[:, VEC["gn"] + t:VEC["gn"] + t + 1],
                                               in1=bank(("rs", h))[:, 0:NT], op0=ALU.mult, op1=ALU.mult)
                frees(i, ("rs", h))
                freed(dve, ("rs", h))
                o = oT[:, 4 * h:4 * h + 4, :]
                V.tensor_tensor(o, o, gT[:, 4 * h:4 * h + 4, :], ALU.mult).then_inc(o_ok, 1)

            def low_part(n):
                dve.wait_ge(fw_hi_ok, n + 1)
                V.tensor_tensor(block_part(fw_lo, n), block_raw(n), block_part(fw_hi, n).bitcast(F32), ALU.subtract)\
                    .then_inc(fw_lo_ok, 1)

            for n in range(FPL):
                low_part(n)
            residual("wo")
            freed(dve, ("ms", 1))
            link(V.reciprocal(rstd[:, :], std[:, :]))
            filled(dve, ("ms", 1))
            g0 = VEC["ffn"]
            for k in range(KD + 1):
                if k < KD:
                    V.scalar_tensor_tensor(out=h_full[:, k, :], in0=xT[:, k, :], scalar=vec[:, g0 + k:g0 + k + 1],
                                           in1=rstd[:, :], op0=ALU.mult, op1=ALU.mult).then_inc(h_full_ok, 1)
                if k:
                    dve.wait_ge(h_hi_ok, k)
                    V.tensor_tensor(h_lo[:, k - 1, :], h_full[:, k - 1, :], h_hi[:, k - 1, :].bitcast(F32),
                                    ALU.subtract).then_inc(h_ready, 1)
            for n in range(NB):
                kind, i = blocks[n][0]
                if kind == "fu":
                    filled(dve, ("fu", i))
                    freed(dve, ("fg", i))
                    frees(V.tensor_tensor(hid[:, i % 2, :], sg[:, i % 2, :], bank(("fu", i))[:, 0:NT], ALU.mult),
                          ("fu", i))
                if kind == "fd" and block_closes(n):
                    filled(dve, ("fd", i))
                    frees(V.tensor_tensor(xT[:, i, :], xT[:, i, :], bank(("fd", i))[:, 0:NT], ALU.add), ("fd", i))
                if n + FPL < NB:
                    low_part(n + FPL)
                if kind == "fu":
                    dve.wait_ge(hid_hi_ok, i + 1)
                    V.tensor_tensor(hid_lo[:, i, :], hid[:, i % 2, :], hid_hi[:, i, :].bitcast(F32), ALU.subtract)\
                        .then_inc(hid_ok, 1)
            freed(dve, ("fd", 7))
            norm(2, VEC["mix"] + 8)
            for h in range(HH):
                freed(dve, ("hf", h))
                link(V.tensor_scalar(hf[:, h, :], hf[:, h, :], oml[:, h:h + 1], lb[:, h:h + 1], ALU.mult, ALU.add))
                V.tensor_scalar(hk[:, h, :], hf[:, h, :], -1.0, 1.0, ALU.mult, ALU.add)
                i = V.tensor_copy(fsmp[:, h, :], hf[:, h, NP_:NT])
                i.then_inc(f_ok, 1)
            dve.wait_ge(logf_ok, 1)
            for h in range(HH):
                i = V.tensor_tensor_scan(bcum[:, h, :], cc("reset"), hf[:, h, 0:NP_], 0.0, ALU.mult, ALU.add)
            link(i)
            bch = bcum.rearrange("p h (c t) -> p h c t", t=CHUNK)
            T = [bch[:, :, c, CHUNK - 1] for c in range(4)]
            V.tensor_copy(tots[:, 2, :], T[3])
            link(V.tensor_tensor(tots[:, 1, :], T[2], T[3], ALU.add))
            link(V.tensor_tensor(tots[:, 0, :], tots[:, 1, :], T[1], ALU.add))

            def reader(l):
                return ("lv", l + 1, 3) if l <= 6 else ("cr", 1)

            def exponents(l):
                if l >= 2:
                    filled(dve, reader(l - 2))
                L = lev[l % 2]
                lc = L.rearrange("p (h c t) -> p h c t", h=8, t=CHUNK)
                tot = lambda a, b: bch[:, :, a:b, CHUNK - 1:CHUNK].to_broadcast([P, 8, b - a, CHUNK])
                if l <= 5:
                    m = 1 << l
                    n = 2048 // (2 * m)
                    bv = bcum.rearrange("p h t -> p (h t)").rearrange("p (n t) -> p n t", t=2 * m)
                    lv = L.rearrange("p (n t) -> p n t", t=2 * m)
                    mid = bv[:, :, m - 1:m].to_broadcast([P, n, m])
                    V.tensor_tensor(lv[:, :, m:], bv[:, :, m:], mid, ALU.subtract)
                    i = V.tensor_tensor(lv[:, :, 0:m], mid, bv[:, :, 0:m], ALU.subtract)
                elif l == 6:
                    for c in (0, 2):
                        V.tensor_tensor(lc[:, :, c:c + 1, :], tot(c, c + 1), bch[:, :, c:c + 1, :], ALU.subtract)
                        i = V.tensor_copy(lc[:, :, c + 1, :], bch[:, :, c + 1, :])
                elif l == 7:
                    link(V.tensor_tensor(lc[:, :, 0:2, :], tot(0, 2), bch[:, :, 0:2, :], ALU.subtract))
                    V.tensor_tensor(lc[:, :, 0, :], lc[:, :, 0, :], tot(1, 2)[:, :, 0, :], ALU.add)
                    V.tensor_copy(lc[:, :, 2, :], bch[:, :, 2, :])
                    i = V.tensor_tensor(lc[:, :, 3, :], bch[:, :, 3, :], tot(2, 3)[:, :, 0, :], ALU.add)
                else:
                    link(V.tensor_tensor(lc, tot(0, 4), bch, ALU.subtract))
                    for c in range(3):
                        i = V.tensor_tensor(lc[:, :, c, :], lc[:, :, c, :],
                                            tots[:, c, :].unsqueeze(2).to_broadcast([P, 8, CHUNK]), ALU.add)
                i.then_inc(lev_sub, 1)

            def operands(l):
                dve.wait_ge(lev_exp, l + 1)
                L = lev[l % 2]
                if l < 8:
                    m = min(1 << l, 128)
                    lv = L.rearrange("p (h n t) -> p h n t", h=8, t=2 * m)
                    kv = hk[:, :, 0:NP_].rearrange("p h (n t) -> p h n t", t=2 * m)
                    qv = hq[:, :, 0:NP_].rearrange("p h (n t) -> p h n t", t=2 * m)
                    V.tensor_tensor(lv[:, :, :, m:], lv[:, :, :, m:], qv[:, :, :, m:], ALU.mult)
                    i = V.tensor_tensor(lv[:, :, :, 0:m], lv[:, :, :, 0:m], kv[:, :, :, 0:m], ALU.mult)
                else:
                    L = L.rearrange("p (h t) -> p h t", h=8)
                    i = V.tensor_tensor(L, L, hk[:, :, 0:NP_], ALU.mult)
                i.then_inc(lev_x, 1)

            def choose(l):
                if l:
                    freed(dve, ("lv", l - 1, 3))
                for j in range(4):
                    filled(dve, ("lv", l, j))
                    src = bank(("lv", l, j)).rearrange("p (a t) -> p a t", a=4)
                    dst = att[:, 2 * j:2 * j + 2, :, :].rearrange("p h a t -> p (h a) t")
                    if l == 0:
                        i = V.tensor_tensor(dst, src, ident.unsqueeze(1).to_broadcast([P, 4, P]), ALU.mult)
                    else:
                        i = V.copy_predicated(dst, lvl[:, l - 1, :].unsqueeze(1).to_broadcast([P, 4, P]), src)
                    frees(i, ("lv", l, j))

            for h in range(UNITS):
                dve.wait_ge(unit_out[h], 16 * NS)
            for j in range(2):
                dve.wait_ge(s_store[j], 32)
            for i in range(8):
                filled(dve, ("itr", i))
                s = bank(("itr", i))
                V.tensor_copy(i_tok[:, :, P * i:P * i + P], s[:, 0:256].rearrange("p (a e) -> p a e", a=2))
                frees(V.tensor_copy(i_smp[:, P * i:P * i + P], s[0:NS, 256:384]), ("itr", i))
            exponents(0)
            choose(0)
            for l in range(9):
                if l < 8:
                    exponents(l + 1)
                operands(l)
                if 1 <= l <= 7:
                    choose(l)
            filled(dve, ("hso", 0))
            frees(V.tensor_copy(oH[:, :, NP_:NT], bank(("hso", 0))[:, 0:64].rearrange("p (h b) -> p h b", h=8)),
                  ("hso", 0))
            dve.wait_ge(i_stored, 16)
            for j in range(2):
                filled(dve, ("cr", j))
                frees(V.tensor_copy(cross[:, 4 * j:4 * j + 4, :], bank(("cr", j)).rearrange("p (a t) -> p a t", a=4)),
                      ("cr", j))
            freed(dve, ("hvar", 0))
            V.reciprocal(rstd[0:8, :], std[0:8, :]).then_inc(r8_ok, 1)
            for h in range(HH):
                filled(dve, ("hrs", h))
                frees(V.scalar_tensor_tensor(out=oH[:, h, :], in0=oH[:, h, :],
                                             scalar=vec[:, VEC["hgn"] + h:VEC["hgn"] + h + 1],
                                             in1=bank(("hrs", h))[:, 0:NT], op0=ALU.mult, op1=ALU.mult), ("hrs", h))
            freed(dve, ("hrs", 7))
            dve.wait_ge(hgate_ok, 1)
            V.tensor_tensor(oH[:, :, :], oH[:, :, :], hgt, ALU.mult).then_inc(o_ok, 1)
            residual("hw")
            norm(3, VEC["ffn"] + 8)
            V.memset(h_tok[:, 2, :], 0.0).then_inc(pad_ok, 1)
            link(V.memset(lg, 0.0))
            filled(dve, ("lg", 0))
            for t in range(3):
                m = P if t < 2 else NS
                i = V.tensor_copy(lg[0:m, t, :], bank(("lg", 0))[0:m, 8 * t:8 * t + 8])
            frees(i, ("lg", 0))
            freed(dve, ("lg", 0))
            link(V.reduce_max(red3, lg, AX.X))
            V.tensor_tensor(prb, lg, red3.unsqueeze(2).to_broadcast([P, 3, 8]), ALU.subtract).then_inc(e_in, 1)
            dve.wait_ge(e_ok, 1)
            link(V.reduce_sum(red3, prb, AX.X))
            link(V.reciprocal(fsum, red3))
            link(V.tensor_tensor(prb, prb, fsum.unsqueeze(2).to_broadcast([P, 3, 8]), ALU.mult))
            for t in range(3):
                link(V.max(m8[:, t, :], prb[:, t, :]))
                i = V.max_index(ix[:, t, :], m8[:, t, :], prb[:, t, :])
            link(i)
            link(V.tensor_copy(ixf, ix))
            valid = cc("valid")
            for t in range(3):
                V.tensor_scalar(oa[:, t, :], cc("exp8"), ixf[:, t, 0:1], valid[:, t:t + 1], ALU.is_equal, ALU.mult)
                i = V.tensor_scalar(ob[:, t, :], cc("exp8"), ixf[:, t, 1:2], valid[:, t:t + 1], ALU.is_equal, ALU.mult)
            link(i)
            V.tensor_tensor(mm_, oa, ob, ALU.add).then_inc(mask_ok, 1)
            link(V.tensor_tensor(wab[:, :, 2], m8[:, :, 0], m8[:, :, 1], ALU.add))
            link(V.reciprocal(wab[:, :, 3], wab[:, :, 2]))
            V.tensor_tensor(wab[:, :, 0], m8[:, :, 0], wab[:, :, 3], ALU.mult)
            V.tensor_tensor(wab[:, :, 1], m8[:, :, 1], wab[:, :, 3], ALU.mult)
            filled(dve, ("rk", 0))
            frees(V.tensor_copy(rk, bank(("rk", 0))[:, 0:32].rearrange("p (a e) -> p a e", a=4)), ("rk", 0))
            freed(dve, ("rk", 0))
            def select(i):
                for t in range(3):
                    s = V.tensor_scalar(gsel[:, t, :], cc("slot"), reff[:, t, bass.ds(i, 1)], None, ALU.is_equal)
                s.then_inc(sel_ok, 1)

            dve.wait_ge(mask_ok, 1)
            link(V.memset(reff, -1.0))
            for r in range(ROUNDS):
                link(V.tensor_scalar(r1, rk[:, 0:3, :], 1.0 - r * C, None, ALU.add))
                link(V.tensor_tensor(r1, r1, mm_, ALU.mult))
                link(V.tensor_scalar(reff[:, :, 8 * r:8 * r + 8], r1, -1.0, None, ALU.add))
            link(V.reduce_max(nrf[:, 0:1], rk[:, 3, :], AX.X))
            link(V.memset(nrf[:, 1:2], 1.0))
            for r in range(1, ROUNDS):
                link(V.tensor_scalar(nrf[:, 2:3], nrf[:, 0:1], float(r * C), None, ALU.is_gt))
                link(V.tensor_tensor(nrf[:, 1:2], nrf[:, 1:2], nrf[:, 2:3], ALU.add))
            V.tensor_copy(nri, nrf[:, 1:2]).then_inc(route_ok, 1)
            dve.sem_inc(hide_ok, 1)
            select(0)
            for w, o in enumerate((oa, ob)):
                link(V.tensor_tensor(r1, rk[:, 0:3, :], o, ALU.mult))
                link(V.reduce_sum(va[:, w, :], r1, AX.X))
                link(V.tensor_scalar(rowf[:, w, :], ixf[:, :, w], float(C), None, ALU.mult))
                link(V.tensor_tensor(rowf[:, w, :], rowf[:, w, :], va[:, w, :], ALU.add))
                for r in range(1, ROUNDS):
                    link(V.tensor_scalar(vt[:, w, :], va[:, w, :], float(r * C), float((NE - 1) * C), ALU.is_ge,
                                         ALU.mult))
                    link(V.tensor_tensor(rowf[:, w, :], rowf[:, w, :], vt[:, w, :], ALU.add))
            V.tensor_copy(rowi, rowf).then_inc(rows_ok, 1)
            dve.wait_ge(route_ok, 1)
            rounds = dve.value_load(nri[0:1, 0:1], min_val=1, max_val=ROUNDS)
            with dve.Fori(0, rounds) as r:
                with dve.Fori(0, NE) as e:
                    i = r * NE + e
                    dve.wait_ge(xg_full, i + 1)
                    for q in range(2):
                        V.tensor_copy(xe[:, 4 * q:4 * q + 4, :],
                                      ps[:, 6 + q, 0:4 * C].rearrange("p (a s) -> p a s", a=4)).then_inc(xe_ok, 1)
                    select(i + 1)

                    def low_parts(c, js):
                        for j in js:
                            dve.wait_ge(w_hi_ok, i * (4 * NCH) + (4 * c + j + 1))
                            V.tensor_tensor(w_lo[:, (4 * c + j) % WPL, :], piece(epos["d", c] % RING)[:, D * j:D * j + D],
                                            w_hi[:, (4 * c + j) % WPL, :].bitcast(F32), ALU.subtract).then_inc(w_lo_ok, 1)

                    for c in range(NCH + 1):
                        if c:
                            low_parts(c - 1, (0, 1))
                        if c < NCH:
                            dve.wait_ge(piece_used, i * (2 * NCH) + (2 * c + 2))
                            dve.wait_ge(gate_ok, i * NCH + (c + 1))
                            V.tensor_tensor(hide[:, c % 2, :], act_g[:, c % 2, :], ps[:, 2 + c % 2, 0:4 * C], ALU.mult)\
                                .then_inc(hide_ok, 1)
                        if c:
                            low_parts(c - 1, (2, 3))
                        if c < NCH:
                            dve.wait_ge(hide_hi_ok, i * NCH + (c + 1))
                            V.tensor_tensor(hide_lo[:, c % 2, :], hide[:, c % 2, :],
                                            hide_hi[:, c % 2, :].bitcast(F32), ALU.subtract).then_inc(hide_lo_ok, 1)
            for t in range(4):
                if t < 3:
                    m = P if t < 2 else NS
                    dve.wait_ge(ya_in[t], 32)
                    link(V.scalar_tensor_tensor(out=yf[0:m, t, :], in0=ya[0:m, t, :], scalar=wab[0:m, t, 0:1],
                                                in1=x_tok[0:m, t, :], op0=ALU.mult, op1=ALU.add))
                    V.scalar_tensor_tensor(out=yf[0:m, t, :], in0=yb[0:m, t, :], scalar=wab[0:m, t, 1:2],
                                           in1=yf[0:m, t, :], op0=ALU.mult, op1=ALU.add).then_inc(fin_in, 1)
                if t:
                    z = t - 1
                    m = P if z < 2 else NS
                    dve.wait_ge(fin_std, z + 1)
                    link(V.reciprocal(frs[0:m, z:z + 1], fsum[0:m, z:z + 1]))
                    V.scalar_tensor_tensor(out=yf[0:m, z, :], in0=yf[0:m, z, :], scalar=frs[0:m, z:z + 1],
                                           in1=gfin[0:m, :], op0=ALU.mult, op1=ALU.mult).then_inc(fin_ok, 1)

        @block.tensor
        def _(pe):
            def claim(name):
                b, k = FILL[name]
                if k:
                    pe.wait_ge(bank_free[b], k)

            def close(ins, name):
                ins.then_inc(bank_full[FILL[name][0]], 1)

            def mm(out, lhsT, rhs, first=True, last=True):
                return nc.tensor.matmul(out, lhsT, rhs, start=first, stop=last)

            pe.wait_ge(s_c, 16)
            pe.wait_ge(s_x, 32)
            for j in range(4):
                claim(("xt", j))
                for a in range(4):
                    k = 4 * (j % 2) + a
                    i = nc.tensor.transpose(bank(("xt", j))[:, P * a:P * a + P], x_in[:, j // 2, P * k:P * k + P], ident)
                close(i, ("xt", j))
            for k in range(KD):
                i = nc.tensor.transpose(bank(("xt", 4))[:, NS * k:NS * k + NS], x_in[0:NS, 2, P * k:P * k + P],
                                        ident[0:NS, 0:NS])
            close(i, ("xt", 4))
            pe.wait_ge(s_v, 80)
            close(nc.tensor.transpose(bank(("xt", 5))[:, 0:NVEC], vrow[0:NVEC, :], ident[0:NVEC, 0:NVEC]), ("xt", 5))

            def mean_square(n):
                claim(("ms", n))
                for k in range(KD):
                    if k % 4 == 0:
                        pe.wait_ge(squares, 2 * n + k // 4 + 1)
                    i = mm(bank(("ms", n))[:, 0:NT], cc("mean_d"), hT[:, k, :], k == 0, k == KD - 1)
                close(i, ("ms", n))

            def arrive(name):
                pe.wait_ge(arrived[where[name]], need[name])

            def project(name, w, n_norm=None):
                claim(name)
                for k in range(KD):
                    if n_norm is not None:
                        pe.wait_ge(h_ready, 8 * n_norm + k + 1)
                    i = mm(bank(name)[:, 0:NT], w[:, k, :], hT[:, k, :], k == 0, k == KD - 1)
                close(i, name)

            def pview(name, k, off=0, n=None):
                w = (n or PIECE // k) * k
                return piece(where[name])[:, off:off + w].rearrange("p (k n) -> p k n", k=k)

            def to_tokens(kind, src, dst):
                freed(pe, src)
                claim(dst)
                o = bank(dst)
                for a in range(2):
                    nc.tensor.transpose(o[:, P * a:P * a + P], kind[:, P * a:P * a + P], ident)
                close(nc.tensor.transpose(o[0:NS, 256:384], kind[:, NP_:NT], ident), dst)

            mean_square(0)
            def attention(h):
                claim(("sc", h))
                s = bank(("sc", h))
                for k in range(2):
                    mm(s[:, 0:256], kT[:, 2 * h + k, 0:P], qT[:, 2 * h + k, 0:256], k == 0, k == 1)
                for k in range(2):
                    i = mm(s[:, 256:384], kT[:, 2 * h + k, P:256], qT[:, 2 * h + k, P:256], k == 0, k == 1)
                close(i, ("sc", h))
                claim(("kdt", h))
                for st in range(2):
                    for k in range(2):
                        i = nc.tensor.transpose(bank(("kdt", h))[:, 256 * st + P * k:256 * st + P * k + P],
                                                kT[:, 2 * h + k, P * st:P * st + P], ident)
                close(i, ("kdt", h))
                freed(pe, ("sc", h))
                for j in range(2):
                    claim(("o", h, j))
                    for e in range(2):
                        a = 512 * h + 256 * j + P * e
                        o = bank(("o", h, j))[:, 256 * e:256 * e + 256]
                        mm(o, v_tok[:, 0, a:a + P], prob[:, 0:256], True, False)
                        i = mm(o[:, P:256], v_tok[:, 1, a:a + P], prob[:, 256:384], False, True)
                    close(i, ("o", h, j))
                freed(pe, ("kdt", h))
                for j in range(2):
                    claim(("st", h, j))
                    for st in range(2):
                        i = mm(bank(("st", h, j)), kdec[:, st, P * j:P * j + P], v_tok[:, st, 512 * h:512 * h + 512],
                               st == 0, st == 1)
                    close(i, ("st", h, j))

            def sample_unit(u):
                b, h = unit_of(u)
                if u == 0:
                    claim(("so", 0))
                pe.wait_ge(unit_new, u + 1)
                for e in range(4):
                    for k in range(2):
                        c = NS * (4 * h + e) + b
                        i = mm(bank(("so", 0))[:, c:c + 1], unit[:, u % UNITS, 512 * k + P * e:512 * k + P * e + P],
                               qT[:, 2 * h + k, NP_ + b:NP_ + b + 1], k == 0, k == 1)
                if u == NS * RH - 1:
                    close(i, ("so", 0))
                else:
                    i.then_inc(unit_pe, 1)

            def sample_units(tile_):
                for u in units_after(tile_ - UNIT_LAG):
                    sample_unit(u)

            for h in range(RH):
                for n, i in enumerate(QK_TILES[h]):
                    p_ = ("rwi", i // 4)
                    arrive(p_)
                    project(("qk", i), pview(p_, 8)[:, :, P * (i % 4):P * (i % 4) + P], 0 if i == 0 else None)
                    sample_units(8 * h + n)
                arrive(("rwi", 4 + h))
                for n in range(4):
                    i = 4 * h + n
                    project(("v", i), pview(("rwi", 4 + h), 8)[:, :, P * n:P * n + P])
                    if n:
                        to_tokens(tmpT[:, (i - 1) % 2, :], ("v", i - 1), ("vtr", i - 1))
                    sample_units(8 * h + 4 + n)
                to_tokens(tmpT[:, 1, :], ("v", 4 * h + 3), ("vtr", 4 * h + 3))
                pe.wait_ge(qk_ready, 2 * (h + 1))
                freed(pe, ("vtr", 4 * h + 2))
                freed(pe, ("vtr", 4 * h + 3))
                attention(h)
            for i in range(16):
                p_ = ("rwi", 8 + i // 4)
                if i % 4 == 0:
                    arrive(p_)
                project(("g", i), pview(p_, 8)[:, :, P * (i % 4):P * (i % 4) + P])
                sample_units(32 + i)
            for tile_ in range(48, 48 + UNIT_LAG):
                sample_units(tile_)
            freed(pe, ("so", 0))
            pe.wait_ge(s_c2, 16)
            for h in range(RH):
                freed(pe, ("o", h, 0))
                freed(pe, ("o", h, 1))
                claim(("mu", h))
                for e in range(4):
                    i = mm(bank(("mu", h))[:, 0:NT], cc("mean_gn"), oT[:, 4 * h + e, :], e == 0, e == 3)
                close(i, ("mu", h))
            claim(("var", 0))
            for h in range(RH):
                pe.wait_ge(sq_ok, h + 1)
                for e in range(4):
                    i = mm(bank(("var", 0), 8)[:, 0:NT], col_gn[:, h, :], sqg[:, e, :], h + e == 0, h + e == 6)
                if h < 3:
                    i.then_inc(sq_summed, 1)
            close(i, ("var", 0))
            pe.wait_ge(r8_ok, 1)
            for h in range(RH):
                claim(("rs", h))
                close(mm(bank(("rs", h))[:, 0:NT], rowsel[0:8, h, :], rstd[0:8, :]), ("rs", h))
            for j in range(4):
                p_ = ("rwo", j)
                arrive(p_)
                w = pview(p_, 16)
                for a in range(2):
                    name = ("wo", 2 * j + a)
                    claim(name)
                    for k in range(16):
                        if name[1] == 0 and k % 4 == 0:
                            pe.wait_ge(o_ok, k // 4 + 1)
                        i = mm(bank(name)[:, 0:NT], w[:, k, P * a:P * a + P], oT[:, k, :], k == 0, k == 15)
                    close(i, name)
            mean_square(1)
            for n in range(NB):
                name, _, _, _, _, k0, k1, base = blocks[n]
                if k0 + base == 0:
                    claim(name)
                pe.wait_ge(fw_lo_ok, n + 1)
                for k in range(k0, k1):
                    kk = base + k
                    if name[0] == "fd":
                        if name[1] == 0:
                            pe.wait_ge(hid_ok, kk + 1)
                        x_hi, x_lo = hid_hi[:, kk, :], hid_lo[:, kk, :]
                    else:
                        if n == 0:
                            pe.wait_ge(h_ready, 8 + kk + 1)
                        x_hi, x_lo = h_hi[:, kk, :], h_lo[:, kk, :]
                    whi, wlo = block_part(fw_hi, n)[:, k - k0, :], block_part(fw_lo, n)[:, k - k0, :]
                    o = bank(name)[:, 0:NT]
                    last = kk == (FT if name[0] == "fd" else KD) - 1
                    mm(o, whi, x_hi, kk == 0, False)
                    mm(o, whi, x_lo, False, False)
                    i = mm(o, wlo, x_hi, False, last)
                if block_closes(n):
                    close(i, name)
                else:
                    i.then_inc(fw_used, 1)
            mean_square(2)
            for a, kind in enumerate(("hf", "hi", "hq")):
                for i in range(8):
                    p_ = ("hwi", 2 * a + i // 4)
                    if i % 4 == 0:
                        arrive(p_)
                    project((kind, i), pview(p_, 8)[:, :, P * (i % 4):P * (i % 4) + P], 2 if a + i == 0 else None)
                    if kind == "hi" and i:
                        to_tokens(itmp[:, (i - 1) % 2, :], ("hi", i - 1), ("itr", i - 1))
                if kind == "hi":
                    to_tokens(itmp[:, 1, :], ("hi", 7), ("itr", 7))
            claim(("hso", 0))
            pe.wait_ge(f_ok, 8)
            freed(pe, ("hq", 7))
            for l in range(8):
                if l:
                    pe.wait_ge(lev_x, l)
                for j in range(4):
                    name = ("lv", l, j)
                    claim(name)
                    for a in range(4):
                        h, t = 2 * j + a // 2, a % 2
                        if l:
                            L = lev[(l - 1) % 2].rearrange("p (h t) -> p h t", h=8)
                            x, y = L[:, h, P * t:P * t + P], L[:, h, P * t:P * t + P]
                        else:
                            x, y = hk[:, h, P * t:P * t + P], hq[:, h, P * t:P * t + P]
                        i = mm(bank(name)[:, P * a:P * a + P], x, y)
                    close(i, name)
                p_ = ("hwi", 6 + l // 4)
                if l % 4 == 0:
                    arrive(p_)
                project(("hg", l), pview(p_, 8)[:, :, P * (l % 4):P * (l % 4) + P])
                pe.wait_ge(hu_new, l + 1)
                for h in range(HH):
                    i = mm(bank(("hso", 0))[:, NS * h + l:NS * h + l + 1], hunit[l % 2][:, 0, P * h:P * h + P],
                           hq[:, h, NP_ + l:NP_ + l + 1])
                if l < NS - 1:
                    i.then_inc(hu_pe, 1)
                else:
                    close(i, ("hso", 0))
            pe.wait_ge(lev_x, 8)
            L = lev[1].rearrange("p (h t) -> p h t", h=8)
            for j in range(2):
                claim(("cr", j))
                for a in range(4):
                    h = 4 * j + a
                    i = mm(bank(("cr", j))[:, P * a:P * a + P], L[:, h, 0:P], L[:, h, P:256])
                close(i, ("cr", j))
            pe.wait_ge(lev_x, 9)
            L = lev[0].rearrange("p (n t) -> p n t", t=P)
            for j in range(4):
                claim(("kt", j))
                for a in range(4):
                    i = nc.tensor.transpose(bank(("kt", j))[:, P * a:P * a + P], L[:, 4 * j + a, :], ident)
                close(i, ("kt", j))
            freed(pe, ("itr", 7))
            freed(pe, ("itr", 6))
            for j in range(2):
                freed(pe, ("kt", 2 * j))
                freed(pe, ("kt", 2 * j + 1))
                claim(("hs", j))
                for a in range(4):
                    h = 4 * j + a
                    for st in range(2):
                        i = mm(bank(("hs", j))[:, P * a:P * a + P], kd_tok[:, 2 * h + st, :],
                               i_tok[:, st, P * h:P * h + P], st == 0, st == 1)
                close(i, ("hs", j))
            freed(pe, ("lv", 7, 3))
            freed(pe, ("cr", 0))
            freed(pe, ("cr", 1))
            for j in range(4):
                claim(("ho", j))
                for a in range(2):
                    h = 2 * j + a
                    o = bank(("ho", j))[:, 256 * a:256 * a + 256]
                    i0, i1 = i_tok[:, 0, P * h:P * h + P], i_tok[:, 1, P * h:P * h + P]
                    mm(o[:, 0:P], i0, att[:, h, 0, :])
                    mm(o[:, P:256], i0, cross[:, h, :], True, False)
                    i = mm(o[:, P:256], i1, att[:, h, 1, :], False, True)
                close(i, ("ho", j))
            pe.wait_ge(sq_ok, RH + 1)
            claim(("hvar", 0))
            for h in range(HH):
                i = mm(bank(("hvar", 0), 8)[:, 0:NT], col_hg[:, h, :], hsq[:, h, :], h == 0, h == 7)
            close(i, ("hvar", 0))
            pe.wait_ge(r8_ok, 2)
            for h in range(HH):
                claim(("hrs", h))
                close(mm(bank(("hrs", h))[:, 0:NT], rowsel[0:8, h, :], rstd[0:8, :]), ("hrs", h))
            pe.wait_ge(o_ok, RH + 1)
            for i_ in range(8):
                p_ = ("hwo", i_ // 4)
                if i_ % 4 == 0:
                    arrive(p_)
                w = pview(p_, 8)
                claim(("hw", i_))
                for k in range(KD):
                    i = mm(bank(("hw", i_))[:, 0:NT], w[:, k, P * (i_ % 4):P * (i_ % 4) + P], oH[:, k, :], k == 0, k == 7)
                close(i, ("hw", i_))
            mean_square(3)
            pe.wait_ge(h_ready, 32)
            for j in range(12):
                src, t, q = (xT, j // 2, j % 2) if j < 6 else (hT, (j - 6) // 2, j % 2)
                m = P if t < 2 else NS
                claim(("tok", j))
                for a in range(4):
                    i = nc.tensor.transpose(bank(("tok", j))[0:m, P * a:P * a + P], src[:, 4 * q + a, P * t:P * t + m],
                                            ident)
                close(i, ("tok", j))
            pe.wait_ge(rt_in, 32)
            claim(("lg", 0))
            for t in range(3):
                m = P if t < 2 else NS
                for k in range(KD):
                    i = mm(bank(("lg", 0))[0:m, 8 * t:8 * t + 8], hT[:, k, P * t:P * t + m], w_rt[:, k, :], k == 0, k == 7)
            close(i, ("lg", 0))
            pe.wait_ge(mask_ok, 1)
            claim(("rk", 0))
            for t in range(4):
                for s in range(min(t + 1, 3)):
                    i = mm(bank(("rk", 0))[:, 8 * t:8 * t + 8], cc("ltri") if s == t else ones, mm_[:, s, :],
                           s == 0, s == min(t, 2))
            close(i, ("rk", 0))
            for j in range(6, 12):
                freed(pe, ("tok", j))
            freed(pe, ("rk", 0))
            pe.wait_ge(route_ok, 1)
            rounds = pe.value_load(nri[0:1, 0:1], min_val=1, max_val=ROUNDS)
            pe.sem_inc(w_used, 2)
            with pe.Fori(0, rounds) as r:
                with pe.Fori(0, NE) as e:
                    n = r * NE + e

                    def expert_arrived(kind, c):
                        t = epos[kind, c]
                        pe.wait_ge(moe_arrived[t % RING], n * (16 * (EP // RING)) + 16 * (t // RING + 1))

                    def up(c):
                        pe.wait_ge(hide_ok, n * NCH + (1 + max(c - 1, 0)))
                        for z, kind in enumerate("gu"):
                            expert_arrived(kind, c)
                            w = piece(epos[kind, c] % RING).rearrange("p (k n) -> p k n", k=8)
                            for j in range(4):
                                for k in range(KD):
                                    i = mm(ps[:, 2 * z + c % 2, C * j:C * j + C], w[:, k, P * j:P * j + P],
                                           xe[:, k, :], k == 0, k == 7)
                            i.then_inc(piece_used, 1)

                    def down(c):
                        pe.wait_ge(hide_lo_ok, n * NCH + (c + 1))
                        if c == 0:
                            pe.wait_ge(y_free, n + 1)
                        for j in range(4):
                            x_hi = hide_hi[:, c % 2, C * j:C * j + C]
                            x_lo = hide_lo[:, c % 2, C * j:C * j + C]
                            pe.wait_ge(w_hi_ok, n * (4 * NCH) + (4 * c + j + 1))
                            for q in range(2):
                                w = w_hi[:, (4 * c + j) % WPL, 512 * q:512 * q + 512]
                                mm(ps[0:C, 4 + q, :], x_hi, w, c + j == 0, False)
                                mm(ps[0:C, 4 + q, :], x_lo, w, False, False)
                            pe.wait_ge(w_lo_ok, n * (4 * NCH) + (4 * c + j + 1))
                            for q in range(2):
                                i = mm(ps[0:C, 4 + q, :], x_hi, w_lo[:, (4 * c + j) % WPL, 512 * q:512 * q + 512],
                                       False, c + j == NCH + 2)
                            i.then_inc(w_used, 1)

                    pe.wait_ge(sel_ok, n + 1)
                    for k in range(KD):
                        for t in range(3):
                            i = mm(ps[:, 6 + k // 4, C * (k % 4):C * (k % 4) + C], h_tok[:, t, P * k:P * k + P],
                                   gsel[:, t, :], t == 0, t == 2)
                    i.then_inc(xg_full, 1)
                    pe.wait_ge(xe_ok, n * 2 + 2)
                    for c in range(NCH + 1):
                        if c < NCH:
                            up(c)
                        if c:
                            down(c - 1)


INPUTS = ["x_prompt", "x_sample", "state_retention", "state_hgrn", "norm_mix_g", "norm_ffn_g", "final_norm_g",
          "ret_w_in", "ret_gn_g", "ret_w_out", "hg_w_in", "hg_lb_param", "hg_norm_g", "hg_w_out", "ffn_w_gate",
          "ffn_w_up", "ffn_w_down", "moe_router", "moe_w_gate", "moe_w_up", "moe_w_down"]
OUTPUTS = [("y_p", (1, NP_, D)), ("y_s", (NS, 1, D)), ("ret_p", (1, 1, RH, RDK, RDV)),
           ("ret_s", (1, NS, RH, RDK, RDV)), ("hg_p", (1, 1, HH, P, P)), ("hg_s", (1, NS, HH, P, P))]


def kernel(**inputs):
    import concourse.bacc as bacc
    from concourse.bass_utils import run_bass_kernel_spmd

    nc = bacc.Bacc("TRN2", target_bir_lowering=False, num_devices=1)
    arrays = {name: np.ascontiguousarray(inputs[name]) for name in INPUTS}
    arrays["consts"] = constants()
    ins = {n: nc.dram_tensor("in_" + n, a.shape, mybir.dt.from_np(a.dtype), kind="ExternalInput").ap()
           for n, a in arrays.items()}
    outs = {n: nc.dram_tensor("out_" + n, s, F32, kind="ExternalOutput").ap() for n, s in OUTPUTS}
    hybrid_step(nc, ins, outs)
    r = run_bass_kernel_spmd(nc, [{"in_" + n: a for n, a in arrays.items()}], core_ids=[0])
    return tuple(r.results[0]["out_" + n] for n, _ in OUTPUTS)
```
